# Optimizing a Trainium2 kernel written in Bass

```python
import math
import jax, jax.numpy as jnp
from jax import lax
import numpy as np

D_MODEL = 1024
BATCH = 1
SEQ = 512
DEPTH = 1
DEC_BATCH = 1
DEC_SEQ = 32
PAST_LEN = 512

CHUNK = 64
CONV_W = 4
EPS = 1e-6
DN_HEADS = 8
DN_DK = 128
DN_DV = 128
DN_QK = DN_HEADS * DN_DK
DN_V = DN_HEADS * DN_DV
DN_CONV_CH = 2 * DN_QK + DN_V
LRU_WIDTH = D_MODEL
LRU_BLOCKS = 8
LRU_BDIM = LRU_WIDTH // LRU_BLOCKS
LRU_C = 8.0
PEER_HEADS = 8
PEER_NKEYS = 128
PEER_N = PEER_NKEYS * PEER_NKEYS
PEER_DK = 128
PEER_DKH = PEER_DK // 2
PEER_TOPK = 16
PEER_TOKEN_BLOCK = 128
IN_SPLITS = (DN_CONV_CH, DN_V, LRU_WIDTH, LRU_WIDTH, D_MODEL, D_MODEL, DN_HEADS, DN_HEADS)
IN_COLS = DN_CONV_CH + DN_V + 2 * LRU_WIDTH + 2 * D_MODEL + 2 * DN_HEADS

kernel_name = "hybrid_gdn_rglru_peer_stream_step"

def rmsnorm(x, g):
    xf = x.astype(jnp.float32)
    r = lax.rsqrt(jnp.mean(xf * xf, axis=-1, keepdims=True) + EPS)
    return (xf * r).astype(x.dtype) * g

def l2norm(x):
    return x * lax.rsqrt(jnp.sum(x * x, axis=-1, keepdims=True) + EPS)

def split_cols(t, sizes):
    offs = [int(o) for o in np.cumsum(sizes)[:-1]]
    return jnp.split(t, offs, axis=-1)

def causal_conv(x, buf, w, b=None):
    T = x.shape[1]
    xp = jnp.concatenate([buf.astype(x.dtype), x], axis=1)
    y = xp[:, 0:T] * w[0]
    for j in range(1, CONV_W):
        y = y + xp[:, j:j + T] * w[j]
    if b is not None:
        y = y + b
    return y, xp[:, -(CONV_W - 1):]

def gated_delta_rule(q, k, v, g, beta, S0):
    B, T, H, DK = q.shape
    L = min(CHUNK, T)
    assert T % L == 0
    nc = T // L
    def chunks(t):
        return t.reshape(B, nc, L, H, t.shape[-1]).transpose(1, 0, 3, 2, 4)
    qc, kc, vc = chunks(q), chunks(k), chunks(v)
    gc = g.reshape(B, nc, L, H).transpose(1, 0, 3, 2)
    bc = beta.reshape(B, nc, L, H).transpose(1, 0, 3, 2)
    G = jnp.cumsum(gc, axis=-1)
    incl = jnp.tril(jnp.ones((L, L), dtype=bool))
    strict = jnp.tril(jnp.ones((L, L), dtype=bool), -1)
    diff = G[..., :, None] - G[..., None, :]
    dec = jnp.where(incl, jnp.exp(jnp.where(incl, diff, 0.0)), 0.0)
    kk = jnp.einsum('cbhid,cbhjd->cbhij', kc, kc)
    A = jnp.where(strict, bc[..., :, None] * kk * dec, 0.0) + jnp.eye(L, dtype=q.dtype)
    gam = jnp.exp(G)
    rhs = jnp.concatenate([(bc * gam)[..., None] * kc, bc[..., None] * vc], axis=-1)
    sol = lax.linalg.triangular_solve(A, rhs, left_side=True, lower=True, unit_diagonal=True)
    Wm, Uv = sol[..., :DK], sol[..., DK:]
    QK = jnp.einsum('cbhid,cbhjd->cbhij', qc, kc) * dec
    qg = qc * gam[..., None]
    kend = kc * jnp.exp(G[..., -1:] - G)[..., None]
    gend = gam[..., -1]

    def step(S, inp):
        Wc, Uvc, QKc, qgc, kendc, gendc = inp
        U = Uvc - jnp.einsum('bhlk,bhkv->bhlv', Wc, S)
        o = jnp.einsum('bhlk,bhkv->bhlv', qgc, S) + jnp.einsum('bhij,bhjv->bhiv', QKc, U)
        S = gendc[..., None, None] * S + jnp.einsum('bhlk,bhlv->bhkv', kendc, U)
        return S, o

    S, o = lax.scan(step, S0, (Wm, Uv, QK, qg, kend, gend))
    o = o.transpose(1, 0, 3, 2, 4).reshape(B, T, H, vc.shape[-1])
    return o, S

def rg_lru(x, h0, w_r, b_r, w_i, b_i, lam):
    B, T, _ = x.shape
    xb = x.reshape(B, T, LRU_BLOCKS, LRU_BDIM)
    r = jax.nn.sigmoid(jnp.einsum('btnd,nde->btne', xb, w_r) + b_r).reshape(B, T, LRU_WIDTH)
    i = jax.nn.sigmoid(jnp.einsum('btnd,nde->btne', xb, w_i) + b_i).reshape(B, T, LRU_WIDTH)
    log_a = -LRU_C * r * jax.nn.softplus(-lam)
    a = jnp.exp(log_a)
    bterm = jnp.sqrt(-jnp.expm1(2.0 * log_a)) * (i * x)

    def comb(lhs, rhs):
        a1, b1 = lhs
        a2, b2 = rhs
        return a1 * a2, a2 * b1 + b2

    Acum, Bcum = lax.associative_scan(comb, (a, bterm), axis=1)
    h = Acum * h0[:, None, :] + Bcum
    return h, h[:, -1]

def peer(n, w_q, keys, u_tab, v_tab):
    B, T, D = n.shape
    N = B * T
    nb = -(-N // PEER_TOKEN_BLOCK)
    flat = jnp.pad(n.reshape(N, D), ((0, nb * PEER_TOKEN_BLOCK - N), (0, 0)))
    flat = flat.reshape(nb, PEER_TOKEN_BLOCK, D)

    def block(xb):
        m = xb.shape[0]
        q = (xb @ w_q).reshape(m, PEER_HEADS, 2, PEER_DKH)
        s = jnp.einsum('nhpc,hpkc->nhpk', q, keys).astype(jnp.float32)
        s1, i1 = lax.top_k(s[:, :, 0], PEER_TOPK)
        s2, i2 = lax.top_k(s[:, :, 1], PEER_TOPK)
        cand = (s1[..., :, None] + s2[..., None, :]).reshape(m, PEER_HEADS, PEER_TOPK * PEER_TOPK)
        top, pos = lax.top_k(cand, PEER_TOPK)
        e = (jnp.take_along_axis(i1, pos // PEER_TOPK, axis=-1) * PEER_NKEYS
             + jnp.take_along_axis(i2, pos % PEER_TOPK, axis=-1))
        gate = jax.nn.softmax(top, axis=-1).astype(xb.dtype)
        e = e.reshape(m, PEER_HEADS * PEER_TOPK)
        gate = gate.reshape(m, PEER_HEADS * PEER_TOPK)
        u = jnp.take(u_tab, e, axis=0)
        act = jax.nn.gelu(jnp.einsum('nkd,nd->nk', u, xb), approximate=False) * gate
        vv = jnp.take(v_tab, e, axis=0)
        return jnp.einsum('nk,nkd->nd', act, vv)

    out = lax.map(block, flat).reshape(nb * PEER_TOKEN_BLOCK, D)[:N]
    return out.reshape(B, T, D)

def layer(x, S0, dn_buf0, h0, lru_buf0, w_in, dn_conv_w, dn_a_log, dn_dt_bias, dn_norm_g,
          lru_conv_w, lru_conv_b, lru_w_r, lru_b_r, lru_w_i, lru_b_i, lru_lambda,
          w_branch_a, w_branch_b, w_out, ln1_g, ln2_g, peer_w_q, peer_keys, peer_u, peer_v):
    f32 = jnp.float32
    B, T, _ = x.shape
    n = rmsnorm(x, ln1_g)
    proj = n @ w_in
    qkv, z, lx, ly, ga, gb, bt, dc = split_cols(proj, IN_SPLITS)
    qkv_c, dn_buf = causal_conv(qkv, dn_buf0, dn_conv_w)
    qkv_c = jax.nn.silu(qkv_c).astype(f32)
    q, k, v = jnp.split(qkv_c, [DN_QK, 2 * DN_QK], axis=-1)
    q = l2norm(q.reshape(B, T, DN_HEADS, DN_DK)) * (DN_DK ** -0.5)
    k = l2norm(k.reshape(B, T, DN_HEADS, DN_DK))
    v = v.reshape(B, T, DN_HEADS, DN_DV)
    beta = jax.nn.sigmoid(bt.astype(f32))
    g = -jnp.exp(dn_a_log.astype(f32)) * jax.nn.softplus(dc.astype(f32) + dn_dt_bias.astype(f32))
    o, S = gated_delta_rule(q, k, v, g, beta, S0.astype(f32))
    o = rmsnorm(o, dn_norm_g.astype(f32)) * jax.nn.silu(z.astype(f32).reshape(B, T, DN_HEADS, DN_DV))
    o_a = o.reshape(B, T, DN_V).astype(x.dtype)
    lc, lru_buf = causal_conv(lx, lru_buf0, lru_conv_w, lru_conv_b)
    h, hT = rg_lru(lc.astype(f32), h0.astype(f32), lru_w_r.astype(f32), lru_b_r.astype(f32),
                   lru_w_i.astype(f32), lru_b_i.astype(f32), lru_lambda.astype(f32))
    o_b = h.astype(x.dtype) * jax.nn.gelu(ly)
    mix = jax.nn.sigmoid(ga) * (o_a @ w_branch_a) + jax.nn.sigmoid(gb) * (o_b @ w_branch_b)
    x = x + mix @ w_out
    x = x + peer(rmsnorm(x, ln2_g), peer_w_q, peer_keys, peer_u, peer_v)
    return x, S.astype(x.dtype), dn_buf, hT.astype(x.dtype), lru_buf

def setup_inputs(seed: int = 0) -> dict:
    key = jax.random.key(seed)
    ks = jax.random.split(key, 32)
    f32 = jnp.float32

    def nrm(k, shape, s):
        return jax.random.normal(k, shape, f32) * s

    a0 = jax.random.uniform(ks[17], (DEPTH, LRU_WIDTH), f32, 0.9, 0.999) ** (1.0 / LRU_C)
    dt = jnp.exp(jax.random.uniform(ks[9], (DEPTH, DN_HEADS), f32, math.log(1e-3), math.log(1e-1)))
    return {
        'x_prompt': nrm(ks[0], (BATCH, SEQ, D_MODEL), 1.0),
        'x_sample': nrm(ks[1], (DEC_BATCH, DEC_SEQ, D_MODEL), 1.0),
        'state_dn': nrm(ks[2], (DEPTH, DEC_BATCH, DN_HEADS, DN_DK, DN_DV), 0.1),
        'state_dn_conv': nrm(ks[3], (DEPTH, DEC_BATCH, CONV_W - 1, DN_CONV_CH), 1.0),
        'state_lru_h': nrm(ks[4], (DEPTH, DEC_BATCH, LRU_WIDTH), 0.5),
        'state_lru_conv': nrm(ks[5], (DEPTH, DEC_BATCH, CONV_W - 1, LRU_WIDTH), 1.0),
        'w_in': nrm(ks[6], (DEPTH, D_MODEL, IN_COLS), D_MODEL ** -0.5),
        'dn_conv_w': nrm(ks[7], (DEPTH, CONV_W, DN_CONV_CH), CONV_W ** -0.5),
        'dn_a_log': jnp.log(jax.random.uniform(ks[8], (DEPTH, DN_HEADS), f32, 1.0, 16.0)),
        'dn_dt_bias': dt + jnp.log(-jnp.expm1(-dt)),
        'dn_norm_g': 1.0 + nrm(ks[10], (DEPTH, DN_DV), 0.02),
        'lru_conv_w': nrm(ks[11], (DEPTH, CONV_W, LRU_WIDTH), CONV_W ** -0.5),
        'lru_conv_b': nrm(ks[12], (DEPTH, LRU_WIDTH), 0.02),
        'lru_w_r': nrm(ks[13], (DEPTH, LRU_BLOCKS, LRU_BDIM, LRU_BDIM), LRU_BDIM ** -0.5),
        'lru_b_r': nrm(ks[14], (DEPTH, LRU_BLOCKS, LRU_BDIM), 0.02),
        'lru_w_i': nrm(ks[15], (DEPTH, LRU_BLOCKS, LRU_BDIM, LRU_BDIM), LRU_BDIM ** -0.5),
        'lru_b_i': nrm(ks[16], (DEPTH, LRU_BLOCKS, LRU_BDIM), 0.02),
        'lru_lambda': jnp.log(a0) - jnp.log1p(-a0),
        'w_branch_a': nrm(ks[18], (DEPTH, DN_V, D_MODEL), DN_V ** -0.5),
        'w_branch_b': nrm(ks[19], (DEPTH, LRU_WIDTH, D_MODEL), LRU_WIDTH ** -0.5),
        'w_out': nrm(ks[20], (DEPTH, D_MODEL, D_MODEL), D_MODEL ** -0.5),
        'ln1_g': 1.0 + nrm(ks[21], (DEPTH, D_MODEL), 0.02),
        'ln2_g': 1.0 + nrm(ks[22], (DEPTH, D_MODEL), 0.02),
        'peer_w_q': nrm(ks[23], (DEPTH, D_MODEL, PEER_HEADS * PEER_DK), D_MODEL ** -0.5),
        'peer_keys': nrm(ks[24], (DEPTH, PEER_HEADS, 2, PEER_NKEYS, PEER_DKH), PEER_DKH ** -0.5),
        'peer_u': nrm(ks[25], (DEPTH, PEER_N, D_MODEL), D_MODEL ** -0.5),
        'peer_v': nrm(ks[26], (DEPTH, PEER_N, D_MODEL), 0.5),
        'final_g': 1.0 + nrm(ks[27], (D_MODEL,), 0.02),
    }

def reference(x_prompt, x_sample, state_dn, state_dn_conv, state_lru_h, state_lru_conv,
              w_in, dn_conv_w, dn_a_log, dn_dt_bias, dn_norm_g, lru_conv_w, lru_conv_b,
              lru_w_r, lru_b_r, lru_w_i, lru_b_i, lru_lambda, w_branch_a, w_branch_b, w_out,
              ln1_g, ln2_g, peer_w_q, peer_keys, peer_u, peer_v, final_g):
    bp = x_prompt.shape[0]
    dt = x_prompt.dtype
    xp, xs = x_prompt, x_sample
    dn_p, dnc_p, lh_p, lc_p = [], [], [], []
    dn_s, dnc_s, lh_s, lc_s = [], [], [], []
    for l in range(DEPTH):
        params = (w_in[l], dn_conv_w[l], dn_a_log[l], dn_dt_bias[l], dn_norm_g[l],
                  lru_conv_w[l], lru_conv_b[l], lru_w_r[l], lru_b_r[l], lru_w_i[l], lru_b_i[l],
                  lru_lambda[l], w_branch_a[l], w_branch_b[l], w_out[l], ln1_g[l], ln2_g[l],
                  peer_w_q[l], peer_keys[l], peer_u[l], peer_v[l])
        xp, S, db, hT, lb = layer(
            xp,
            jnp.zeros((bp, DN_HEADS, DN_DK, DN_DV), dt),
            jnp.zeros((bp, CONV_W - 1, DN_CONV_CH), dt),
            jnp.zeros((bp, LRU_WIDTH), dt),
            jnp.zeros((bp, CONV_W - 1, LRU_WIDTH), dt),
            *params)
        dn_p.append(S); dnc_p.append(db); lh_p.append(hT); lc_p.append(lb)
        xs, S, db, hT, lb = layer(xs, state_dn[l], state_dn_conv[l], state_lru_h[l], state_lru_conv[l], *params)
        dn_s.append(S); dnc_s.append(db); lh_s.append(hT); lc_s.append(lb)
    y_prompt = rmsnorm(xp, final_g)
    y_sample = rmsnorm(xs, final_g)
    new_dn_p = jnp.stack(dn_p)
    new_dn_conv_p = jnp.stack(dnc_p)
    new_lru_h_p = jnp.stack(lh_p)
    new_lru_conv_p = jnp.stack(lc_p)
    new_dn_s = jnp.stack(dn_s)
    new_dn_conv_s = jnp.stack(dnc_s)
    new_lru_h_s = jnp.stack(lh_s)
    new_lru_conv_s = jnp.stack(lc_s)
    return (y_prompt, y_sample, new_dn_p, new_dn_conv_p, new_lru_h_p, new_lru_conv_p,
            new_dn_s, new_dn_conv_s, new_lru_h_s, new_lru_conv_s)


_drawn_inputs = setup_inputs


def setup_inputs(seed=0):
    import zlib

    import numpy as np

    out = dict(_drawn_inputs(seed))
    spreads = {}
    factors = {'lru_b_r': 8.0, 'lru_b_i': 5.976, 'final_g': 3.104}
    for name, (base, spread) in spreads.items():
        noise = np.random.default_rng([zlib.crc32(name.encode()), seed]).standard_normal(out[name].shape)
        drawn = base * np.exp(spread * noise) if base else spread * noise
        out[name] = __import__('jax').numpy.asarray(drawn.astype(out[name].dtype))
    for name, factor in factors.items():
        out[name] = (out[name] * factor).astype(out[name].dtype)
    return out
```

```python
from contextlib import ExitStack

import concourse.bass as bass
import numpy as np
from concourse import mybir

F32 = mybir.dt.float32
I32 = mybir.dt.int32
U32 = mybir.dt.uint32
ALU = mybir.AluOpType
ACT = mybir.ActivationFunctionType
AX_X = mybir.AxisListType.X
ds = bass.ds

P = 128
D = 1024
KC = D // P
TP, TS = 512, 32
NT = TP + TS
HALF = NT // 2
NTILE = TP // P
H = 8
CW = 4
HIST = CW - 1
PADW = HIST + TP + HIST + TS
SMP0 = HIST + TP + HIST
CONVW = PADW - HIST
YS0 = TP + HIST
EPS = 1e-6
LRU_C = 8.0
NKEYS = 128
TOPK = 16
LEVELS = 7
RING = 4
SLOTS = 8
NEG = -3.0e38

N_LX, N_LY, N_ZG, N_QKV, N_BR = KC, KC, 3 * KC, 3 * KC, KC
N_STREAM = N_LX + N_LY + N_ZG + N_QKV + 3 * N_BR


def trunk_program(nc, a, o):
    ctx = ExitStack()
    with ctx:
        def sb(name, shape, dt=F32):
            return ctx.enter_context(nc.sbuf_tensor(name, shape, dt))

        def sem(name):
            return ctx.enter_context(nc.semaphore(name))

        ident = sb("ident", [P, P])
        ones = sb("ones", [P, P])
        upper = sb("upper", [P, P])
        lvl = sb("lvl", [P, LEVELS, P])
        fold = sb("fold", [P, TS])
        iota16 = sb("iota16", [P, TOPK])
        ln1 = sb("ln1", [P, KC])
        dn_w = sb("dn_w", [P, 3 * KC, CW])
        lru_w = sb("lru_w", [P, KC, CW])
        lru_b = sb("lru_b", [P, KC])
        b_r = sb("b_r", [P, KC])
        b_i = sb("b_i", [P, KC])
        lam = sb("lam", [P, KC])
        h0 = sb("h0", [P, KC])
        dn_hist = sb("dn_hist", [P, 3 * KC, HIST])
        lru_hist = sb("lru_hist", [P, KC, HIST])
        alog = sb("alog", [P, H])
        dtb = sb("dtb", [P, H])
        dn_g = sb("dn_g", [P, 1])
        w_ba = sb("w_ba", [P, KC, 2 * H])
        cn = sb("cn", [P, KC])
        tails = sb("tails", [P, 4 * KC, 2 * HIST])
        lru_last = sb("lru_last", [P, KC, 2])
        spx = sb("spx", [P, KC + (NTILE + 1) * H])
        spl = sb("spl", [P, KC + (NTILE + 1) * H])
        glog = sb("glog", [P, (NTILE + 1) * H])
        rs2 = sb("rs2", [P, NTILE + 1])
        bg = sb("bg", [P, NTILE + 1, 2 * H])
        beta = sb("beta", [P, NTILE + 1, H])
        gcum = sb("gcum", [P, NTILE + 1, H])
        gam_col = sb("gam_col", [P, NTILE + 1, H])
        eps_col = sb("eps_col", [P, 1])

        arena = sb("arena", [P, 46600])

        def view(at, *dims):
            n = int(np.prod(dims))
            v = arena[:, at:at + n]
            if len(dims) == 1:
                return v
            if len(dims) == 2:
                return v.rearrange("p (a b) -> p a b", b=dims[1])
            return v.rearrange("p (a b c) -> p a b c", b=dims[1], c=dims[2])

        W = KC * NT
        n_t = view(0, KC, NT)
        z_t = view(W, KC, NT)
        ga_t = view(2 * W, KC, NT)
        gb_t = view(3 * W, KC, NT)
        ob_t = view(4 * W, KC, NT)
        qkv_t = view(5 * W, 3 * KC, NT)
        lru_a = view(5 * W, KC, NT)
        lru_i = view(6 * W, KC, NT)
        lru_th = view(7 * W, KC, NT)
        TAIL = 8 * W
        wring = [view(TAIL + s * KC * P, KC, P) for s in range(RING)]
        o1 = TAIL + RING * KC * P
        xpad = [view(o1 + s * 552, 552) for s in range(2)]
        ycv = [view(o1 + 1104 + s * 552, 552) for s in range(2)]
        lru_v = [view(o1 + 2208 + s * NT, NT) for s in range(2)]
        gelu_y = view(o1 + 2208 + 2 * NT, KC, NT)
        assert o1 + 2208 + 2 * NT + W <= 46600
        rstd1 = ycv[0][:, 0:NT]
        sq_x = qkv_t
        homes = iter([k * 1024 for k in range(4)] + [4 * W + k * 1024 for k in range(4)]
                     + [o1 + k * 1024 for k in range(7)])

        def head_buf():
            return view(next(homes), H, P)

        dgam, dbet = head_buf(), head_buf()
        kn, qn = head_buf(), head_buf()
        vn, dec = head_buf(), head_buf()
        gam, nmat = head_buf(), head_buf()
        ct, tinv, tinvt = head_buf(), head_buf(), head_buf()
        pmat, qk = head_buf(), head_buf()
        kend, vtok = head_buf(), head_buf()
        sq_q, sq_k = tinv, tinvt
        rmat, umat = ct, pmat
        o_sb, o_sq = dgam, dbet
        state = {True: sb("state_p", [P, H, P]), False: sb("state_s", [P, H, P])}
        wr_v = view(3 * W, KC, P)
        wi_v = view(3 * W + KC * P, KC, P)

        x2 = view(4 * W, NTILE + 1, D)
        X2END = 4 * W + (NTILE + 1) * D
        w_out = view(X2END, KC, D)
        n2_t = z_t
        q_t = ga_t
        g2 = view(3 * W, D)
        gf = view(3 * W + D, D)
        keys = view(3 * W + 2 * D, H, NKEYS)
        n2 = view(3 * W + 3 * D, D)
        ybuf = view(0, D)
        assert 3 * W + 4 * D <= 4 * W
        qs = view(D, H, P)
        acc = [view(2 * D, D), view(3 * D, D)]
        ring = [view(X2END + s * 2 * D, 2 * D) for s in range(SLOTS)]
        o2 = X2END + SLOTS * 2 * D
        sc = view(o2, 2 * H, NKEYS)
        cand = view(o2 + 2048, H, TOPK * TOPK)
        sc_flat = view(o2, 2048)
        cand_flat = view(o2 + 2048, 2048)
        assert o2 + 4096 <= 46600, o2
        n2p = view(W, D)
        v16 = view(W + D, 2 * H, TOPK)
        i16 = sb("i16", [P, 2 * H, TOPK], U32)
        i16f = view(W + D + 256, 2 * H, TOPK)
        top = sb("top", [P, H, TOPK])
        pos = sb("pos", [P, H, TOPK], U32)
        posu = sb("posu", [P, 2, H * TOPK], U32)
        posf = view(W + D + 512, 2, H * TOPK)
        e12 = view(W + D + 768, 2, H * TOPK)
        idx = sb("idx", [P, H * TOPK], I32)
        idxp = sb("idxp", [P, TS], I32)
        gate = sb("gate", [P, H, TOPK])
        gatep = sb("gatep", [P, TS])
        gsum = sb("gsum", [P, 2, H])
        idxs = [sb(f"idxs{b}", [P, SLOTS], I32) for b in range(2)]
        dots = [sb(f"dots{b}", [P, 2]) for b in range(4)]
        gelu_d = [sb(f"gelu_d{b}", [P, 2]) for b in range(4)]
        coef = [sb(f"coef{b}", [P, 2]) for b in range(4)]
        ssum = sb("ssum", [P, 4])

        ps = ctx.enter_context(nc.psum_tensor("ps", [P, 8, 512], F32))

        def both(b):
            return ps[:, b:b + 2, 0:HALF]

        params_in = sem("params_in")
        x_in = sem("x_in")
        chunk_in = [sem(f"chunk_in{s}") for s in range(RING)]
        sq_done = sem("sq_done")
        ssq_done = sem("ssq_done")
        root_done = sem("root_done")
        rstd_done = sem("rstd_done")
        n_ready = sem("n_ready")
        ba_done = sem("ba_done")
        prod_ready = sem("prod_ready")
        prod_used = sem("prod_used")
        pad_ready = sem("pad_ready")
        tail_done = sem("tail_done")
        conv_step = sem("conv_step")
        conv_ready = sem("conv_ready")
        conv_used = sem("conv_used")
        lru_sq = sem("lru_sq")
        lru_exp = sem("lru_exp")
        lru_one = sem("lru_one")
        lru_root = sem("lru_root")
        lru_step = sem("lru_step")
        lru_done = sem("lru_done")
        lru_ob_n = sem("lru_ob_n")
        sp_x = sem("sp_x")
        sp_abs = sem("sp_abs")
        sp_log = sem("sp_log")
        sp_sum = sem("sp_sum")
        g_ready = sem("g_ready")
        bg_zero = sem("bg_zero")
        bg_ready = sem("bg_ready")
        gcum_mm = sem("gcum_mm")
        gcum_ready = sem("gcum_ready")
        gam_ready = sem("gam_ready")
        state_zero = sem("state_zero")
        state_in = sem("state_in")

        d_diag = sem("d_diag")
        d_bc = sem("d_bc")
        d_sq = sem("d_sq")
        d_vn = sem("d_vn")
        d_ssq = sem("d_ssq")
        d_root = sem("d_root")
        d_rcp = sem("d_rcp")
        d_norm = sem("d_norm")
        d_diff = sem("d_diff")
        d_min = sem("d_min")
        d_exp = sem("d_exp")
        d_mask = sem("d_mask")
        d_dec = sem("d_dec")
        d_tr = sem("d_tr")
        d_kend = sem("d_kend")
        d_vtok = sem("d_vtok")
        d_kk = sem("d_kk")
        d_nm = sem("d_nm")
        d_qg = sem("d_qg")
        d_ct = sem("d_ct")
        d_p = sem("d_p")
        d_pc = sem("d_pc")
        d_xy = sem("d_xy")
        d_t = sem("d_t")
        d_ks = sem("d_ks")
        d_r1 = sem("d_r1")
        d_r2 = sem("d_r2")
        d_r = sem("d_r")
        d_u = sem("d_u")
        d_uc = sem("d_uc")
        d_os = sem("d_os")
        d_s1 = sem("d_s1")
        d_s = sem("d_s")
        d_oc = sem("d_oc")
        d_oss = sem("d_oss")
        d_or = sem("d_or")
        d_o1 = sem("d_o1")
        d_o2 = sem("d_o2")
        d_og = sem("d_og")

        late_w = sem("late_w")
        late_p = sem("late_p")
        mix_step = sem("mix_step")
        mix_ready = sem("mix_ready")
        out_mm = sem("out_mm")
        x2_ready = sem("x2_ready")
        n2_sq = sem("n2_sq")
        n2_root = sem("n2_root")
        n2_rcp = sem("n2_rcp")
        n2_ready = sem("n2_ready")
        n2_tr = sem("n2_tr")
        n2_copied = sem("n2_copied")

        qs_ready = sem("qs_ready")
        sc_mm = sem("sc_mm")
        sc_ready = sem("sc_ready")
        pick_step = sem("pick_step")
        shift_ready = sem("shift_ready")
        gate_exp = sem("gate_exp")
        idx_ready = sem("idx_ready")
        tile_ready = sem("tile_ready")
        idxs_ready = sem("idxs_ready")
        slot_free = sem("slot_free")
        row_in = [sem(f"row_in{s}") for s in range(SLOTS)]
        dot_ready = sem("dot_ready")
        gelu_ready = sem("gelu_ready")
        coef_ready = sem("coef_ready")
        packed = sem("packed")
        fold_mm = sem("fold_mm")
        fin_step = sem("fin_step")
        fin_add = sem("fin_add")
        fin_sq = sem("fin_sq")
        fin_root = sem("fin_root")
        y_ready = sem("y_ready")
        y_out = sem("y_out")
        small_out = sem("small_out")

        block = ctx.enter_context(nc.Block())

        PARAMS = [(ident, "ident"), (ones, "ones"), (upper, "upper"), (lvl, "lvl"), (fold, "fold"),
                  (iota16, "iota16"), (ln1, "ln1_g"), (dn_w, "dn_conv_w"), (lru_w, "lru_conv_w"),
                  (lru_b, "lru_conv_b"), (b_r, "lru_b_r"), (b_i, "lru_b_i"), (lam, "lru_lambda"),
                  (h0, "state_lru_h"), (dn_hist, "state_dn_conv"), (lru_hist, "state_lru_conv"),
                  (dn_g, "dn_norm_g"), (w_ba, "w_ba")]
        N_PARAMS = 16 * (len(PARAMS) + 4)

        PR_GATE = N_LX + N_LY
        PR_ZG = PR_GATE + 2 * KC
        PR_QKV = PR_ZG + N_ZG
        PR_BB = PR_QKV + N_QKV
        PR_BA = PR_BB + N_BR
        PR_Q = PR_BA + N_BR
        PR_END = PR_Q + N_BR
        SHIFT = 2 * KC
        CONVS = N_LX + N_QKV
        NPAIR = TOPK // 2

        def rows(t):
            return TS if isinstance(t, int) and t == NTILE else P

        def uses(k):
            return k * 16

        def heads(bank, L):
            return ps[0:L, bank:bank + 2, :].rearrange("p b (h i) -> p (b h) i", h=4)

        def wait_apart(eng, sem_, value, constant):
            if not isinstance(value, int):
                value = eng.compute_val(value)
            eng.wait_ge(constant, 1)
            eng.wait_ge(sem_, value)

        def chain(eng, sem_, base, constant=None):
            n = [0]

            def link(ins):
                n[0] += 1
                ins.then_inc(sem_, 1)
                if constant is not None:
                    wait_apart(eng, sem_, base + n[0], constant)
                else:
                    eng.wait_ge(sem_, base + n[0])
            return link, n

        @block.sync
        def _(sp):
            for c in range(KC):
                sp.dma_start(n_t[:, c, :], a["x_t"][:, c, :]).then_inc(x_in, 16)
            for dst, name in PARAMS:
                sp.dma_start(dst[:], a[name]).then_inc(params_in, 16)
            for dst, name in ((wr_v, "lru_w_r"), (wi_v, "lru_w_i")):
                sp.dma_start(dst, a[name]).then_inc(params_in, 16)
            for dst, name in ((alog, "dn_a_log"), (dtb, "dn_dt_bias")):
                sp.dma_start(dst[:], a[name].broadcast_to([P, H])).then_inc(params_in, 16)
            sp.dma_start(state[False][:], a["state_dn"]).then_inc(state_in, 16)

            for s in range(RING):
                sp.dma_start(wring[s], a["stream"][s]).then_inc(chunk_in[s], 16)
            refills = PR_GATE // RING + 1
            for first, last, shift in ((1, refills, 0), (refills, N_STREAM // RING, SHIFT)):
                with sp.Fori(first, last) as i:
                    for s in range(RING):
                        sp.wait_ge(prod_ready, i * RING + (s - RING + 1 + shift))
                        sp.dma_start(wring[s], a["stream"][ds(i * RING + s, 1)].rearrange(
                            "o p k n -> (o p) k n")).then_inc(chunk_in[s], 16)

            sp.wait_ge(tile_ready, NTILE + 1)
            for q in range(P // TS):
                to = slice(q * TS, (q + 1) * TS)
                sp.dma_start(idxp[to, :], idx[0:TS, to]).then_inc(packed, 16)
                sp.dma_start(gatep[to, :], gate[0:TS, 2 * q:2 * q + 2, :].rearrange("p h k -> p (h k)")
                             ).then_inc(packed, 16)
                sp.dma_start(n2p[to, :], n2[0:TS, :]).then_inc(packed, 16)
            sp.wait_ge(y_out, uses(NTILE + 1))
            sp.wait_ge(small_out, uses(4))

        @block.tensor
        def _(pe):
            def quads(first, last, shift, rhs, head=0):
                def body(i, unheld):
                    for s in range(RING):
                        n = i * RING + s
                        pe.wait_ge(chunk_in[s], uses(i + 1))
                        if s >= unheld:
                            pe.wait_ge(prod_used, n + (shift - 1))
                        b = 2 * ((s + shift) % 2)
                        for half in range(2):
                            for k in range(KC):
                                mm = pe.matmul(ps[:, b + half, 0:HALF], wring[s][:, k, :],
                                               rhs[:, k, half * HALF:(half + 1) * HALF],
                                               start=(k == 0), stop=(k == KC - 1))
                        mm.then_inc(prod_ready, 1)
                i0 = first // RING
                if first == 0:
                    body(0, 2)
                    i0 = 1
                with pe.Fori(i0, last // RING) as i:
                    body(i, 0)

            pe.wait_ge(params_in, N_PARAMS)
            pe.wait_ge(sq_done, 1)
            for half in range(2):
                for c in range(KC):
                    mm = pe.matmul(ps[:, half, 0:HALF], ones[:, :], sq_x[:, c, half * HALF:(half + 1) * HALF],
                                   start=(c == 0), stop=(c == KC - 1))
            mm.then_inc(ssq_done, 1)
            pe.wait_ge(n_ready, KC)
            for t in range(NTILE + 1):
                n = rows(t)
                for c in range(KC):
                    mm = pe.matmul(ps[0:n, 4, t * 16:(t + 1) * 16], n_t[:, c, t * P:t * P + n], w_ba[:, c, :],
                                   start=(c == 0), stop=(c == KC - 1))
            mm.then_inc(ba_done, 1)
            quads(0, PR_GATE, 0, n_t)
            for n in range(KC):
                pe.wait_ge(conv_used, n + 1)
                for j, w in enumerate((wr_v, wi_v)):
                    pr = PR_GATE + 2 * n + j
                    pe.wait_ge(prod_used, pr - 1)
                    for half in range(2):
                        mm = pe.matmul(ps[:, 2 * (pr % 2) + half, 0:HALF], w[:, n, :],
                                       ob_t[:, n, half * HALF:(half + 1) * HALF], start=True, stop=True)
                    mm.then_inc(prod_ready, 1)
            pe.wait_ge(g_ready, 1)
            pe.matmul(ps[:, 5, 0:(NTILE + 1) * H], upper[:, :], glog[:, :], start=True, stop=True
                      ).then_inc(gcum_mm, 1)
            quads(PR_GATE, PR_BB - SHIFT, SHIFT, n_t)
            pe.wait_ge(lru_ob_n, KC)
            quads(PR_BB - SHIFT, PR_BA - SHIFT, SHIFT, ob_t)

            def delta(t, first):
                L = rows(t)
                NL = (L - 1).bit_length()
                S = state[L == P]
                pe.wait_ge(d_diag, t + 1)
                if first:
                    pe.wait_ge(prod_used, PR_BA)
                else:
                    pe.wait_ge(d_og, t)
                for b, src in ((0, dgam), (2, dbet)):
                    for g in range(2):
                        mm = pe.matmul(heads(b, P)[:, 4 * g:4 * g + 4, 0:L], ones[0:L, :],
                                       src[0:L, 4 * g:4 * g + 4, 0:L], start=True, stop=True)
                mm.then_inc(d_bc, 1)
                pe.wait_ge(d_sq, t + 1)
                if first:
                    pe.wait_ge(gcum_ready, 1)
                for b, src in ((4, sq_q), (6, sq_k)):
                    for g in range(2):
                        mm = pe.matmul(heads(b, P)[:, 4 * g:4 * g + 4, 0:L], ones[:, :],
                                       src[:, 4 * g:4 * g + 4, 0:L], start=True, stop=True)
                mm.then_inc(d_ssq, 1)
                pe.wait_ge(d_norm, t + 1)
                pe.wait_ge(d_vn, t + 1)
                for h in range(H):
                    pe.transpose(heads(4, L)[:, h, :], kn[:, h, 0:L], ident[:, :])
                    mm = pe.transpose(heads(6, L)[:, h, :], vn[:, h, 0:L], ident[:, :])
                mm.then_inc(d_tr, 1)
                pe.wait_ge(d_dec, t + 1)
                for h in range(H):
                    pe.matmul(heads(0, L)[:, h, 0:L], kn[:, h, 0:L], kn[:, h, 0:L], start=True, stop=True)
                    mm = pe.matmul(heads(2, L)[:, h, 0:L], kn[:, h, 0:L], qn[:, h, 0:L], start=True, stop=True)
                mm.then_inc(d_kk, 1)
                for lv in range(NL):
                    pe.wait_ge(d_ct, LEVELS * t + lv + 1)
                    if lv:
                        pe.wait_ge(d_t, LEVELS * t + lv)
                    for h in range(H):
                        mm = pe.matmul(heads(0, L)[:, h, 0:L], ct[0:L, h, 0:L],
                                       tinv[0:L, h, 0:L] if lv else ident[0:L, 0:L], start=True, stop=True)
                    mm.then_inc(d_p, 1)
                    if lv == 0:
                        continue
                    pe.wait_ge(d_pc, (LEVELS - 1) * t + lv)
                    if lv == 1:
                        pe.wait_ge(d_kend, t + 1)
                        pe.wait_ge(d_vtok, t + 1)
                    for h in range(H):
                        if lv < NL - 1:
                            pe.matmul(heads(4, L)[:, h, 0:L], tinvt[0:L, h, 0:L], pmat[0:L, h, 0:L],
                                      start=True, stop=True)
                        mm = pe.matmul(heads(6, L)[:, h, 0:L], pmat[0:L, h, 0:L], tinvt[0:L, h, 0:L],
                                       start=True, stop=True)
                    mm.then_inc(d_xy, 1)
                pe.wait_ge(d_t, LEVELS * t + NL)
                if L != P:
                    pe.wait_ge(state_in, 16)
                elif first:
                    pe.wait_ge(state_zero, 1)
                else:
                    pe.wait_ge(d_s, t)
                for h in range(H):
                    mm = pe.matmul(heads(0, L)[:, h, :], kn[:, h, 0:L], S[:, h, :], start=True, stop=True)
                mm.then_inc(d_ks, 1)
                pe.wait_ge(d_r, t + 1)
                for h in range(H):
                    mm = pe.matmul(heads(2, L)[:, h, :], tinvt[0:L, h, 0:L], rmat[0:L, h, :],
                                   start=True, stop=True)
                mm.then_inc(d_u, 1)
                pe.wait_ge(d_uc, t + 1)
                pe.wait_ge(d_qg, t + 1)
                for h in range(H):
                    pe.matmul(heads(4, P)[:, h, 0:L], S[:, h, :], qn[:, h, 0:L], start=True, stop=False)
                    pe.matmul(heads(4, P)[:, h, 0:L], umat[0:L, h, :], qk[0:L, h, 0:L], start=False, stop=True)
                for h in range(H):
                    mm = pe.matmul(heads(6, P)[:, h, :], kend[0:L, h, :], umat[0:L, h, :],
                                   start=True, stop=True)
                mm.then_inc(d_os, 1)
                pe.wait_ge(d_oc, t + 1)
                for g in range(2):
                    mm = pe.matmul(heads(0, P)[:, 4 * g:4 * g + 4, 0:L], ones[:, :],
                                   o_sq[:, 4 * g:4 * g + 4, 0:L], start=True, stop=True)
                mm.then_inc(d_oss, 1)

            delta(0, True)
            with pe.Fori(1, NTILE) as t:
                delta(t, False)
            delta(NTILE, False)
            pe.wait_ge(d_og, NTILE + 1)
            quads(PR_BA - SHIFT, PR_Q - SHIFT, SHIFT, z_t)

            pe.wait_ge(mix_ready, KC)
            pe.wait_ge(late_w, uses(3))
            for t in range(NTILE + 1):
                n = rows(t)
                if t:
                    pe.wait_ge(x2_ready, t)
                for half in range(2):
                    for k in range(KC):
                        mm = pe.matmul(ps[0:n, 4 + half, :], n_t[:, k, t * P:t * P + n],
                                       w_out[:, k, half * 512:(half + 1) * 512], start=(k == 0), stop=(k == KC - 1))
                mm.then_inc(out_mm, 1)
                pe.wait_ge(n2_ready, t + 1)
                if t:
                    pe.wait_ge(n2_copied, t)
                for c in range(KC):
                    mm = pe.transpose(heads(6, P)[:, c, 0:n], n2[0:n, c * P:(c + 1) * P], ident[0:n, 0:n])
                mm.then_inc(n2_tr, 1)
            pe.wait_ge(n2_copied, NTILE + 1)
            quads(PR_Q - SHIFT, N_STREAM, SHIFT, n2_t)

            def scores(t, first):
                L = rows(t)
                pe.wait_ge(qs_ready, t + 1)
                if not first:
                    pe.wait_ge(sc_ready, t)
                for h in range(H):
                    for p in range(2):
                        mm = pe.matmul(heads(4 + 2 * p, L)[:, h, :], qs[64 * p:64 * p + 64, h, 0:L],
                                       keys[64 * p:64 * p + 64, h, :], start=True, stop=True)
                mm.then_inc(sc_mm, 1)

            pe.wait_ge(late_p, uses(3))
            scores(0, True)
            with pe.Fori(1, NTILE) as t:
                scores(t, False)
            scores(NTILE, False)
            pe.wait_ge(slot_free, SLOTS + NTILE * P + TS)
            for half in range(2):
                for j in range(2):
                    mm = pe.matmul(ps[0:TS, half, :], fold[:, :], acc[j][:, half * 512:(half + 1) * 512],
                                   start=(j == 0), stop=(j == 1))
            mm.then_inc(fold_mm, 1)

        @block.scalar
        def _(act):
            def evac(j, pr, hist, slot, held):
                act.wait_ge(prod_ready, pr + 1)
                if held:
                    act.wait_ge(conv_ready, j - 1)
                    act.wait_ge(tail_done, j - 1)
                b = 2 * slot
                x = xpad[slot]
                act.copy(x[:, HIST:HIST + HALF], ps[:, b, 0:HALF])
                act.copy(x[:, HIST + HALF:HIST + TP], ps[:, b + 1, 0:TP - HALF])
                act.copy(x[:, SMP0:SMP0 + TS], ps[:, b + 1, TP - HALF:HALF]).then_inc(prod_used, 1)
                act.copy(x[:, TP + HIST:SMP0], hist).then_inc(pad_ready, 1)

            def post(j, slot, dst, func, bias=0.0):
                act.wait_ge(conv_ready, j + 1)
                y = ycv[slot]
                act.activation(dst[:, 0:TP], y[:, 0:TP], func, bias=bias)
                act.activation(dst[:, TP:NT], y[:, YS0:YS0 + TS], func, bias=bias).then_inc(conv_used, 1)

            def row(m, c):
                return m[:, ds(c, 1), :].rearrange("p o n -> p (o n)")

            act.wait_ge(x_in, uses(KC))
            act.activation(sq_x[:, 0:KC, :], n_t[:, :, :], ACT.Square).then_inc(sq_done, 1)
            act.wait_ge(ssq_done, 1)
            act.wait_ge(bg_zero, 1)
            act.activation(rstd1.rearrange("p (b n) -> p b n", b=2), both(0), ACT.Sqrt, scale=1.0 / D,
                           bias=eps_col[:, 0:1]).then_inc(root_done, 1)
            act.wait_ge(sp_x, 1)
            act.activation(spl[:, :], spx[:, :], ACT.Abs).then_inc(sp_abs, 1)
            act.wait_ge(sp_abs, 1)
            act.activation(spl[:, :], spl[:, :], ACT.Exp, scale=-1.0).then_inc(sp_abs, 1)
            act.activation(alog[:, :], alog[:, :], ACT.Exp)
            act.wait_ge(sp_abs, 2)
            act.activation(spl[:, :], spl[:, :], ACT.Ln, bias=1.0).then_inc(sp_log, 1)
            act.activation(beta[:, :, :], bg[:, :, 0:H], ACT.Sigmoid).then_inc(sp_log, 1)

            def conv_group(first, last, pr0, hist, c0, finish):
                def step(i, j, s, held, has_prev):
                    evac(j, j + (pr0 - first), row(hist, j - c0), s, held)
                    if has_prev:
                        finish(j - 1, 1 - s)
                step(None, first, 0, first > 0, False)
                step(None, first + 1, 1, first > 0, True)
                with act.Fori(first // 2 + 1, last // 2) as i:
                    for s in range(2):
                        step(i, i * 2 + s, s, True, True)
                finish(last - 1, 1)

            conv_group(0, N_LX, 0, lru_hist, 0,
                       lambda j, s: post(j, s, row(ob_t, j), ACT.Identity, bias=lru_b[:, ds(j, 1)]))
            with act.Fori(0, N_LY // 2) as i:
                for s in range(2):
                    act.wait_ge(prod_ready, i * 2 + (N_LX + s + 1))
                    act.activation(row(gelu_y, i * 2 + s).rearrange("p (b n) -> p b n", b=2), both(2 * s),
                                   ACT.Gelu_apprx_tanh).then_inc(prod_used, 1)
            with act.Fori(0, KC) as n:
                for s, (dst, b) in enumerate(((lru_a, b_r), (lru_i, b_i))):
                    act.wait_ge(prod_ready, n * 2 + (PR_GATE + s + 1))
                    act.activation(row(dst, n).rearrange("p (b n) -> p b n", b=2), both(2 * s), ACT.Sigmoid,
                                   bias=b[:, ds(n, 1)]).then_inc(prod_used, 1)
            act.wait_ge(prod_used, PR_ZG)
            act.wait_ge(g_ready, 1)
            with act.Fori(0, KC) as n:
                act.activation(row(lru_th, n), row(lru_a, n), ACT.Tanh, scale=cn[:, ds(n, 1)])
                act.activation(row(lru_a, n), row(lru_a, n), ACT.Exp, scale=cn[:, ds(n, 1)]).then_inc(lru_exp, 1)
            with act.Fori(0, KC) as n:
                act.wait_ge(lru_one, n + 1)
                act.activation(row(lru_th, n), row(lru_th, n), ACT.Sqrt, scale=-1.0).then_inc(lru_root, 1)
            for first, dst, func in ((0, z_t, ACT.Silu), (KC, ga_t, ACT.Sigmoid), (2 * KC, gb_t, ACT.Sigmoid)):
                with act.Fori(0, KC // 2) as i:
                    for s in range(2):
                        act.wait_ge(prod_ready, i * 2 + (PR_ZG + first + s + 1))
                        act.activation(row(dst, i * 2 + s).rearrange("p (b n) -> p b n", b=2), both(2 * s),
                                       func).then_inc(prod_used, 1)
            act.wait_ge(lru_done, 1)
            conv_group(N_LX, CONVS, PR_QKV, dn_hist, N_LX,
                       lambda j, s: post(j, s, row(qkv_t, j - N_LX), ACT.Silu))
            act.wait_ge(gcum_ready, 1)
            act.activation(gam_col[:, :, :], gcum[:, :, :], ACT.Exp).then_inc(gam_ready, 1)

            act.wait_ge(prod_ready, PR_BA)
            act.wait_ge(conv_used, CONVS)
            act.wait_ge(tail_done, CONVS)

            def delta(t, first):
                L = rows(t)
                NL = (L - 1).bit_length()
                cols = ds(t * P, L)
                if not first:
                    act.wait_ge(d_os, t)
                act.activation(sq_q[:, :, 0:L], qkv_t[:, 0:H, cols], ACT.Square)
                act.activation(sq_k[:, :, 0:L], qkv_t[:, H:2 * H, cols], ACT.Square).then_inc(d_sq, 1)
                act.copy(vn[:, :, 0:L], qkv_t[:, 2 * H:3 * H, cols]).then_inc(d_vn, 1)
                act.wait_ge(d_ssq, t + 1)
                act.activation(ct[:, :, 0:L], heads(4, P)[:, :, 0:L], ACT.Sqrt, bias=eps_col[:, 0:1])
                act.activation(pmat[:, :, 0:L], heads(6, P)[:, :, 0:L], ACT.Sqrt, bias=eps_col[:, 0:1]
                               ).then_inc(d_root, 1)
                act.wait_ge(d_min, t + 1)
                act.activation(dec[0:L, :, 0:L], dec[0:L, :, 0:L], ACT.Exp)
                act.activation(gam[:, :, 0:L], heads(0, P)[:, :, 0:L], ACT.Exp).then_inc(d_exp, 1)
                act.wait_ge(d_tr, t + 1)
                act.copy(vtok[0:L, :, :], heads(6, L)).then_inc(d_vtok, 1)
                for lv in range(1, NL):
                    act.wait_ge(d_p, LEVELS * t + lv + 1)
                    act.copy(pmat[0:L, :, 0:L], heads(0, L)[:, :, 0:L]).then_inc(d_pc, 1)
                act.wait_ge(d_u, t + 1)
                act.copy(umat[0:L, :, :], heads(2, L)).then_inc(d_uc, 1)
                act.wait_ge(d_os, t + 1)
                act.copy(o_sb[:, :, 0:L], heads(4, P)[:, :, 0:L])
                act.activation(o_sq[:, :, 0:L], heads(4, P)[:, :, 0:L], ACT.Square).then_inc(d_oc, 1)
                act.wait_ge(d_oss, t + 1)
                act.activation(o_sq[:, :, 0:L], heads(0, P)[:, :, 0:L], ACT.Sqrt, scale=1.0 / P,
                               bias=eps_col[:, 0:1]).then_inc(d_or, 1)

            delta(0, True)
            with act.Fori(1, NTILE) as t:
                delta(t, False)
            delta(NTILE, False)

            for t in range(NTILE + 1):
                n = rows(t)
                act.wait_ge(x2_ready, t + 1)
                act.activation(cand_flat[0:n, 0:D], x2[0:n, t, :], ACT.Square, accum_out=ssum[0:n, 0:1]).then_inc(n2_sq, 1)
                act.wait_ge(n2_sq, t + 1)
                act.activation(ssum[0:n, 1:2], ssum[0:n, 0:1], ACT.Sqrt, scale=1.0 / D,
                               bias=eps_col[0:n, 0:1]).then_inc(n2_root, 1)
                act.wait_ge(n2_tr, t + 1)
                act.copy(n2_t[:, :, t * P:t * P + n], heads(6, P)[:, :, 0:n]).then_inc(n2_copied, 1)
            with act.Fori(0, KC // 2) as i:
                for s in range(2):
                    act.wait_ge(prod_ready, i * 2 + (PR_Q + s + 1))
                    act.copy(row(q_t, i * 2 + s).rearrange("p (b n) -> p b n", b=2), both(2 * s)
                             ).then_inc(prod_used, 1)

            act.wait_ge(prod_used, PR_END)

            def peer(t, first):
                L = rows(t)
                if not first:
                    act.wait_ge(sc_mm, t)
                act.copy(qs[:, :, 0:L], q_t[:, :, ds(t * P, L)]).then_inc(qs_ready, 1)
                act.wait_ge(sc_mm, t + 1)
                if not first:
                    act.wait_ge(idx_ready, t)
                act.copy(sc_flat[0:L, :], ps[0:L, 4:8, :].rearrange("p b n -> p (b n)")).then_inc(sc_ready, 1)
                act.wait_ge(shift_ready, t + 1)
                act.activation(gate[0:L, :, :], gate[0:L, :, :], ACT.Exp).then_inc(gate_exp, 1)
                steps = H if L == P else TS // TOPK
                with act.Fori(0, steps) as i:
                    for u in range(NPAIR):
                        act.wait_ge(dot_ready, (t * H + i) * NPAIR + (u + 1))
                        act.activation(gelu_d[u % 4][:, :], dots[u % 4][:, :], ACT.Gelu).then_inc(gelu_ready, 1)
                act.wait_ge(fin_add, t + 1)
                act.activation(cand_flat[0:L, 0:D], acc[0][0:L, :], ACT.Square, accum_out=ssum[0:L, 0:1]
                               ).then_inc(fin_sq, 1)
                act.wait_ge(fin_sq, t + 1)
                act.activation(ssum[0:L, 1:2], ssum[0:L, 0:1], ACT.Sqrt, scale=1.0 / D,
                               bias=eps_col[0:L, 0:1]).then_inc(fin_root, 1)
                act.wait_ge(y_ready, t + 1)
                act.dma_start(o["y"][ds(t * P, L), :], ybuf[0:L, :]).then_inc(y_out, 16)

            peer(0, True)
            with act.Fori(1, NTILE) as t:
                peer(t, False)
            peer(NTILE, False)

        @block.gpsimd
        def _(pool):
            pool.memset(state[True][:, :, :], 0.0).then_inc(state_zero, 1)
            with pool.Fori(0, CONVS // 2) as i:
                for s in range(2):
                    pool.wait_ge(pad_ready, i * 2 + (s + 1))
                    to = tails[:, ds(i * 2 + s, 1), :].rearrange("p o n -> p (o n)")
                    pool.tensor_copy(to[:, 0:HIST], xpad[s][:, TP:TP + HIST])
                    pool.tensor_copy(to[:, HIST:2 * HIST], xpad[s][:, PADW - HIST:PADW]).then_inc(tail_done, 1)
            pool.wait_ge(tail_done, CONVS)
            pool.dma_start(o["tails"], tails[:, :, :]).then_inc(small_out, 16)
            pool.wait_ge(lru_done, 1)
            pool.dma_start(o["lru_last"], lru_last[:, :, :]).then_inc(small_out, 16)
            pool.wait_ge(d_s, NTILE)
            pool.dma_start(o["dn_p"], state[True][:, :, :]).then_inc(small_out, 16)
            pool.wait_ge(d_s, NTILE + 1)
            pool.dma_start(o["dn_s"], state[False][:, :, :]).then_inc(small_out, 16)
            pool.wait_ge(d_og, NTILE + 1)
            pool.dma_start(w_out, a["w_out"]).then_inc(late_w, 16)
            pool.dma_start(x2[:, 0:NTILE, :], a["x_prompt"].rearrange("(t p) d -> p t d", p=P)).then_inc(late_w, 16)
            pool.dma_start(x2[0:TS, NTILE, :], a["x_sample"]).then_inc(late_w, 16)
            pool.wait_ge(mix_ready, KC)
            pool.dma_start(g2, a["ln2_g"].broadcast_to([P, D])).then_inc(late_p, 16)
            pool.dma_start(gf, a["final_g"].broadcast_to([P, D])).then_inc(late_p, 16)
            pool.dma_start(keys, a["keys"]).then_inc(late_p, 16)

            def gathers(t, src, steps):
                with pool.Fori(0, steps) as i:
                    n = t * H + i
                    for b in range(2):
                        pool.wait_ge(slot_free, n * TOPK + (SLOTS * b + 1))
                        pool.tensor_copy(idxs[b][:, :], src[:, ds(i * TOPK + SLOTS * b, SLOTS)]
                                         ).then_inc(idxs_ready, 1)
                        wait_apart(pool, idxs_ready, n * 2 + (b + 1), idx_ready)
                        for s in range(SLOTS):
                            wait_apart(pool, slot_free, n * TOPK + (SLOTS * b + s + 1), idx_ready)
                            pool.indirect_dma_start(
                                out=ring[s], out_offset=None, in_=a["uv"],
                                in_offset=bass.IndirectOffsetOnAxis(ap=idxs[b][:, s:s + 1], axis=0),
                            ).then_inc(row_in[s], 16)

            with pool.Fori(0, NTILE) as t:
                wait_apart(pool, idx_ready, t + 1, state_zero)
                gathers(t, idx, H)
            pool.wait_ge(packed, uses(3 * P // TS))
            gathers(NTILE, idxp, TS // TOPK)

        @block.vector
        def _(dve):
            def row(m, c):
                return m[:, ds(c, 1), :].rearrange("p o n -> p (o n)")

            dve.memset(bg[:, :, :], 0.0)
            for s in range(2):
                dve.memset(xpad[s][:, 0:HIST], 0.0)
            dve.memset(eps_col[:, :], EPS).then_inc(bg_zero, 1)
            dve.wait_ge(root_done, 1)
            dve.wait_ge(params_in, N_PARAMS)
            dve.reciprocal(rstd1, rstd1).then_inc(rstd_done, 1)
            dve.wait_ge(rstd_done, 1)
            for c in range(KC):
                dve.scalar_tensor_tensor(out=n_t[:, c, :], in0=n_t[:, c, :], scalar=ln1[:, c:c + 1], in1=rstd1,
                                         op0=ALU.mult, op1=ALU.mult).then_inc(n_ready, 1)
            dve.wait_ge(ba_done, 1)
            dve.wait_ge(bg_zero, 1)
            dve.tensor_copy(bg[:, 0:NTILE, :], ps[:, 4, 0:NTILE * 16].rearrange("p (t n) -> p t n", t=NTILE))
            dve.tensor_copy(bg[0:TS, NTILE, :], ps[0:TS, 4, NTILE * 16:NTILE * 16 + 16]).then_inc(bg_ready, 1)
            dve.wait_ge(bg_ready, 1)
            dve.tensor_scalar(spx[:, 0:KC], lam[:, :], -1.0, None, ALU.mult)
            dve.tensor_tensor(spx[:, KC:].rearrange("p (t h) -> p t h", h=H), bg[:, :, H:2 * H],
                              dtb[:, :].unsqueeze(1).broadcast_to([P, NTILE + 1, H]), ALU.add).then_inc(sp_x, 1)
            dve.wait_ge(sp_log, 2)
            dve.scalar_tensor_tensor(out=spx[:, :], in0=spx[:, :], scalar=0.0, in1=spl[:, :],
                                     op0=ALU.max, op1=ALU.add).then_inc(sp_sum, 1)
            dve.wait_ge(sp_sum, 1)
            dve.tensor_scalar(cn[:, :], spx[:, 0:KC], -LRU_C, None, ALU.mult)
            dve.scalar_tensor_tensor(out=glog[:, :].rearrange("p (t h) -> p t h", h=H),
                                     in0=spx[:, KC:].rearrange("p (t h) -> p t h", h=H), scalar=-1.0,
                                     in1=alog[:, :].unsqueeze(1).broadcast_to([P, NTILE + 1, H]),
                                     op0=ALU.mult, op1=ALU.mult).then_inc(g_ready, 1)

            def conv(j, w, s, held):
                dve.wait_ge(pad_ready, j + 1)
                if held:
                    dve.wait_ge(conv_used, j - 1)
                x, y = xpad[s], ycv[s]
                ins = dve.tensor_scalar(y[:, 0:CONVW], x[:, 0:CONVW], w[:, 0:1], None, ALU.mult)
                for k in range(1, CW):
                    ins.then_inc(conv_step, 1)
                    dve.wait_ge(conv_step, j * HIST + k)
                    ins = dve.scalar_tensor_tensor(out=y[:, 0:CONVW], in0=x[:, k:k + CONVW], scalar=w[:, k:k + 1],
                                                   in1=y[:, 0:CONVW], op0=ALU.mult, op1=ALU.add)
                ins.then_inc(conv_ready, 1)

            for j in range(2):
                conv(j, lru_w[:, j, :], j, False)
            with dve.Fori(1, N_LX // 2) as i:
                for s in range(2):
                    conv(i * 2 + s, row(lru_w, i * 2 + s), s, True)
            with dve.Fori(0, KC // 2) as i:
                for s in range(2):
                    n = i * 2 + s
                    dve.wait_ge(lru_exp, n + 1)
                    dve.tensor_tensor(lru_v[s], row(lru_a, n), row(lru_a, n), ALU.mult).then_inc(lru_sq, 1)
                    dve.wait_ge(lru_sq, n + 1)
                    dve.scalar_tensor_tensor(out=row(lru_th, n), in0=lru_v[s], scalar=1.0, in1=row(lru_th, n),
                                             op0=ALU.add, op1=ALU.mult).then_inc(lru_one, 1)
            with dve.Fori(0, KC) as n:
                A, I = row(lru_a, n), row(lru_i, n)
                link, made = chain(dve, lru_step, n * 3)
                link(dve.tensor_tensor(I, I, row(ob_t, n), ALU.mult))
                dve.wait_ge(lru_root, n + 1)
                link(dve.tensor_tensor(I, I, row(lru_th, n), ALU.mult))
                dve.tensor_tensor_scan(A[:, 0:TP], A[:, 0:TP], I[:, 0:TP], 0.0, ALU.mult, ALU.add)
                link(dve.tensor_tensor_scan(A[:, TP:NT], A[:, TP:NT], I[:, TP:NT], h0[:, ds(n, 1)],
                                            ALU.mult, ALU.add))
                dve.tensor_tensor(row(ob_t, n), A, row(gelu_y, n), ALU.mult).then_inc(lru_ob_n, 1)
                assert made[0] == 3
            dve.wait_ge(lru_ob_n, KC)
            dve.tensor_copy(lru_last[:, :, 0:1], lru_a[:, :, TP - 1:TP])
            dve.tensor_copy(lru_last[:, :, 1:2], lru_a[:, :, NT - 1:NT]).then_inc(lru_done, 1)
            dve.wait_ge(gcum_mm, 1)
            dve.tensor_copy(gcum[:, :, :], ps[:, 5, 0:(NTILE + 1) * H].rearrange("p (t h) -> p t h", h=H)
                            ).then_inc(gcum_ready, 1)
            with dve.Fori(N_LX // 2, CONVS // 2) as i:
                for s in range(2):
                    conv(i * 2 + s, row(dn_w, i * 2 + (s - N_LX)), s, True)
            dve.wait_ge(prod_used, PR_BB)
            with dve.Fori(0, KC // 2) as i:
                for s in range(2):
                    n = i * 2 + s
                    dve.wait_ge(prod_ready, n + (PR_BB + 1))
                    gb = row(gb_t, n).rearrange("p (b n) -> p b n", b=2)
                    dve.tensor_tensor(gb, both(2 * s), gb, ALU.mult).then_inc(prod_used, 1)

            dve.wait_ge(gam_ready, 1)

            def over_i(col, L):
                return col[0:L, :].unsqueeze(2).broadcast_to([L, H, L])

            def over_d(col, L):
                return col[0:L, :].unsqueeze(2).broadcast_to([L, H, P])

            def over_h(m, L):
                return m.unsqueeze(1).broadcast_to([L, H, L])

            def delta(t, first):
                L = rows(t)
                NL = (L - 1).bit_length()
                cols = ds(t * P, L)
                G, B, GC = (m[:, ds(t, 1), :].rearrange("p o h -> p (o h)") for m in (gcum, beta, gam_col))
                S = state[L == P]
                eye = over_h(ident[0:L, 0:L], L)
                if not first:
                    dve.wait_ge(d_og, t)
                dve.tensor_tensor(dgam[0:L, :, 0:L], eye, over_i(G, L), ALU.mult)
                dve.tensor_tensor(dbet[0:L, :, 0:L], eye, over_i(B, L), ALU.mult).then_inc(d_diag, 1)
                dve.wait_ge(d_root, t + 1)
                dve.reciprocal(ct[:, :, 0:L], ct[:, :, 0:L])
                dve.reciprocal(pmat[:, :, 0:L], pmat[:, :, 0:L]).then_inc(d_rcp, 1)
                dve.wait_ge(d_rcp, t + 1)
                dve.scalar_tensor_tensor(out=qn[:, :, 0:L], in0=qkv_t[:, 0:H, cols], scalar=float(P) ** -0.5,
                                         in1=ct[:, :, 0:L], op0=ALU.mult, op1=ALU.mult)
                dve.tensor_tensor(kn[:, :, 0:L], qkv_t[:, H:2 * H, cols], pmat[:, :, 0:L], ALU.mult
                                  ).then_inc(d_norm, 1)
                dve.wait_ge(d_bc, t + 1)
                dve.tensor_tensor(dec[0:L, :, 0:L], heads(0, L)[:, :, 0:L], over_i(G, L), ALU.subtract
                                  ).then_inc(d_diff, 1)
                dve.wait_ge(d_diff, t + 1)
                dve.tensor_scalar(dec[0:L, :, 0:L], dec[0:L, :, 0:L], 0.0, None, ALU.min).then_inc(d_min, 1)
                dve.wait_ge(d_exp, t + 1)
                dve.tensor_tensor(dec[0:L, :, 0:L], dec[0:L, :, 0:L], over_h(upper[0:L, 0:L], L), ALU.mult
                                  ).then_inc(d_mask, 1)
                dve.wait_ge(d_mask, t + 1)
                dve.tensor_tensor(nmat[0:L, :, 0:L], heads(2, L)[:, :, 0:L], dec[0:L, :, 0:L], ALU.mult
                                  ).then_inc(d_dec, 1)
                dve.wait_ge(d_tr, t + 1)
                dve.tensor_tensor(kend[0:L, :, :], heads(4, L), dec[0:L, :, L - 1:L].broadcast_to([L, H, P]),
                                  ALU.mult).then_inc(d_kend, 1)
                dve.wait_ge(d_kk, t + 1)
                dve.wait_ge(d_dec, t + 1)
                dve.tensor_tensor(nmat[0:L, :, 0:L], heads(0, L)[:, :, 0:L], nmat[0:L, :, 0:L], ALU.mult
                                  ).then_inc(d_nm, 1)
                dve.tensor_tensor(qk[0:L, :, 0:L], heads(2, L)[:, :, 0:L], dec[0:L, :, 0:L], ALU.mult)
                dve.wait_ge(d_nm, t + 1)
                for lv in range(NL):
                    if lv:
                        dve.wait_ge(d_p, LEVELS * t + lv)
                        dve.wait_ge(d_t, LEVELS * t + lv)
                    dve.tensor_tensor(ct[0:L, :, 0:L], nmat[0:L, :, 0:L], over_h(lvl[0:L, lv, 0:L], L), ALU.mult
                                      ).then_inc(d_ct, 1)
                    if lv == 0:
                        dve.tensor_tensor(qn[:, :, 0:L], qn[:, :, 0:L], gam[:, :, 0:L], ALU.mult).then_inc(d_qg, 1)
                        dve.wait_ge(d_ct, LEVELS * t + 1)
                        dve.tensor_tensor(tinvt[0:L, :, 0:L], eye, ct[0:L, :, 0:L], ALU.subtract)
                        dve.wait_ge(d_p, LEVELS * t + 1)
                        dve.tensor_tensor(tinv[0:L, :, 0:L], eye, heads(0, L)[:, :, 0:L], ALU.subtract
                                          ).then_inc(d_t, 1)
                        continue
                    dve.wait_ge(d_xy, (LEVELS - 1) * t + lv)
                    if lv < NL - 1:
                        dve.tensor_tensor(tinv[0:L, :, 0:L], tinv[0:L, :, 0:L], heads(4, L)[:, :, 0:L], ALU.subtract)
                    dve.tensor_tensor(tinvt[0:L, :, 0:L], tinvt[0:L, :, 0:L], heads(6, L)[:, :, 0:L], ALU.subtract
                                      ).then_inc(d_t, 1)
                dve.wait_ge(d_ks, t + 1)
                dve.wait_ge(d_vtok, t + 1)
                dve.tensor_tensor(rmat[0:L, :, :], heads(0, L), over_d(GC, L), ALU.mult).then_inc(d_r1, 1)
                dve.wait_ge(d_r1, t + 1)
                dve.tensor_tensor(rmat[0:L, :, :], vtok[0:L, :, :], rmat[0:L, :, :], ALU.subtract).then_inc(d_r2, 1)
                dve.wait_ge(d_r2, t + 1)
                dve.tensor_tensor(rmat[0:L, :, :], rmat[0:L, :, :], over_d(B, L), ALU.mult).then_inc(d_r, 1)
                dve.wait_ge(d_os, t + 1)
                dve.tensor_tensor(S[:, :, :], S[:, :, :], gam[:, :, L - 1:L].broadcast_to([P, H, P]), ALU.mult
                                  ).then_inc(d_s1, 1)
                dve.wait_ge(d_s1, t + 1)
                dve.tensor_tensor(S[:, :, :], S[:, :, :], heads(6, P), ALU.add).then_inc(d_s, 1)
                dve.wait_ge(d_or, t + 1)
                dve.reciprocal(o_sq[:, :, 0:L], o_sq[:, :, 0:L]).then_inc(d_o1, 1)
                dve.wait_ge(d_o1, t + 1)
                dve.scalar_tensor_tensor(out=o_sb[:, :, 0:L], in0=o_sb[:, :, 0:L], scalar=dn_g[:, 0:1],
                                         in1=o_sq[:, :, 0:L], op0=ALU.mult, op1=ALU.mult).then_inc(d_o2, 1)
                dve.wait_ge(d_o2, t + 1)
                dve.tensor_tensor(z_t[:, :, cols], o_sb[:, :, 0:L], z_t[:, :, cols], ALU.mult).then_inc(d_og, 1)

            delta(0, True)
            with dve.Fori(1, NTILE) as t:
                delta(t, False)
            delta(NTILE, False)
            with dve.Fori(0, KC // 2) as i:
                for s in range(2):
                    n = i * 2 + s
                    dve.wait_ge(prod_ready, n + (PR_BA + 1))
                    ga = row(ga_t, n).rearrange("p (b n) -> p b n", b=2)
                    dve.tensor_tensor(ga, both(2 * s), ga, ALU.mult).then_inc(prod_used, 1)
                    dve.wait_ge(prod_used, n + (PR_BA + 1))
                    dve.tensor_tensor(row(n_t, n), row(ga_t, n), row(gb_t, n), ALU.add).then_inc(mix_ready, 1)
            dve.wait_ge(late_w, uses(3))
            dve.wait_ge(late_p, uses(3))
            for t in range(NTILE + 1):
                n = rows(t)
                dve.wait_ge(out_mm, t + 1)
                dve.tensor_tensor(x2[0:n, t, :], ps[0:n, 4:6, :].rearrange("p b n -> p (b n)"), x2[0:n, t, :],
                                  ALU.add).then_inc(x2_ready, 1)
                dve.wait_ge(n2_root, t + 1)
                dve.reciprocal(rs2[0:n, t:t + 1], ssum[0:n, 1:2]).then_inc(n2_rcp, 1)
                dve.wait_ge(n2_rcp, t + 1)
                if t:
                    dve.wait_ge(n2_tr, t)
                dve.scalar_tensor_tensor(out=n2[0:n, :], in0=x2[0:n, t, :], scalar=rs2[0:n, t:t + 1],
                                         in1=g2[0:n, :], op0=ALU.mult, op1=ALU.mult).then_inc(n2_ready, 1)

            dve.wait_ge(n2_tr, NTILE + 1)
            dve.wait_ge(prod_ready, PR_END)
            dve.sem_inc(slot_free, SLOTS)
            PICKS = 19

            def top16(src, n, width, vals, inds, L, link):
                for half in range(2):
                    to = slice(8 * half, 8 * half + 8)
                    for j in range(n):
                        ins = dve.max(out=vals[0:L, j, to], in_=src[0:L, j, :])
                    link(ins)
                    for j in range(n):
                        ins = dve.max_index(out=inds[0:L, j, to], in_max=vals[0:L, j, to], in_values=src[0:L, j, :])
                    if half:
                        break
                    for j in range(n):
                        ins = dve.match_replace(out=src[0:L, j, :], in_to_replace=vals[0:L, j, to],
                                                in_values=src[0:L, j, :], imm_value=NEG)
                    link(ins)
                link(ins)

            def pick(t):
                L = rows(t)
                link, made = chain(dve, pick_step, PICKS * t, constant=n_ready)
                wait_apart(dve, sc_ready, t + 1, n_ready)
                top16(sc, 2 * H, NKEYS, v16, i16, L, link)
                dve.tensor_copy(i16f[0:L, :, :], i16[0:L, :, :])
                for h in range(H):
                    ins = dve.tensor_tensor(cand[0:L, h, :].rearrange("p (a b) -> p a b", a=TOPK),
                                            v16[0:L, h, :].unsqueeze(2).broadcast_to([L, TOPK, TOPK]),
                                            v16[0:L, H + h, :].unsqueeze(1).broadcast_to([L, TOPK, TOPK]), ALU.add)
                link(ins)
                top16(cand, H, TOPK * TOPK, top, pos, L, link)
                dve.tensor_tensor(gate[0:L, :, :], top[0:L, :, :], top[0:L, :, 0:1].broadcast_to([L, H, TOPK]),
                                  ALU.subtract).then_inc(shift_ready, 1)
                pf = pos[0:L, :, :].rearrange("p h k -> p (h k)")
                dve.tensor_scalar(posu[0:L, 0, :], pf, 4, None, ALU.logical_shift_right)
                link(dve.tensor_scalar(posu[0:L, 1, :], pf, 15, None, ALU.bitwise_and))
                link(dve.tensor_copy(posf[0:L, :, :], posu[0:L, :, :]))
                for p in range(2):
                    hot = sc_flat[0:L, :].rearrange("p (h k j) -> p h k j", h=H, k=TOPK)
                    link(dve.tensor_tensor(
                        sc_flat[0:L, :].rearrange("p (n j) -> p n j", j=TOPK),
                        posf[0:L, p, :].unsqueeze(2).broadcast_to([L, H * TOPK, TOPK]),
                        iota16[0:L, :].unsqueeze(1).broadcast_to([L, H * TOPK, TOPK]), ALU.is_equal))
                    link(dve.tensor_tensor(
                        hot, hot, i16f[0:L, p * H:(p + 1) * H, :].unsqueeze(2).broadcast_to([L, H, TOPK, TOPK]),
                        ALU.mult))
                    link(dve.tensor_reduce(e12[0:L, p, :], sc_flat[0:L, :].rearrange("p (n j) -> p n j", j=TOPK),
                                           AX_X, ALU.add))
                dve.scalar_tensor_tensor(out=idx[0:L, :], in0=e12[0:L, 0, :], scalar=float(NKEYS),
                                         in1=e12[0:L, 1, :], op0=ALU.mult, op1=ALU.add).then_inc(idx_ready, 1)
                dve.wait_ge(gate_exp, t + 1)
                link(dve.tensor_reduce(gsum[0:L, 0, :], gate[0:L, :, :], AX_X, ALU.add))
                link(dve.reciprocal(gsum[0:L, 1, :], gsum[0:L, 0, :]))
                dve.tensor_tensor(gate[0:L, :, :], gate[0:L, :, :],
                                  gsum[0:L, 1, :].unsqueeze(2).broadcast_to([L, H, TOPK]), ALU.mult)
                dve.scalar_tensor_tensor(out=n2[0:L, :], in0=row(x2, t)[0:L, :], scalar=rs2[0:L, ds(t, 1)],
                                         in1=g2[0:L, :], op0=ALU.mult, op1=ALU.mult).then_inc(tile_ready, 1)
                assert made[0] == PICKS, made
                dve.wait_ge(tile_ready, t + 1)

            def dot_pair(n, u, norm):
                for j in range(2):
                    k = 2 * u + j
                    s = k % SLOTS
                    dve.wait_ge(row_in[s], uses(n * 2 + (k // SLOTS + 1)))
                    ins = dve.tensor_tensor_reduce(ring[s][:, 0:D], ring[s][:, 0:D], norm, 1.0, 0.0,
                                                   ALU.mult, ALU.add, dots[u % 4][:, j:j + 1])
                ins.then_inc(dot_ready, 1)

            def add_pair(n, u, gates):
                m = n * NPAIR + (u + 1)
                dve.wait_ge(gelu_ready, m)
                dve.tensor_tensor(coef[u % 4][:, :], gelu_d[u % 4][:, :], gates, ALU.mult).then_inc(coef_ready, 1)
                dve.wait_ge(coef_ready, m)
                for j in range(2):
                    s = (2 * u + j) % SLOTS
                    dve.scalar_tensor_tensor(out=acc[j], in0=ring[s][:, D:2 * D], scalar=coef[u % 4][:, j:j + 1],
                                             in1=acc[j], op0=ALU.mult, op1=ALU.add).then_inc(slot_free, 1)

            def experts(t, norm, gates, steps):
                def step(i, last):
                    n = t * H + i
                    for u in range(NPAIR):
                        if u < NPAIR - 1:
                            dot_pair(n, u + 1, norm)
                        elif not last:
                            dot_pair(n + 1, 0, norm)
                        add_pair(n, u, gates[:, ds(i * TOPK + 2 * u, 2)])
                dve.memset(acc[0], 0.0)
                dve.memset(acc[1], 0.0)
                dot_pair(t * H, 0, norm)
                with dve.Fori(0, steps - 1) as i:
                    step(i, False)
                step(steps - 1, True)

            def finish(t, first):
                L = rows(t)
                dve.wait_ge(slot_free, SLOTS + P * (t + 1) if L == P else SLOTS + P * NTILE + TS)
                if L == P:
                    dve.tensor_tensor(acc[0], acc[0], acc[1], ALU.add).then_inc(fin_step, 1)
                    dve.wait_ge(fin_step, t * 2 + 1)
                    dve.tensor_tensor(acc[0], acc[0], row(x2, t), ALU.add).then_inc(fin_add, 1)
                else:
                    dve.wait_ge(fold_mm, 1)
                    dve.tensor_tensor(acc[0][0:L, :], ps[0:L, 0:2, :].rearrange("p b n -> p (b n)"),
                                      x2[0:L, NTILE, :], ALU.add).then_inc(fin_add, 1)
                dve.wait_ge(fin_root, t + 1)
                dve.reciprocal(ssum[0:L, 2:3], ssum[0:L, 1:2]).then_inc(fin_step, 1)
                dve.wait_ge(fin_step, t * 2 + (2 if L == P else 1))
                if not first:
                    dve.wait_ge(y_out, uses(t))
                dve.scalar_tensor_tensor(out=ybuf[0:L, :], in0=acc[0][0:L, :], scalar=ssum[0:L, 2:3],
                                         in1=gf[0:L, :], op0=ALU.mult, op1=ALU.mult).then_inc(y_ready, 1)

            gate_flat = gate[:, :, :].rearrange("p h k -> p (h k)")

            def tile(t, first):
                pick(t)
                experts(t, n2, gate_flat, H)
                finish(t, first)

            tile(0, True)
            with dve.Fori(1, NTILE) as t:
                tile(t, False)
            pick(NTILE)
            dve.wait_ge(packed, uses(3 * P // TS))
            experts(NTILE, n2p, gatep, TS // TOPK)
            finish(NTILE, False)


def _chunks(w):
    k, n = w.shape
    return np.ascontiguousarray(w.reshape(k // P, P, n // P, P).transpose(2, 1, 0, 3))


def _features(v):
    v = v.reshape(*v.shape[:-1], v.shape[-1] // P, P)
    return np.ascontiguousarray(np.moveaxis(np.moveaxis(v, -1, 0), -1, 1))


def _constants():
    i = np.arange(P)
    upper = (i[None, :] >= i[:, None]).astype(np.float32)
    lvl = np.zeros((P, LEVELS, P), np.float32)
    for lv in range(LEVELS):
        s = 1 << lv
        same = (i[:, None] // (2 * s)) == (i[None, :] // (2 * s))
        lvl[:, lv, :] = same & ((i[:, None] // s) % 2 == 0) & ((i[None, :] // s) % 2 == 1)
    return {
        "ident": np.eye(P, dtype=np.float32), "ones": np.ones((P, P), np.float32), "upper": upper, "lvl": lvl,
        "fold": (i[:, None] % TS == np.arange(TS)[None, :]).astype(np.float32),
        "iota16": np.broadcast_to(np.arange(TOPK, dtype=np.float32), (P, TOPK)).copy(),
    }


_OUTS = {"y": (NT, D), "tails": (P, 4 * KC, 2 * HIST), "lru_last": (P, KC, 2), "dn_p": (P, H, P),
         "dn_s": (P, H, P)}


def kernel(**inputs):
    import concourse.bacc as bacc
    from concourse.bass_utils import run_bass_kernel_spmd

    v = {k: np.asarray(x) for k, x in inputs.items()}
    w_in = v["w_in"][0]
    at = np.cumsum([0, 3 * D, D, D, D, D, D])
    part = [w_in[:, at[n]:at[n + 1]] for n in range(6)]
    qkv, z, lx, ly, ga, gb = part
    arrays = _constants()
    arrays["x_t"] = _features(np.concatenate([v["x_prompt"][0], v["x_sample"][0]], 0))
    arrays["x_prompt"], arrays["x_sample"] = v["x_prompt"][0], v["x_sample"][0]
    arrays["stream"] = np.concatenate([_chunks(w) for w in (
        lx, ly, z, ga, gb, qkv, v["w_branch_b"][0], v["w_branch_a"][0], v["peer_w_q"][0])], 0)
    arrays["w_ba"] = np.ascontiguousarray(w_in[:, at[6]:].reshape(KC, P, 2 * H).transpose(1, 0, 2))
    arrays["w_out"] = np.ascontiguousarray(v["w_out"][0].reshape(KC, P, D).transpose(1, 0, 2))
    arrays["ln1_g"] = _features(v["ln1_g"][0])
    arrays["dn_conv_w"] = _features(v["dn_conv_w"][0])
    arrays["lru_conv_w"] = _features(v["lru_conv_w"][0])
    arrays["lru_conv_b"] = _features(v["lru_conv_b"][0])
    arrays["lru_b_r"] = np.ascontiguousarray(v["lru_b_r"][0].T)
    arrays["lru_b_i"] = np.ascontiguousarray(v["lru_b_i"][0].T)
    arrays["lru_lambda"] = _features(v["lru_lambda"][0])
    arrays["state_lru_h"] = _features(v["state_lru_h"][0, 0])
    arrays["state_dn_conv"] = _features(v["state_dn_conv"][0, 0])
    arrays["state_lru_conv"] = _features(v["state_lru_conv"][0, 0])
    arrays["dn_norm_g"] = v["dn_norm_g"][0].reshape(P, 1)
    arrays["dn_a_log"], arrays["dn_dt_bias"] = v["dn_a_log"], v["dn_dt_bias"]
    arrays["lru_w_r"] = np.ascontiguousarray(v["lru_w_r"][0].transpose(1, 0, 2))
    arrays["lru_w_i"] = np.ascontiguousarray(v["lru_w_i"][0].transpose(1, 0, 2))
    arrays["state_dn"] = np.ascontiguousarray(v["state_dn"][0, 0].transpose(1, 0, 2))
    arrays["ln2_g"], arrays["final_g"] = v["ln2_g"], v["final_g"].reshape(1, D)
    arrays["keys"] = np.ascontiguousarray(v["peer_keys"][0].transpose(1, 3, 0, 2).reshape(P, H, NKEYS))
    arrays["uv"] = np.concatenate([v["peer_u"][0], v["peer_v"][0]], 1)

    nc = bacc.Bacc("TRN2", target_bir_lowering=False, num_devices=1)
    arrays = {k: np.ascontiguousarray(x) for k, x in arrays.items()}
    a = {k: nc.dram_tensor(f"in_{k}", x.shape, mybir.dt.from_np(x.dtype), kind="ExternalInput").ap()
         for k, x in arrays.items()}
    o = {k: nc.dram_tensor(f"out_{k}", s, F32, kind="ExternalOutput").ap() for k, s in _OUTS.items()}
    trunk_program(nc, a, o)
    r = run_bass_kernel_spmd(nc, [{f"in_{k}": x for k, x in arrays.items()}], core_ids=[0]).results[0]
    y, tails, last = r["out_y"], r["out_tails"], r["out_lru_last"]

    def rows(x):
        return np.ascontiguousarray(x.transpose(2, 1, 0)).reshape(x.shape[2], -1)

    def conv_state(first, c0, c1):
        return rows(tails[:, c0:c1, first:first + HIST])[None, None]

    def lru_h(n):
        return rows(last[:, :, n:n + 1])[None]

    return (y[None, :TP], y[None, TP:],
            r["out_dn_p"].transpose(1, 0, 2)[None, None], conv_state(0, KC, 4 * KC), lru_h(0), conv_state(0, 0, KC),
            r["out_dn_s"].transpose(1, 0, 2)[None, None], conv_state(HIST, KC, 4 * KC), lru_h(1),
            conv_state(HIST, 0, KC))
```

```python
from contextlib import ExitStack

import concourse.bass as bass
import numpy as np
from concourse import mybir

F32 = mybir.dt.float32
I32 = mybir.dt.int32
U32 = mybir.dt.uint32
ALU = mybir.AluOpType
ACT = mybir.ActivationFunctionType
AX_X = mybir.AxisListType.X
ds = bass.ds

P = 128
D = 1024
KC = D // P
TP, TS = 512, 32
NT = TP + TS
HALF = NT // 2
NTILE = TP // P
H = 8
CW = 4
HIST = CW - 1
PADW = HIST + TP + HIST + TS
SMP0 = HIST + TP + HIST
CONVW = PADW - HIST
YS0 = TP + HIST
EPS = 1e-6
LRU_C = 8.0
NKEYS = 128
TOPK = 16
LEVELS = 7
RING = 4
SLOTS = 8
NEG = -3.0e38

N_LX, N_LY, N_ZG, N_QKV, N_BR = KC, KC, 3 * KC, 3 * KC, KC
N_STREAM = N_LX + N_LY + N_ZG + N_QKV + 3 * N_BR


def trunk_program(nc, a, o):
    ctx = ExitStack()
    with ctx:
        def sb(name, shape, dt=F32):
            return ctx.enter_context(nc.sbuf_tensor(name, shape, dt))

        def sem(name):
            return ctx.enter_context(nc.semaphore(name))

        ident = sb("ident", [P, P])
        ones = sb("ones", [P, P])
        upper = sb("upper", [P, P])
        lvl = sb("lvl", [P, LEVELS, P])
        fold = sb("fold", [P, TS])
        iota16 = sb("iota16", [P, TOPK])
        ln1 = sb("ln1", [P, KC])
        dn_w = sb("dn_w", [P, 3 * KC, CW])
        lru_w = sb("lru_w", [P, KC, CW])
        lru_b = sb("lru_b", [P, KC])
        b_r = sb("b_r", [P, KC])
        b_i = sb("b_i", [P, KC])
        lam = sb("lam", [P, KC])
        h0 = sb("h0", [P, KC])
        dn_hist = sb("dn_hist", [P, 3 * KC, HIST])
        lru_hist = sb("lru_hist", [P, KC, HIST])
        alog = sb("alog", [P, H])
        dtb = sb("dtb", [P, H])
        dn_g = sb("dn_g", [P, 1])
        w_ba = sb("w_ba", [P, KC, 2 * H])
        cn = sb("cn", [P, KC])
        tails = sb("tails", [P, 4 * KC, 2 * HIST])
        lru_last = sb("lru_last", [P, KC, 2])
        spx = sb("spx", [P, KC + (NTILE + 1) * H])
        spl = sb("spl", [P, KC + (NTILE + 1) * H])
        glog = sb("glog", [P, (NTILE + 1) * H])
        rs2 = sb("rs2", [P, NTILE + 1])
        bg = sb("bg", [P, NTILE + 1, 2 * H])
        beta = sb("beta", [P, NTILE + 1, H])
        gcum = sb("gcum", [P, NTILE + 1, H])
        gam_col = sb("gam_col", [P, NTILE + 1, H])
        eps_col = sb("eps_col", [P, 1])

        arena = sb("arena", [P, 46600])

        def view(at, *dims):
            n = int(np.prod(dims))
            v = arena[:, at:at + n]
            if len(dims) == 1:
                return v
            if len(dims) == 2:
                return v.rearrange("p (a b) -> p a b", b=dims[1])
            return v.rearrange("p (a b c) -> p a b c", b=dims[1], c=dims[2])

        W = KC * NT
        n_t = view(0, KC, NT)
        z_t = view(W, KC, NT)
        ga_t = view(2 * W, KC, NT)
        gb_t = view(3 * W, KC, NT)
        ob_t = view(4 * W, KC, NT)
        qkv_t = view(5 * W, 3 * KC, NT)
        lru_a = view(5 * W, KC, NT)
        lru_i = view(6 * W, KC, NT)
        lru_th = view(7 * W, KC, NT)
        TAIL = 8 * W
        wring = [view(TAIL + s * KC * P, KC, P) for s in range(RING)]
        o1 = TAIL + RING * KC * P
        xpad = [view(o1 + s * 552, 552) for s in range(2)]
        ycv = [view(o1 + 1104 + s * 552, 552) for s in range(2)]
        lru_v = [view(o1 + 2208 + s * NT, NT) for s in range(2)]
        gelu_y = view(o1 + 2208 + 2 * NT, KC, NT)
        assert o1 + 2208 + 2 * NT + W <= 46600
        rstd1 = ycv[0][:, 0:NT]
        fin_sq_junk = view(o1 + 2 * D, D)
        sq_x = qkv_t
        homes = iter([k * 1024 for k in range(4)] + [4 * W + k * 1024 for k in range(4)]
                     + [o1 + k * 1024 for k in range(7)])

        def head_buf():
            return view(next(homes), H, P)

        dgam, dbet = head_buf(), head_buf()
        kn, qn = head_buf(), head_buf()
        vn, dec = head_buf(), head_buf()
        gam, nmat = head_buf(), head_buf()
        ct, tinv, tinvt = head_buf(), head_buf(), head_buf()
        pmat, qk = head_buf(), head_buf()
        kend, vtok = head_buf(), head_buf()
        sq_q, sq_k = tinv, tinvt
        rmat, umat = ct, pmat
        o_sb, o_sq = dgam, dbet
        state = {True: sb("state_p", [P, H, P]), False: sb("state_s", [P, H, P])}
        wr_v = view(3 * W, KC, P)
        wi_v = view(3 * W + KC * P, KC, P)

        x2 = view(4 * W, NTILE + 1, D)
        X2END = 4 * W + (NTILE + 1) * D
        w_out = view(X2END, KC, D)
        n2_t = z_t
        q_t = ga_t
        g2 = view(3 * W, D)
        gf = view(3 * W + D, D)
        keys = view(3 * W + 2 * D, H, NKEYS)
        n2 = view(3 * W + 3 * D, D)
        ybuf = view(0, D)
        assert 3 * W + 4 * D <= 4 * W
        qs = view(D, H, P)
        fin = view(2 * D, D)
        fin_sq_t = view(3 * D, D)
        ring = [view(X2END + s * 2 * D, 2 * D) for s in range(SLOTS)]
        o2 = X2END + SLOTS * 2 * D
        assert o2 + 768 + 2 * NT <= 46600
        n2p = view(W, D)
        diag = [view(W + D + b * P, P) for b in range(8)]
        sch = view(o2, 2, NKEYS)
        v16 = sb("v16", [P, 2, TOPK])
        i16 = sb("i16", [P, 2, TOPK], U32)
        i16f = sb("i16f", [P, 2, TOPK])
        cand = view(o2 + 256, 1, TOPK * TOPK)
        hot = view(o2 + 512, TOPK, TOPK)
        top = sb("top", [P, 1, TOPK])
        pos = sb("pos", [P, 1, TOPK], U32)
        posu = sb("posu", [P, 2, TOPK], U32)
        posf = sb("posf", [P, 2, TOPK])
        e12 = sb("e12", [P, 2, TOPK])
        gexp = sb("gexp", [P, TOPK])
        gsum = sb("gsum", [P, 2])
        idx = view(o2 + 768, NT).bitcast(I32)
        gate = view(o2 + 768 + NT, NT)
        qsp = view(W + 2 * D, H, P)
        idxs = [sb(f"idxs{b}", [P, SLOTS], I32) for b in range(2)]
        dots = [sb(f"dots{b}", [P, 2]) for b in range(4)]
        gelu_d = [sb(f"gelu_d{b}", [P, 2]) for b in range(4)]
        ssum = sb("ssum", [P, 4])

        ps = ctx.enter_context(nc.psum_tensor("ps", [P, 8, 512], F32))

        def both(b):
            return ps[:, b:b + 2, 0:HALF]

        params_in = sem("params_in")
        x_in = sem("x_in")
        chunk_in = [sem(f"chunk_in{s}") for s in range(RING)]
        sq_done = sem("sq_done")
        ssq_done = sem("ssq_done")
        root_done = sem("root_done")
        rstd_done = sem("rstd_done")
        n_ready = sem("n_ready")
        ba_done = sem("ba_done")
        prod_ready = sem("prod_ready")
        prod_used = sem("prod_used")
        pad_ready = sem("pad_ready")
        tail_done = sem("tail_done")
        conv_step = sem("conv_step")
        conv_ready = sem("conv_ready")
        conv_used = sem("conv_used")
        lru_sq = sem("lru_sq")
        lru_exp = sem("lru_exp")
        lru_one = sem("lru_one")
        lru_root = sem("lru_root")
        lru_step = sem("lru_step")
        lru_done = sem("lru_done")
        lru_ob_n = sem("lru_ob_n")
        sp_x = sem("sp_x")
        sp_abs = sem("sp_abs")
        sp_log = sem("sp_log")
        sp_sum = sem("sp_sum")
        g_ready = sem("g_ready")
        bg_zero = sem("bg_zero")
        bg_ready = sem("bg_ready")
        gcum_mm = sem("gcum_mm")
        gcum_ready = sem("gcum_ready")
        gam_ready = sem("gam_ready")
        state_zero = sem("state_zero")
        state_in = sem("state_in")

        d_diag = sem("d_diag")
        d_bc = sem("d_bc")
        d_sq = sem("d_sq")
        d_vn = sem("d_vn")
        d_ssq = sem("d_ssq")
        d_root = sem("d_root")
        d_rcp = sem("d_rcp")
        d_norm = sem("d_norm")
        d_diff = sem("d_diff")
        d_min = sem("d_min")
        d_exp = sem("d_exp")
        d_mask = sem("d_mask")
        d_dec = sem("d_dec")
        d_tr = sem("d_tr")
        d_kend = sem("d_kend")
        d_vtok = sem("d_vtok")
        d_kk = sem("d_kk")
        d_nm = sem("d_nm")
        d_qg = sem("d_qg")
        d_ct = sem("d_ct")
        d_p = sem("d_p")
        d_pc = sem("d_pc")
        d_xy = sem("d_xy")
        d_t = sem("d_t")
        d_ks = sem("d_ks")
        d_r1 = sem("d_r1")
        d_r2 = sem("d_r2")
        d_r = sem("d_r")
        d_u = sem("d_u")
        d_uc = sem("d_uc")
        d_os = sem("d_os")
        d_s1 = sem("d_s1")
        d_s = sem("d_s")
        d_oc = sem("d_oc")
        d_oss = sem("d_oss")
        d_or = sem("d_or")
        d_o1 = sem("d_o1")
        d_o2 = sem("d_o2")
        d_og = sem("d_og")

        late_w = sem("late_w")
        late_p = sem("late_p")
        mix_step = sem("mix_step")
        mix_ready = sem("mix_ready")
        out_mm = sem("out_mm")
        x2_ready = sem("x2_ready")
        n2_sq = sem("n2_sq")
        n2_root = sem("n2_root")
        n2_rcp = sem("n2_rcp")
        n2_ready = sem("n2_ready")
        n2_tr = sem("n2_tr")
        n2_copied = sem("n2_copied")

        qs_ready = sem("qs_ready")
        sc_mm = sem("sc_mm")
        sc_ready = sem("sc_ready")
        pick_step = sem("pick_step")
        shift_ready = sem("shift_ready")
        gate_exp = sem("gate_exp")
        idx_ready = sem("idx_ready")
        gate_ready = sem("gate_ready")
        tile_ready = sem("tile_ready")
        idxs_ready = sem("idxs_ready")
        slot_free = sem("slot_free")
        row_in = [sem(f"row_in{s}") for s in range(SLOTS)]
        dot_ready = sem("dot_ready")
        gelu_ready = sem("gelu_ready")
        diag_ready = sem("diag_ready")
        sch_ready = sem("sch_ready")
        acc_mm = sem("acc_mm")
        packed = sem("packed")
        qsp_zero = sem("qsp_zero")
        fin_step = sem("fin_step")
        fin_copy = sem("fin_copy")
        fin_sq = sem("fin_sq")
        fin_root = sem("fin_root")
        y_ready = sem("y_ready")
        y_out = sem("y_out")
        small_out = sem("small_out")

        block = ctx.enter_context(nc.Block())

        PARAMS = [(ident, "ident"), (ones, "ones"), (upper, "upper"), (lvl, "lvl"), (fold, "fold"),
                  (iota16, "iota16"), (ln1, "ln1_g"), (dn_w, "dn_conv_w"), (lru_w, "lru_conv_w"),
                  (lru_b, "lru_conv_b"), (b_r, "lru_b_r"), (b_i, "lru_b_i"), (lam, "lru_lambda"),
                  (h0, "state_lru_h"), (dn_hist, "state_dn_conv"), (lru_hist, "state_lru_conv"),
                  (dn_g, "dn_norm_g"), (w_ba, "w_ba")]
        N_PARAMS = 16 * (len(PARAMS) + 4)

        PR_GATE = N_LX + N_LY
        PR_ZG = PR_GATE + 2 * KC
        PR_QKV = PR_ZG + N_ZG
        PR_BB = PR_QKV + N_QKV
        PR_BA = PR_BB + N_BR
        PR_Q = PR_BA + N_BR
        PR_END = PR_Q + N_BR
        SHIFT = 2 * KC
        CONVS = N_LX + N_QKV
        NPAIR = TOPK // 2
        PICK_AT = (2, 5)
        LAG = 2
        QUARTERS = P // TS
        SPREAD = H // QUARTERS
        assert SPREAD == LAG

        def rows(t):
            return TS if isinstance(t, int) and t == NTILE else P

        def uses(k):
            return k * 16

        def heads(bank, L):
            return ps[0:L, bank:bank + 2, :].rearrange("p b (h i) -> p (b h) i", h=4)

        HG = H // 2
        GROUPS = [(g, slice(g * HG, (g + 1) * HG)) for g in range(2)]

        def nth(t, g):
            return t * 2 + (g + 1)

        def nth_level(t, lv, g):
            return t * (2 * LEVELS) + (2 * lv + g + 1)

        def nth_inner(t, lv, g):
            return t * (2 * (LEVELS - 1)) + (2 * (lv - 1) + g + 1)

        def wait_apart(eng, sem_, value, constant):
            if not isinstance(value, int):
                value = eng.compute_val(value)
            eng.wait_ge(constant, 1)
            eng.wait_ge(sem_, value)

        def chain(eng, sem_, base, constant=None):
            n = [0]

            def link(ins):
                n[0] += 1
                ins.then_inc(sem_, 1)
                if constant is not None:
                    wait_apart(eng, sem_, base + n[0], constant)
                else:
                    eng.wait_ge(sem_, base + n[0])
            return link, n

        def part(m, c, cols):
            return m[:, HG * c:HG * (c + 1), cols]

        @block.sync
        def _(sp):
            for c in range(KC):
                sp.dma_start(n_t[:, c, :], a["x_t"][:, c, :]).then_inc(x_in, 16)
            for dst, name in PARAMS:
                sp.dma_start(dst[:], a[name]).then_inc(params_in, 16)
            for dst, name in ((wr_v, "lru_w_r"), (wi_v, "lru_w_i")):
                sp.dma_start(dst, a[name]).then_inc(params_in, 16)
            for dst, name in ((alog, "dn_a_log"), (dtb, "dn_dt_bias")):
                sp.dma_start(dst[:], a[name].broadcast_to([P, H])).then_inc(params_in, 16)
            sp.dma_start(state[False][:], a["state_dn"]).then_inc(state_in, 16)

            for s in range(RING):
                sp.dma_start(wring[s], a["stream"][s]).then_inc(chunk_in[s], 16)
            refills = PR_GATE // RING + 1
            for first, last, shift in ((1, refills, 0), (refills, N_STREAM // RING, SHIFT)):
                with sp.Fori(first, last) as i:
                    for s in range(RING):
                        sp.wait_ge(prod_ready, i * RING + (s - RING + 1 + shift))
                        sp.dma_start(wring[s], a["stream"][ds(i * RING + s, 1)].rearrange(
                            "o p k n -> (o p) k n")).then_inc(chunk_in[s], 16)

            sp.wait_ge(n2_tr, NTILE + 1)
            sp.wait_ge(prod_ready, PR_END)
            for q in range(QUARTERS):
                sp.dma_start(n2p[q * TS:(q + 1) * TS, :], n2[0:TS, :]).then_inc(packed, 16)
            sp.wait_ge(y_out, uses(NTILE + 1))
            sp.wait_ge(small_out, uses(4))

        @block.tensor
        def _(pe):
            def row(m, c):
                return m[:, ds(c, 1), :].rearrange("p o n -> p (o n)")

            def quads(first, last, shift, rhs, head=0):
                def body(i, unheld):
                    for s in range(RING):
                        n = i * RING + s
                        pe.wait_ge(chunk_in[s], uses(i + 1))
                        if s >= unheld:
                            pe.wait_ge(prod_used, n + (shift - 1))
                        b = 2 * ((s + shift) % 2)
                        for half in range(2):
                            for k in range(KC):
                                mm = pe.matmul(ps[:, b + half, 0:HALF], wring[s][:, k, :],
                                               rhs[:, k, half * HALF:(half + 1) * HALF],
                                               start=(k == 0), stop=(k == KC - 1))
                        mm.then_inc(prod_ready, 1)
                i0 = first // RING
                if first == 0:
                    body(0, 2)
                    i0 = 1
                with pe.Fori(i0, last // RING) as i:
                    body(i, 0)

            pe.wait_ge(params_in, N_PARAMS)
            pe.wait_ge(sq_done, 1)
            for half in range(2):
                for c in range(KC):
                    mm = pe.matmul(ps[:, half, 0:HALF], ones[:, :], sq_x[:, c, half * HALF:(half + 1) * HALF],
                                   start=(c == 0), stop=(c == KC - 1))
            mm.then_inc(ssq_done, 1)
            pe.wait_ge(n_ready, KC)
            for t in range(NTILE + 1):
                n = rows(t)
                for c in range(KC):
                    mm = pe.matmul(ps[0:n, 4, t * 16:(t + 1) * 16], n_t[:, c, t * P:t * P + n], w_ba[:, c, :],
                                   start=(c == 0), stop=(c == KC - 1))
            mm.then_inc(ba_done, 1)
            quads(0, PR_GATE, 0, n_t)
            for n in range(KC):
                pe.wait_ge(conv_used, n + 1)
                for j, w in enumerate((wr_v, wi_v)):
                    pr = PR_GATE + 2 * n + j
                    pe.wait_ge(prod_used, pr - 1)
                    for half in range(2):
                        mm = pe.matmul(ps[:, 2 * (pr % 2) + half, 0:HALF], w[:, n, :],
                                       ob_t[:, n, half * HALF:(half + 1) * HALF], start=True, stop=True)
                    mm.then_inc(prod_ready, 1)
            pe.wait_ge(g_ready, 1)
            pe.matmul(ps[:, 5, 0:(NTILE + 1) * H], upper[:, :], glog[:, :], start=True, stop=True
                      ).then_inc(gcum_mm, 1)
            quads(PR_GATE, PR_BB - SHIFT, SHIFT, n_t)
            pe.wait_ge(lru_ob_n, KC)
            quads(PR_BB - SHIFT, PR_BA - SHIFT, SHIFT, ob_t)

            def delta(t, first):
                L = rows(t)
                NL = (L - 1).bit_length()
                S = state[L == P]
                if first:
                    pe.wait_ge(prod_used, PR_BA)
                else:
                    pe.wait_ge(d_og, nth(t - 1, 1))
                for g, hs in GROUPS:
                    pe.wait_ge(d_diag, nth(t, g))
                    for b, src in ((0, dgam), (2, dbet)):
                        mm = pe.matmul(heads(b, P)[:, hs, 0:L], ones[0:L, :], src[0:L, hs, 0:L],
                                       start=True, stop=True)
                    mm.then_inc(d_bc, 1)
                if first:
                    pe.wait_ge(gcum_ready, 1)
                for g, hs in GROUPS:
                    pe.wait_ge(d_sq, nth(t, g))
                    for b, src in ((4, sq_q), (6, sq_k)):
                        mm = pe.matmul(heads(b, P)[:, hs, 0:L], ones[:, :], src[:, hs, 0:L],
                                       start=True, stop=True)
                    mm.then_inc(d_ssq, 1)
                for g, hs in GROUPS:
                    pe.wait_ge(d_norm, nth(t, g))
                    pe.wait_ge(d_vn, nth(t, g))
                    for h in range(hs.start, hs.stop):
                        pe.transpose(heads(4, L)[:, h, :], kn[:, h, 0:L], ident[:, :])
                        mm = pe.transpose(heads(6, L)[:, h, :], vn[:, h, 0:L], ident[:, :])
                    mm.then_inc(d_tr, 1)
                for g, hs in GROUPS:
                    pe.wait_ge(d_dec, nth(t, g))
                    for h in range(hs.start, hs.stop):
                        pe.matmul(heads(0, L)[:, h, 0:L], kn[:, h, 0:L], kn[:, h, 0:L], start=True, stop=True)
                        mm = pe.matmul(heads(2, L)[:, h, 0:L], kn[:, h, 0:L], qn[:, h, 0:L], start=True, stop=True)
                    mm.then_inc(d_kk, 1)
                for lv in range(NL):
                    for g, hs in GROUPS:
                        pe.wait_ge(d_ct, nth_level(t, lv, g))
                        if lv:
                            pe.wait_ge(d_t, nth_level(t, lv - 1, g))
                        for h in range(hs.start, hs.stop):
                            mm = pe.matmul(heads(0, L)[:, h, 0:L], ct[0:L, h, 0:L],
                                           tinv[0:L, h, 0:L] if lv else ident[0:L, 0:L], start=True, stop=True)
                        mm.then_inc(d_p, 1)
                    if lv == 0:
                        continue
                    for g, hs in GROUPS:
                        pe.wait_ge(d_pc, nth_inner(t, lv, g))
                        if lv == 1:
                            pe.wait_ge(d_kend, nth(t, g))
                            pe.wait_ge(d_vtok, nth(t, g))
                        for h in range(hs.start, hs.stop):
                            if lv < NL - 1:
                                pe.matmul(heads(4, L)[:, h, 0:L], tinvt[0:L, h, 0:L], pmat[0:L, h, 0:L],
                                          start=True, stop=True)
                            mm = pe.matmul(heads(6, L)[:, h, 0:L], pmat[0:L, h, 0:L], tinvt[0:L, h, 0:L],
                                           start=True, stop=True)
                        mm.then_inc(d_xy, 1)
                if L != P:
                    pe.wait_ge(state_in, 16)
                elif first:
                    pe.wait_ge(state_zero, 1)
                else:
                    pe.wait_ge(d_s, nth(t - 1, 1))
                for g, hs in GROUPS:
                    pe.wait_ge(d_t, nth_level(t, NL - 1, g))
                    for h in range(hs.start, hs.stop):
                        mm = pe.matmul(heads(0, L)[:, h, :], kn[:, h, 0:L], S[:, h, :], start=True, stop=True)
                    mm.then_inc(d_ks, 1)
                for g, hs in GROUPS:
                    pe.wait_ge(d_r, nth(t, g))
                    for h in range(hs.start, hs.stop):
                        mm = pe.matmul(heads(2, L)[:, h, :], tinvt[0:L, h, 0:L], rmat[0:L, h, :],
                                       start=True, stop=True)
                    mm.then_inc(d_u, 1)
                for g, hs in GROUPS:
                    pe.wait_ge(d_uc, nth(t, g))
                    pe.wait_ge(d_qg, nth(t, g))
                    for h in range(hs.start, hs.stop):
                        pe.matmul(heads(4, P)[:, h, 0:L], S[:, h, :], qn[:, h, 0:L], start=True, stop=False)
                        pe.matmul(heads(4, P)[:, h, 0:L], umat[0:L, h, :], qk[0:L, h, 0:L],
                                  start=False, stop=True)
                    for h in range(hs.start, hs.stop):
                        mm = pe.matmul(heads(6, P)[:, h, :], kend[0:L, h, :], umat[0:L, h, :],
                                       start=True, stop=True)
                    mm.then_inc(d_os, 1)
                for g, hs in GROUPS:
                    pe.wait_ge(d_oc, nth(t, g))
                    mm = pe.matmul(heads(0, P)[:, hs, 0:L], ones[:, :], o_sq[:, hs, 0:L], start=True, stop=True)
                    mm.then_inc(d_oss, 1)

            delta(0, True)
            with pe.Fori(1, NTILE) as t:
                delta(t, False)
            delta(NTILE, False)
            pe.wait_ge(d_og, nth(NTILE, 1))
            quads(PR_BA - SHIFT, PR_Q - SHIFT, SHIFT, z_t)

            pe.wait_ge(mix_ready, KC)
            pe.wait_ge(late_w, uses(3))
            for t in range(NTILE + 1):
                n = rows(t)
                if t:
                    pe.wait_ge(x2_ready, t)
                for half in range(2):
                    for k in range(KC):
                        mm = pe.matmul(ps[0:n, 4 + half, :], n_t[:, k, t * P:t * P + n],
                                       w_out[:, k, half * 512:(half + 1) * 512], start=(k == 0), stop=(k == KC - 1))
                mm.then_inc(out_mm, 1)
                pe.wait_ge(n2_ready, t + 1)
                if t:
                    pe.wait_ge(n2_copied, t)
                for c in range(KC):
                    mm = pe.transpose(heads(6, P)[:, c, 0:n], n2[0:n, c * P:(c + 1) * P], ident[0:n, 0:n])
                mm.then_inc(n2_tr, 1)
            pe.wait_ge(n2_copied, NTILE + 1)
            quads(PR_Q - SHIFT, N_STREAM, SHIFT, n2_t)

            def scores(t):
                pe.wait_ge(qs_ready, t + 1)
                if not isinstance(t, int) or t:
                    pe.wait_ge(sch_ready, t * H)
                for h in range(H if not isinstance(t, int) or t < NTILE else 0):
                    for p in range(2):
                        mm = pe.matmul(heads(4 + 2 * p, P)[:, h, :], qs[64 * p:64 * p + 64, h, :],
                                       keys[64 * p:64 * p + 64, h, :], start=True, stop=True)
                for r in range(SPREAD if isinstance(t, int) and t == NTILE else 0):
                    for p in range(2):
                        for j in range(QUARTERS):
                            h = SPREAD * j + r
                            mm = pe.matmul(heads(4 + 2 * p, P)[:, r, :], qsp[64 * p:64 * p + 64, h, :],
                                           keys[64 * p:64 * p + 64, h, :], start=(j == 0), stop=(j == QUARTERS - 1))
                mm.then_inc(sc_mm, 1)

            def experts(t, steps):
                L = rows(t)
                if not isinstance(t, int) or t:
                    pe.wait_ge(fin_copy, t)
                for half in range(2):
                    pe.matmul(ps[0:L, half, :], ident[0:L, 0:L],
                              row(x2, t)[0:L, half * 512:(half + 1) * 512], start=True, stop=False)

                def step(i, last):
                    for k in range(TOPK):
                        pe.wait_ge(diag_ready, (t * H + i) * TOPK + (k + 1))
                        for half in range(2):
                            mm = pe.matmul(ps[0:L, half, :], diag[k % 8][:, 0:L],
                                           ring[k % SLOTS][:, D + half * 512:D + (half + 1) * 512],
                                           start=False, stop=last and k == TOPK - 1)
                        mm.then_inc(slot_free, 1)
                if steps == H:
                    with pe.Fori(0, H - LAG) as i:
                        step(i, False)
                    scores(t + 1)
                for i in range(steps - LAG, steps):
                    step(i, i == steps - 1)

            pe.wait_ge(late_p, uses(3))
            scores(0)
            with pe.Fori(0, NTILE - 1) as t:
                experts(t, H)
            experts(NTILE - 1, H)
            experts(NTILE, SPREAD)

        @block.scalar
        def _(act):
            def evac(j, pr, hist, slot, held):
                act.wait_ge(prod_ready, pr + 1)
                if held:
                    act.wait_ge(conv_ready, j - 1)
                    act.wait_ge(tail_done, j - 1)
                b = 2 * slot
                x = xpad[slot]
                act.copy(x[:, HIST:HIST + HALF], ps[:, b, 0:HALF])
                act.copy(x[:, HIST + HALF:HIST + TP], ps[:, b + 1, 0:TP - HALF])
                act.copy(x[:, SMP0:SMP0 + TS], ps[:, b + 1, TP - HALF:HALF]).then_inc(prod_used, 1)
                act.copy(x[:, TP + HIST:SMP0], hist).then_inc(pad_ready, 1)

            def post(j, slot, dst, func, bias=0.0):
                act.wait_ge(conv_ready, j + 1)
                y = ycv[slot]
                act.activation(dst[:, 0:TP], y[:, 0:TP], func, bias=bias)
                act.activation(dst[:, TP:NT], y[:, YS0:YS0 + TS], func, bias=bias).then_inc(conv_used, 1)

            def row(m, c):
                return m[:, ds(c, 1), :].rearrange("p o n -> p (o n)")

            act.wait_ge(x_in, uses(KC))
            act.activation(sq_x[:, 0:KC, :], n_t[:, :, :], ACT.Square).then_inc(sq_done, 1)
            act.wait_ge(ssq_done, 1)
            act.wait_ge(bg_zero, 1)
            act.activation(rstd1.rearrange("p (b n) -> p b n", b=2), both(0), ACT.Sqrt, scale=1.0 / D,
                           bias=eps_col[:, 0:1]).then_inc(root_done, 1)
            act.wait_ge(sp_x, 1)
            act.activation(spl[:, :], spx[:, :], ACT.Abs).then_inc(sp_abs, 1)
            act.wait_ge(sp_abs, 1)
            act.activation(spl[:, :], spl[:, :], ACT.Exp, scale=-1.0).then_inc(sp_abs, 1)
            act.activation(alog[:, :], alog[:, :], ACT.Exp)
            act.wait_ge(sp_abs, 2)
            act.activation(spl[:, :], spl[:, :], ACT.Ln, bias=1.0).then_inc(sp_log, 1)
            act.activation(beta[:, :, :], bg[:, :, 0:H], ACT.Sigmoid).then_inc(sp_log, 1)

            def conv_group(first, last, pr0, hist, c0, finish):
                def step(i, j, s, held, has_prev):
                    evac(j, j + (pr0 - first), row(hist, j - c0), s, held)
                    if has_prev:
                        finish(j - 1, 1 - s)
                step(None, first, 0, first > 0, False)
                step(None, first + 1, 1, first > 0, True)
                with act.Fori(first // 2 + 1, last // 2) as i:
                    for s in range(2):
                        step(i, i * 2 + s, s, True, True)
                finish(last - 1, 1)

            conv_group(0, N_LX, 0, lru_hist, 0,
                       lambda j, s: post(j, s, row(ob_t, j), ACT.Identity, bias=lru_b[:, ds(j, 1)]))
            with act.Fori(0, N_LY // 2) as i:
                for s in range(2):
                    act.wait_ge(prod_ready, i * 2 + (N_LX + s + 1))
                    act.activation(row(gelu_y, i * 2 + s).rearrange("p (b n) -> p b n", b=2), both(2 * s),
                                   ACT.Gelu_apprx_tanh).then_inc(prod_used, 1)
            with act.Fori(0, KC) as n:
                for s, (dst, b) in enumerate(((lru_a, b_r), (lru_i, b_i))):
                    act.wait_ge(prod_ready, n * 2 + (PR_GATE + s + 1))
                    act.activation(row(dst, n).rearrange("p (b n) -> p b n", b=2), both(2 * s), ACT.Sigmoid,
                                   bias=b[:, ds(n, 1)]).then_inc(prod_used, 1)
            act.wait_ge(prod_used, PR_ZG)
            act.wait_ge(g_ready, 1)
            with act.Fori(0, KC) as n:
                act.activation(row(lru_th, n), row(lru_a, n), ACT.Tanh, scale=cn[:, ds(n, 1)])
                act.activation(row(lru_a, n), row(lru_a, n), ACT.Exp, scale=cn[:, ds(n, 1)]).then_inc(lru_exp, 1)
            with act.Fori(0, KC) as n:
                act.wait_ge(lru_one, n + 1)
                act.activation(row(lru_th, n), row(lru_th, n), ACT.Sqrt, scale=-1.0).then_inc(lru_root, 1)
            for first, dst, func in ((0, z_t, ACT.Silu), (KC, ga_t, ACT.Sigmoid), (2 * KC, gb_t, ACT.Sigmoid)):
                with act.Fori(0, KC // 2) as i:
                    for s in range(2):
                        act.wait_ge(prod_ready, i * 2 + (PR_ZG + first + s + 1))
                        act.activation(row(dst, i * 2 + s).rearrange("p (b n) -> p b n", b=2), both(2 * s),
                                       func).then_inc(prod_used, 1)
            act.wait_ge(lru_done, 1)
            conv_group(N_LX, CONVS, PR_QKV, dn_hist, N_LX,
                       lambda j, s: post(j, s, row(qkv_t, j - N_LX), ACT.Silu))
            act.wait_ge(gcum_ready, 1)
            act.activation(gam_col[:, :, :], gcum[:, :, :], ACT.Exp).then_inc(gam_ready, 1)

            act.wait_ge(prod_ready, PR_BA)
            act.wait_ge(conv_used, CONVS)
            act.wait_ge(tail_done, CONVS)

            def delta(t, first):
                L = rows(t)
                NL = (L - 1).bit_length()
                cols = ds(t * P, L)
                if not first:
                    act.wait_ge(d_os, nth(t - 1, 1))
                for g, hs in GROUPS:
                    act.activation(sq_q[:, hs, 0:L], part(qkv_t, g, cols), ACT.Square)
                    act.activation(sq_k[:, hs, 0:L], part(qkv_t, 2 + g, cols), ACT.Square).then_inc(d_sq, 1)
                for g, hs in GROUPS:
                    act.copy(vn[:, hs, 0:L], part(qkv_t, 4 + g, cols)).then_inc(d_vn, 1)
                for g, hs in GROUPS:
                    act.wait_ge(d_ssq, nth(t, g))
                    act.activation(ct[:, hs, 0:L], heads(4, P)[:, hs, 0:L], ACT.Sqrt, bias=eps_col[:, 0:1])
                    act.activation(pmat[:, hs, 0:L], heads(6, P)[:, hs, 0:L], ACT.Sqrt, bias=eps_col[:, 0:1]
                                   ).then_inc(d_root, 1)
                for g, hs in GROUPS:
                    act.wait_ge(d_min, nth(t, g))
                    act.activation(dec[0:L, hs, 0:L], dec[0:L, hs, 0:L], ACT.Exp)
                    act.activation(gam[:, hs, 0:L], heads(0, P)[:, hs, 0:L], ACT.Exp).then_inc(d_exp, 1)
                for g, hs in GROUPS:
                    act.wait_ge(d_tr, nth(t, g))
                    act.copy(vtok[0:L, hs, :], heads(6, L)[:, hs, :]).then_inc(d_vtok, 1)
                for lv in range(1, NL):
                    for g, hs in GROUPS:
                        act.wait_ge(d_p, nth_level(t, lv, g))
                        act.copy(pmat[0:L, hs, 0:L], heads(0, L)[:, hs, 0:L]).then_inc(d_pc, 1)
                for g, hs in GROUPS:
                    act.wait_ge(d_u, nth(t, g))
                    act.copy(umat[0:L, hs, :], heads(2, L)[:, hs, :]).then_inc(d_uc, 1)
                for g, hs in GROUPS:
                    act.wait_ge(d_os, nth(t, g))
                    act.copy(o_sb[:, hs, 0:L], heads(4, P)[:, hs, 0:L])
                    act.activation(o_sq[:, hs, 0:L], heads(4, P)[:, hs, 0:L], ACT.Square).then_inc(d_oc, 1)
                for g, hs in GROUPS:
                    act.wait_ge(d_oss, nth(t, g))
                    act.activation(o_sq[:, hs, 0:L], heads(0, P)[:, hs, 0:L], ACT.Sqrt, scale=1.0 / P,
                                   bias=eps_col[:, 0:1]).then_inc(d_or, 1)

            delta(0, True)
            with act.Fori(1, NTILE) as t:
                delta(t, False)
            delta(NTILE, False)

            for t in range(NTILE + 1):
                n = rows(t)
                act.wait_ge(x2_ready, t + 1)
                act.activation(fin_sq_junk[0:n, :], x2[0:n, t, :], ACT.Square, accum_out=ssum[0:n, 0:1]).then_inc(n2_sq, 1)
                act.wait_ge(n2_sq, t + 1)
                act.activation(ssum[0:n, 1:2], ssum[0:n, 0:1], ACT.Sqrt, scale=1.0 / D,
                               bias=eps_col[0:n, 0:1]).then_inc(n2_root, 1)
                act.wait_ge(n2_tr, t + 1)
                act.copy(n2_t[:, :, t * P:t * P + n], heads(6, P)[:, :, 0:n]).then_inc(n2_copied, 1)
            with act.Fori(0, KC // 2) as i:
                for s in range(2):
                    act.wait_ge(prod_ready, i * 2 + (PR_Q + s + 1))
                    act.copy(row(q_t, i * 2 + s).rearrange("p (b n) -> p b n", b=2), both(2 * s)
                             ).then_inc(prod_used, 1)

            act.wait_ge(prod_used, PR_END)

            def queries(t):
                if not isinstance(t, int) or t:
                    act.wait_ge(sc_mm, t)
                act.copy(qs[:, :, :], q_t[:, :, ds(t * P, P)]).then_inc(qs_ready, 1)

            def spread_queries():
                act.wait_ge(qsp_zero, 1)
                for j in range(QUARTERS):
                    hs = slice(SPREAD * j, SPREAD * (j + 1))
                    ins = act.copy(qsp[:, hs, j * TS:(j + 1) * TS], q_t[:, hs, TP:NT])
                ins.then_inc(qs_ready, 1)

            flat = ps[:, :, :].rearrange("p b n -> p (b n)")

            def pick_scores(t, i, first=False):
                act.wait_ge(sc_mm, t + 1)
                if not first:
                    act.wait_ge(idx_ready, t * H + i)
                for p in range(2):
                    c = act.copy(sch[:, p, :], flat[:, ds(i * P + (2048 + p * 1024), P)])
                c.then_inc(sch_ready, 1)

            def pick_gates(t, i):
                act.wait_ge(shift_ready, t * H + i + 1)
                act.activation(gexp[:, :], gexp[:, :], ACT.Exp).then_inc(gate_exp, 1)

            def gelus(t, i, pairs):
                for u in pairs:
                    act.wait_ge(dot_ready, (t * H + i) * NPAIR + (u + 1))
                    act.activation(gelu_d[u % 4][:, :], dots[u % 4][:, :], ACT.Gelu).then_inc(gelu_ready, 1)

            def experts(t):
                for first, last, t_pick, shift in ((0, H - LAG, t, LAG), (H - LAG, H, t + 1, LAG - H)):
                    with act.Fori(first, last) as i:
                        pick_scores(t_pick, i + shift)
                        gelus(t, i, range(PICK_AT[1] + 1))
                        pick_gates(t_pick, i + shift)
                        gelus(t, i, range(PICK_AT[1] + 1, NPAIR))

            def store(t):
                act.wait_ge(y_ready, t + 1)
                act.dma_start(o["y"][ds(t * P, rows(t)), :], ybuf[0:rows(t), :]).then_inc(y_out, 16)

            def finish(t):
                L = rows(t)
                act.wait_ge(slot_free, (t + 1) * P + SLOTS if L == P else SLOTS + NTILE * P + TS)
                act.copy(fin[0:L, :], ps[0:L, 0:2, :].rearrange("p b n -> p (b n)")).then_inc(fin_copy, 1)
                act.wait_ge(fin_copy, t + 1)
                act.activation(fin_sq_t[0:L, :], fin[0:L, :], ACT.Square, accum_out=ssum[0:L, 0:1]
                               ).then_inc(fin_sq, 1)
                act.wait_ge(fin_sq, t + 1)
                act.activation(ssum[0:L, 1:2], ssum[0:L, 0:1], ACT.Sqrt, scale=1.0 / D,
                               bias=eps_col[0:L, 0:1]).then_inc(fin_root, 1)

            queries(0)
            for i in range(LAG):
                pick_scores(0, i, i == 0)
                pick_gates(0, i)
            queries(1)
            experts(0)
            finish(0)
            with act.Fori(1, NTILE - 1) as t:
                queries(t + 1)
                experts(t)
                store(t - 1)
                finish(t)
            spread_queries()
            experts(NTILE - 1)
            store(NTILE - 2)
            finish(NTILE - 1)
            store(NTILE - 1)
            with act.Fori(0, SPREAD) as i:
                gelus(NTILE, i, range(NPAIR))
            finish(NTILE)
            store(NTILE)

        @block.gpsimd
        def _(pool):
            pool.memset(state[True][:, :, :], 0.0).then_inc(state_zero, 1)
            with pool.Fori(0, CONVS // 2) as i:
                for s in range(2):
                    pool.wait_ge(pad_ready, i * 2 + (s + 1))
                    to = tails[:, ds(i * 2 + s, 1), :].rearrange("p o n -> p (o n)")
                    pool.tensor_copy(to[:, 0:HIST], xpad[s][:, TP:TP + HIST])
                    pool.tensor_copy(to[:, HIST:2 * HIST], xpad[s][:, PADW - HIST:PADW]).then_inc(tail_done, 1)
            pool.wait_ge(tail_done, CONVS)
            pool.dma_start(o["tails"], tails[:, :, :]).then_inc(small_out, 16)
            pool.wait_ge(lru_done, 1)
            pool.dma_start(o["lru_last"], lru_last[:, :, :]).then_inc(small_out, 16)
            pool.wait_ge(d_s, nth(NTILE - 1, 1))
            pool.dma_start(o["dn_p"], state[True][:, :, :]).then_inc(small_out, 16)
            pool.wait_ge(d_s, nth(NTILE, 1))
            pool.dma_start(o["dn_s"], state[False][:, :, :]).then_inc(small_out, 16)
            pool.wait_ge(d_og, nth(NTILE, 1))
            pool.dma_start(w_out, a["w_out"]).then_inc(late_w, 16)
            pool.dma_start(x2[:, 0:NTILE, :], a["x_prompt"].rearrange("(t p) d -> p t d", p=P)).then_inc(late_w, 16)
            pool.dma_start(x2[0:TS, NTILE, :], a["x_sample"]).then_inc(late_w, 16)
            pool.wait_ge(mix_ready, KC)
            pool.dma_start(g2, a["ln2_g"].broadcast_to([P, D])).then_inc(late_p, 16)
            pool.dma_start(gf, a["final_g"].broadcast_to([P, D])).then_inc(late_p, 16)
            pool.dma_start(keys, a["keys"]).then_inc(late_p, 16)

            def gathers(t, steps):
                with pool.Fori(0, steps) as i:
                    n = t * H + i
                    wait_apart(pool, idx_ready, n + 1, state_zero)
                    for b in range(2):
                        pool.wait_ge(slot_free, n * TOPK + (SLOTS * b + 1))
                        pool.tensor_copy(idxs[b][:, :], idx[:, ds(n * TOPK + SLOTS * b, SLOTS)]
                                         ).then_inc(idxs_ready, 1)
                        wait_apart(pool, idxs_ready, n * 2 + (b + 1), idx_ready)
                        for s in range(SLOTS):
                            wait_apart(pool, slot_free, n * TOPK + (SLOTS * b + s + 1), idx_ready)
                            pool.indirect_dma_start(
                                out=ring[s], out_offset=None, in_=a["uv"],
                                in_offset=bass.IndirectOffsetOnAxis(ap=idxs[b][:, s:s + 1], axis=0),
                            ).then_inc(row_in[s], 16)

            with pool.Fori(0, NTILE) as t:
                gathers(t, H)
            gathers(NTILE, SPREAD)

        @block.vector
        def _(dve):
            def row(m, c):
                return m[:, ds(c, 1), :].rearrange("p o n -> p (o n)")

            dve.memset(bg[:, :, :], 0.0)
            for s in range(2):
                dve.memset(xpad[s][:, 0:HIST], 0.0)
            dve.memset(eps_col[:, :], EPS).then_inc(bg_zero, 1)
            dve.wait_ge(root_done, 1)
            dve.wait_ge(params_in, N_PARAMS)
            dve.reciprocal(rstd1, rstd1).then_inc(rstd_done, 1)
            dve.wait_ge(rstd_done, 1)
            for c in range(KC):
                dve.scalar_tensor_tensor(out=n_t[:, c, :], in0=n_t[:, c, :], scalar=ln1[:, c:c + 1], in1=rstd1,
                                         op0=ALU.mult, op1=ALU.mult).then_inc(n_ready, 1)
            dve.wait_ge(ba_done, 1)
            dve.wait_ge(bg_zero, 1)
            dve.tensor_copy(bg[:, 0:NTILE, :], ps[:, 4, 0:NTILE * 16].rearrange("p (t n) -> p t n", t=NTILE))
            dve.tensor_copy(bg[0:TS, NTILE, :], ps[0:TS, 4, NTILE * 16:NTILE * 16 + 16]).then_inc(bg_ready, 1)
            dve.wait_ge(bg_ready, 1)
            dve.tensor_scalar(spx[:, 0:KC], lam[:, :], -1.0, None, ALU.mult)
            dve.tensor_tensor(spx[:, KC:].rearrange("p (t h) -> p t h", h=H), bg[:, :, H:2 * H],
                              dtb[:, :].unsqueeze(1).broadcast_to([P, NTILE + 1, H]), ALU.add).then_inc(sp_x, 1)
            dve.wait_ge(sp_log, 2)
            dve.scalar_tensor_tensor(out=spx[:, :], in0=spx[:, :], scalar=0.0, in1=spl[:, :],
                                     op0=ALU.max, op1=ALU.add).then_inc(sp_sum, 1)
            dve.wait_ge(sp_sum, 1)
            dve.tensor_scalar(cn[:, :], spx[:, 0:KC], -LRU_C, None, ALU.mult)
            dve.scalar_tensor_tensor(out=glog[:, :].rearrange("p (t h) -> p t h", h=H),
                                     in0=spx[:, KC:].rearrange("p (t h) -> p t h", h=H), scalar=-1.0,
                                     in1=alog[:, :].unsqueeze(1).broadcast_to([P, NTILE + 1, H]),
                                     op0=ALU.mult, op1=ALU.mult).then_inc(g_ready, 1)

            def conv(j, w, s, held):
                dve.wait_ge(pad_ready, j + 1)
                if held:
                    dve.wait_ge(conv_used, j - 1)
                x, y = xpad[s], ycv[s]
                ins = dve.tensor_scalar(y[:, 0:CONVW], x[:, 0:CONVW], w[:, 0:1], None, ALU.mult)
                for k in range(1, CW):
                    ins.then_inc(conv_step, 1)
                    dve.wait_ge(conv_step, j * HIST + k)
                    ins = dve.scalar_tensor_tensor(out=y[:, 0:CONVW], in0=x[:, k:k + CONVW], scalar=w[:, k:k + 1],
                                                   in1=y[:, 0:CONVW], op0=ALU.mult, op1=ALU.add)
                ins.then_inc(conv_ready, 1)

            for j in range(2):
                conv(j, lru_w[:, j, :], j, False)
            with dve.Fori(1, N_LX // 2) as i:
                for s in range(2):
                    conv(i * 2 + s, row(lru_w, i * 2 + s), s, True)
            with dve.Fori(0, KC // 2) as i:
                for s in range(2):
                    n = i * 2 + s
                    dve.wait_ge(lru_exp, n + 1)
                    dve.tensor_tensor(lru_v[s], row(lru_a, n), row(lru_a, n), ALU.mult).then_inc(lru_sq, 1)
                    dve.wait_ge(lru_sq, n + 1)
                    dve.scalar_tensor_tensor(out=row(lru_th, n), in0=lru_v[s], scalar=1.0, in1=row(lru_th, n),
                                             op0=ALU.add, op1=ALU.mult).then_inc(lru_one, 1)
            with dve.Fori(0, KC) as n:
                A, I = row(lru_a, n), row(lru_i, n)
                link, made = chain(dve, lru_step, n * 3)
                link(dve.tensor_tensor(I, I, row(ob_t, n), ALU.mult))
                dve.wait_ge(lru_root, n + 1)
                link(dve.tensor_tensor(I, I, row(lru_th, n), ALU.mult))
                dve.tensor_tensor_scan(A[:, 0:TP], A[:, 0:TP], I[:, 0:TP], 0.0, ALU.mult, ALU.add)
                link(dve.tensor_tensor_scan(A[:, TP:NT], A[:, TP:NT], I[:, TP:NT], h0[:, ds(n, 1)],
                                            ALU.mult, ALU.add))
                dve.tensor_tensor(row(ob_t, n), A, row(gelu_y, n), ALU.mult).then_inc(lru_ob_n, 1)
                assert made[0] == 3
            dve.wait_ge(lru_ob_n, KC)
            dve.tensor_copy(lru_last[:, :, 0:1], lru_a[:, :, TP - 1:TP])
            dve.tensor_copy(lru_last[:, :, 1:2], lru_a[:, :, NT - 1:NT]).then_inc(lru_done, 1)
            dve.wait_ge(gcum_mm, 1)
            dve.tensor_copy(gcum[:, :, :], ps[:, 5, 0:(NTILE + 1) * H].rearrange("p (t h) -> p t h", h=H)
                            ).then_inc(gcum_ready, 1)
            with dve.Fori(N_LX // 2, CONVS // 2) as i:
                for s in range(2):
                    conv(i * 2 + s, row(dn_w, i * 2 + (s - N_LX)), s, True)
            dve.wait_ge(prod_used, PR_BB)
            with dve.Fori(0, KC // 2) as i:
                for s in range(2):
                    n = i * 2 + s
                    dve.wait_ge(prod_ready, n + (PR_BB + 1))
                    gb = row(gb_t, n).rearrange("p (b n) -> p b n", b=2)
                    dve.tensor_tensor(gb, both(2 * s), gb, ALU.mult).then_inc(prod_used, 1)

            dve.wait_ge(gam_ready, 1)

            def over(col, L, n):
                return col.unsqueeze(2).broadcast_to([L, HG, n])

            def each(m, L):
                return m.unsqueeze(1).broadcast_to([L, HG, L])

            def delta(t, first):
                L = rows(t)
                NL = (L - 1).bit_length()
                cols = ds(t * P, L)
                G, B, GC = (m[:, ds(t, 1), :].rearrange("p o h -> p (o h)") for m in (gcum, beta, gam_col))
                S = state[L == P]
                eye = each(ident[0:L, 0:L], L)
                if not first:
                    dve.wait_ge(d_og, nth(t - 1, 1))
                for g, hs in GROUPS:
                    dve.tensor_tensor(dgam[0:L, hs, 0:L], eye, over(G[0:L, hs], L, L), ALU.mult)
                    dve.tensor_tensor(dbet[0:L, hs, 0:L], eye, over(B[0:L, hs], L, L), ALU.mult
                                      ).then_inc(d_diag, 1)
                for g, hs in GROUPS:
                    dve.wait_ge(d_bc, nth(t, g))
                    dve.tensor_tensor(dec[0:L, hs, 0:L], heads(0, L)[:, hs, 0:L], over(G[0:L, hs], L, L),
                                      ALU.subtract).then_inc(d_diff, 1)
                for g, hs in GROUPS:
                    dve.wait_ge(d_root, nth(t, g))
                    dve.reciprocal(ct[:, hs, 0:L], ct[:, hs, 0:L])
                    dve.reciprocal(pmat[:, hs, 0:L], pmat[:, hs, 0:L]).then_inc(d_rcp, 1)
                for g, hs in GROUPS:
                    dve.wait_ge(d_diff, nth(t, g))
                    dve.tensor_scalar(dec[0:L, hs, 0:L], dec[0:L, hs, 0:L], 0.0, None, ALU.min).then_inc(d_min, 1)
                for g, hs in GROUPS:
                    dve.wait_ge(d_rcp, nth(t, g))
                    dve.scalar_tensor_tensor(out=qn[:, hs, 0:L], in0=part(qkv_t, g, cols),
                                             scalar=float(P) ** -0.5, in1=ct[:, hs, 0:L], op0=ALU.mult, op1=ALU.mult)
                    dve.tensor_tensor(kn[:, hs, 0:L], part(qkv_t, 2 + g, cols), pmat[:, hs, 0:L], ALU.mult
                                      ).then_inc(d_norm, 1)
                for g, hs in GROUPS:
                    dve.wait_ge(d_exp, nth(t, g))
                    dve.tensor_tensor(dec[0:L, hs, 0:L], dec[0:L, hs, 0:L], each(upper[0:L, 0:L], L), ALU.mult
                                      ).then_inc(d_mask, 1)
                for g, hs in GROUPS:
                    dve.wait_ge(d_mask, nth(t, g))
                    dve.tensor_tensor(nmat[0:L, hs, 0:L], heads(2, L)[:, hs, 0:L], dec[0:L, hs, 0:L], ALU.mult
                                      ).then_inc(d_dec, 1)
                for g, hs in GROUPS:
                    dve.wait_ge(d_tr, nth(t, g))
                    dve.tensor_tensor(kend[0:L, hs, :], heads(4, L)[:, hs, :],
                                      dec[0:L, hs, L - 1:L].broadcast_to([L, HG, P]), ALU.mult).then_inc(d_kend, 1)
                for g, hs in GROUPS:
                    dve.wait_ge(d_kk, nth(t, g))
                    dve.wait_ge(d_dec, nth(t, g))
                    dve.tensor_tensor(nmat[0:L, hs, 0:L], heads(0, L)[:, hs, 0:L], nmat[0:L, hs, 0:L], ALU.mult
                                      ).then_inc(d_nm, 1)
                for lv in range(NL):
                    for g, hs in GROUPS:
                        if lv:
                            dve.wait_ge(d_p, nth_level(t, lv - 1, g))
                            dve.wait_ge(d_t, nth_level(t, lv - 1, g))
                        else:
                            dve.wait_ge(d_nm, nth(t, g))
                        dve.tensor_tensor(ct[0:L, hs, 0:L], nmat[0:L, hs, 0:L], each(lvl[0:L, lv, 0:L], L), ALU.mult
                                          ).then_inc(d_ct, 1)
                    for g, hs in GROUPS:
                        if lv == 0:
                            dve.tensor_tensor(qk[0:L, hs, 0:L], heads(2, L)[:, hs, 0:L], dec[0:L, hs, 0:L], ALU.mult)
                            dve.tensor_tensor(qn[:, hs, 0:L], qn[:, hs, 0:L], gam[:, hs, 0:L], ALU.mult
                                              ).then_inc(d_qg, 1)
                            dve.wait_ge(d_ct, nth_level(t, 0, g))
                            dve.tensor_tensor(tinvt[0:L, hs, 0:L], eye, ct[0:L, hs, 0:L], ALU.subtract)
                            dve.wait_ge(d_p, nth_level(t, 0, g))
                            dve.tensor_tensor(tinv[0:L, hs, 0:L], eye, heads(0, L)[:, hs, 0:L], ALU.subtract
                                              ).then_inc(d_t, 1)
                            continue
                        dve.wait_ge(d_xy, nth_inner(t, lv, g))
                        if lv < NL - 1:
                            dve.tensor_tensor(tinv[0:L, hs, 0:L], tinv[0:L, hs, 0:L], heads(4, L)[:, hs, 0:L],
                                              ALU.subtract)
                        dve.tensor_tensor(tinvt[0:L, hs, 0:L], tinvt[0:L, hs, 0:L], heads(6, L)[:, hs, 0:L],
                                          ALU.subtract).then_inc(d_t, 1)
                for g, hs in GROUPS:
                    dve.wait_ge(d_ks, nth(t, g))
                    dve.wait_ge(d_vtok, nth(t, g))
                    dve.tensor_tensor(rmat[0:L, hs, :], heads(0, L)[:, hs, :], over(GC[0:L, hs], L, P), ALU.mult
                                      ).then_inc(d_r1, 1)
                for g, hs in GROUPS:
                    dve.wait_ge(d_r1, nth(t, g))
                    dve.tensor_tensor(rmat[0:L, hs, :], vtok[0:L, hs, :], rmat[0:L, hs, :], ALU.subtract
                                      ).then_inc(d_r2, 1)
                for g, hs in GROUPS:
                    dve.wait_ge(d_r2, nth(t, g))
                    dve.tensor_tensor(rmat[0:L, hs, :], rmat[0:L, hs, :], over(B[0:L, hs], L, P), ALU.mult
                                      ).then_inc(d_r, 1)
                for g, hs in GROUPS:
                    dve.wait_ge(d_os, nth(t, g))
                    dve.tensor_tensor(S[:, hs, :], S[:, hs, :], gam[:, hs, L - 1:L].broadcast_to([P, HG, P]),
                                      ALU.mult).then_inc(d_s1, 1)
                for g, hs in GROUPS:
                    dve.wait_ge(d_s1, nth(t, g))
                    dve.tensor_tensor(S[:, hs, :], S[:, hs, :], heads(6, P)[:, hs, :], ALU.add).then_inc(d_s, 1)
                for g, hs in GROUPS:
                    dve.wait_ge(d_or, nth(t, g))
                    dve.reciprocal(o_sq[:, hs, 0:L], o_sq[:, hs, 0:L]).then_inc(d_o1, 1)
                for g, hs in GROUPS:
                    dve.wait_ge(d_o1, nth(t, g))
                    dve.scalar_tensor_tensor(out=o_sb[:, hs, 0:L], in0=o_sb[:, hs, 0:L], scalar=dn_g[:, 0:1],
                                             in1=o_sq[:, hs, 0:L], op0=ALU.mult, op1=ALU.mult).then_inc(d_o2, 1)
                for g, hs in GROUPS:
                    dve.wait_ge(d_o2, nth(t, g))
                    dve.tensor_tensor(part(z_t, g, cols), o_sb[:, hs, 0:L], part(z_t, g, cols), ALU.mult
                                      ).then_inc(d_og, 1)

            delta(0, True)
            with dve.Fori(1, NTILE) as t:
                delta(t, False)
            delta(NTILE, False)
            with dve.Fori(0, KC // 2) as i:
                for s in range(2):
                    n = i * 2 + s
                    dve.wait_ge(prod_ready, n + (PR_BA + 1))
                    ga = row(ga_t, n).rearrange("p (b n) -> p b n", b=2)
                    dve.tensor_tensor(ga, both(2 * s), ga, ALU.mult).then_inc(prod_used, 1)
                    dve.wait_ge(prod_used, n + (PR_BA + 1))
                    dve.tensor_tensor(row(n_t, n), row(ga_t, n), row(gb_t, n), ALU.add).then_inc(mix_ready, 1)
            dve.wait_ge(late_w, uses(3))
            dve.wait_ge(late_p, uses(3))
            for t in range(NTILE + 1):
                n = rows(t)
                dve.wait_ge(out_mm, t + 1)
                dve.tensor_tensor(x2[0:n, t, :], ps[0:n, 4:6, :].rearrange("p b n -> p (b n)"), x2[0:n, t, :],
                                  ALU.add).then_inc(x2_ready, 1)
                dve.wait_ge(n2_root, t + 1)
                dve.reciprocal(rs2[0:n, t:t + 1], ssum[0:n, 1:2]).then_inc(n2_rcp, 1)
                dve.wait_ge(n2_rcp, t + 1)
                if t:
                    dve.wait_ge(n2_tr, t)
                dve.scalar_tensor_tensor(out=n2[0:n, :], in0=x2[0:n, t, :], scalar=rs2[0:n, t:t + 1],
                                         in1=g2[0:n, :], op0=ALU.mult, op1=ALU.mult).then_inc(n2_ready, 1)

            dve.wait_ge(n2_tr, NTILE + 1)
            dve.wait_ge(prod_ready, PR_END)
            dve.sem_inc(slot_free, SLOTS)
            dve.memset(qsp[:, :, :], 0.0).then_inc(qsp_zero, 1)

            def top16(src, n, vals, inds, L, link):
                for half in range(2):
                    to = slice(8 * half, 8 * half + 8)
                    for j in range(n):
                        ins = dve.max(out=vals[0:L, j, to], in_=src[0:L, j, :])
                    link(ins)
                    for j in range(n):
                        ins = dve.max_index(out=inds[0:L, j, to], in_max=vals[0:L, j, to], in_values=src[0:L, j, :])
                    if half:
                        break
                    for j in range(n):
                        ins = dve.match_replace(out=src[0:L, j, :], in_to_replace=vals[0:L, j, to],
                                                in_values=src[0:L, j, :], imm_value=NEG)
                    link(ins)
                link(ins)

            PICKS = 19

            def pick_halves(n):
                L = P
                link, made = chain(dve, pick_step, n * PICKS, constant=n_ready)
                wait_apart(dve, sch_ready, n + 1, n_ready)
                top16(sch, 2, v16, i16, L, link)
                dve.tensor_copy(i16f[0:L, :, :], i16[0:L, :, :])
                link(dve.tensor_tensor(cand[0:L, 0, :].rearrange("p (a b) -> p a b", a=TOPK),
                                       v16[0:L, 0, :].unsqueeze(2).broadcast_to([L, TOPK, TOPK]),
                                       v16[0:L, 1, :].unsqueeze(1).broadcast_to([L, TOPK, TOPK]), ALU.add))
                return made[0]

            def pick_experts(n, done):
                L = P
                link, made = chain(dve, pick_step, n * PICKS + done, constant=n_ready)
                top16(cand, 1, top, pos, L, link)
                dve.tensor_scalar(gexp[0:L, :], top[0:L, 0, :], top[0:L, 0, 0:1], None, ALU.subtract
                                  ).then_inc(shift_ready, 1)
                dve.tensor_scalar(posu[0:L, 0, :], pos[0:L, 0, :], 4, None, ALU.logical_shift_right)
                link(dve.tensor_scalar(posu[0:L, 1, :], pos[0:L, 0, :], 15, None, ALU.bitwise_and))
                link(dve.tensor_copy(posf[0:L, :, :], posu[0:L, :, :]))
                for p in range(2):
                    link(dve.tensor_tensor(hot[0:L, :, :],
                                           posf[0:L, p, :].unsqueeze(2).broadcast_to([L, TOPK, TOPK]),
                                           iota16[0:L, :].unsqueeze(1).broadcast_to([L, TOPK, TOPK]), ALU.is_equal))
                    link(dve.tensor_tensor(hot[0:L, :, :], hot[0:L, :, :],
                                           i16f[0:L, p, :].unsqueeze(1).broadcast_to([L, TOPK, TOPK]), ALU.mult))
                    link(dve.tensor_reduce(e12[0:L, p, :], hot[0:L, :, :], AX_X, ALU.add))
                dve.scalar_tensor_tensor(out=idx[:, ds(n * TOPK, TOPK)], in0=e12[0:L, 0, :],
                                         scalar=float(NKEYS), in1=e12[0:L, 1, :], op0=ALU.mult, op1=ALU.add
                                         ).then_inc(idx_ready, 1)
                dve.wait_ge(gate_exp, n + 1)
                link(dve.tensor_reduce(gsum[0:L, 0:1], gexp[0:L, :], AX_X, ALU.add))
                link(dve.reciprocal(gsum[0:L, 1:2], gsum[0:L, 0:1]))
                dve.tensor_scalar(gate[:, ds(n * TOPK, TOPK)], gexp[0:L, :], gsum[0:L, 1:2], None,
                                  ALU.mult).then_inc(gate_ready, 1)
                dve.wait_ge(gate_ready, n + 1)
                assert done + made[0] == PICKS, made

            def dot_pair(n, u, norm):
                for j in range(2):
                    k = 2 * u + j
                    s = k % SLOTS
                    dve.wait_ge(row_in[s], uses(n * 2 + (k // SLOTS + 1)))
                    ins = dve.tensor_tensor_reduce(ring[s][:, 0:D], ring[s][:, 0:D], norm, 1.0, 0.0,
                                                   ALU.mult, ALU.add, dots[u % 4][:, j:j + 1])
                ins.then_inc(dot_ready, 1)

            def diag_pair(n, u, gates, eye, L):
                dve.wait_ge(gelu_ready, n * NPAIR + (u + 1))
                for j in range(2):
                    k = 2 * u + j
                    dve.wait_ge(slot_free, n * TOPK + (k + 1))
                    dve.tensor_scalar(diag[k % 8][:, 0:L], eye, gelu_d[u % 4][:, j:j + 1], gates(k), ALU.mult,
                                      ALU.mult).then_inc(diag_ready, 1)

            def experts(t, norm, steps):
                L = rows(t)
                eye = ident[:, :] if L == P else fold[:, :]
                with dve.Fori(0, steps) as i:
                    n = t * H + i
                    dot_pair(n, 0, norm)
                    for u in range(NPAIR):
                        if u < NPAIR - 1:
                            dot_pair(n, u + 1, norm)
                        diag_pair(n, u, lambda k: gate[:, ds(n * TOPK + k, 1)], eye, L)
                        if steps == H and u == PICK_AT[0]:
                            done = pick_halves(n + LAG)
                        if steps == H and u == PICK_AT[1]:
                            pick_experts(n + LAG, done)

            def norm_of(t):
                L = rows(t)
                if not isinstance(t, int) or t:
                    dve.wait_ge(dot_ready, t * (H * NPAIR))
                else:
                    dve.wait_ge(packed, uses(QUARTERS))
                dve.scalar_tensor_tensor(out=n2[0:L, :], in0=row(x2, t)[0:L, :], scalar=rs2[0:L, ds(t, 1)],
                                         in1=g2[0:L, :], op0=ALU.mult, op1=ALU.mult).then_inc(tile_ready, 1)
                wait_apart(dve, tile_ready, t + 1, n_ready)

            def finish(t):
                L = rows(t)
                dve.wait_ge(fin_root, t + 1)
                dve.reciprocal(ssum[0:L, 2:3], ssum[0:L, 1:2]).then_inc(fin_step, 1)
                dve.wait_ge(fin_step, t + 1)
                if not isinstance(t, int) or t:
                    dve.wait_ge(y_out, uses(t))
                dve.scalar_tensor_tensor(out=ybuf[0:L, :], in0=fin[0:L, :], scalar=ssum[0:L, 2:3],
                                         in1=gf[0:L, :], op0=ALU.mult, op1=ALU.mult).then_inc(y_ready, 1)

            def tile(t):
                norm_of(t)
                experts(t, n2, H)

            for n in range(LAG):
                pick_experts(n, pick_halves(n))
            tile(0)
            with dve.Fori(1, NTILE - 1) as t:
                tile(t)
                finish(t - 1)
            tile(NTILE - 1)
            finish(NTILE - 2)
            finish(NTILE - 1)
            experts(NTILE, n2p, SPREAD)
            finish(NTILE)


def _chunks(w):
    k, n = w.shape
    return np.ascontiguousarray(w.reshape(k // P, P, n // P, P).transpose(2, 1, 0, 3))


def _features(v):
    v = v.reshape(*v.shape[:-1], v.shape[-1] // P, P)
    return np.ascontiguousarray(np.moveaxis(np.moveaxis(v, -1, 0), -1, 1))


def _constants():
    i = np.arange(P)
    upper = (i[None, :] >= i[:, None]).astype(np.float32)
    lvl = np.zeros((P, LEVELS, P), np.float32)
    for lv in range(LEVELS):
        s = 1 << lv
        same = (i[:, None] // (2 * s)) == (i[None, :] // (2 * s))
        lvl[:, lv, :] = same & ((i[:, None] // s) % 2 == 0) & ((i[None, :] // s) % 2 == 1)
    return {
        "ident": np.eye(P, dtype=np.float32), "ones": np.ones((P, P), np.float32), "upper": upper, "lvl": lvl,
        "fold": (i[:, None] % TS == np.arange(TS)[None, :]).astype(np.float32),
        "iota16": np.broadcast_to(np.arange(TOPK, dtype=np.float32), (P, TOPK)).copy(),
    }


_OUTS = {"y": (NT, D), "tails": (P, 4 * KC, 2 * HIST), "lru_last": (P, KC, 2), "dn_p": (P, H, P),
         "dn_s": (P, H, P)}


def kernel(**inputs):
    import concourse.bacc as bacc
    from concourse.bass_utils import run_bass_kernel_spmd

    v = {k: np.asarray(x) for k, x in inputs.items()}
    w_in = v["w_in"][0]
    at = np.cumsum([0, 3 * D, D, D, D, D, D])
    part = [w_in[:, at[n]:at[n + 1]] for n in range(6)]
    qkv, z, lx, ly, ga, gb = part
    arrays = _constants()
    arrays["x_t"] = _features(np.concatenate([v["x_prompt"][0], v["x_sample"][0]], 0))
    arrays["x_prompt"], arrays["x_sample"] = v["x_prompt"][0], v["x_sample"][0]
    arrays["stream"] = np.concatenate([_chunks(w) for w in (
        lx, ly, z, ga, gb, qkv, v["w_branch_b"][0], v["w_branch_a"][0], v["peer_w_q"][0])], 0)
    arrays["w_ba"] = np.ascontiguousarray(w_in[:, at[6]:].reshape(KC, P, 2 * H).transpose(1, 0, 2))
    arrays["w_out"] = np.ascontiguousarray(v["w_out"][0].reshape(KC, P, D).transpose(1, 0, 2))
    arrays["ln1_g"] = _features(v["ln1_g"][0])
    arrays["dn_conv_w"] = _features(v["dn_conv_w"][0])
    arrays["lru_conv_w"] = _features(v["lru_conv_w"][0])
    arrays["lru_conv_b"] = _features(v["lru_conv_b"][0])
    arrays["lru_b_r"] = np.ascontiguousarray(v["lru_b_r"][0].T)
    arrays["lru_b_i"] = np.ascontiguousarray(v["lru_b_i"][0].T)
    arrays["lru_lambda"] = _features(v["lru_lambda"][0])
    arrays["state_lru_h"] = _features(v["state_lru_h"][0, 0])
    arrays["state_dn_conv"] = _features(v["state_dn_conv"][0, 0])
    arrays["state_lru_conv"] = _features(v["state_lru_conv"][0, 0])
    arrays["dn_norm_g"] = v["dn_norm_g"][0].reshape(P, 1)
    arrays["dn_a_log"], arrays["dn_dt_bias"] = v["dn_a_log"], v["dn_dt_bias"]
    arrays["lru_w_r"] = np.ascontiguousarray(v["lru_w_r"][0].transpose(1, 0, 2))
    arrays["lru_w_i"] = np.ascontiguousarray(v["lru_w_i"][0].transpose(1, 0, 2))
    arrays["state_dn"] = np.ascontiguousarray(v["state_dn"][0, 0].transpose(1, 0, 2))
    arrays["ln2_g"], arrays["final_g"] = v["ln2_g"], v["final_g"].reshape(1, D)
    arrays["keys"] = np.ascontiguousarray(v["peer_keys"][0].transpose(1, 3, 0, 2).reshape(P, H, NKEYS))
    arrays["uv"] = np.concatenate([v["peer_u"][0], v["peer_v"][0]], 1)

    nc = bacc.Bacc("TRN2", target_bir_lowering=False, num_devices=1)
    arrays = {k: np.ascontiguousarray(x) for k, x in arrays.items()}
    a = {k: nc.dram_tensor(f"in_{k}", x.shape, mybir.dt.from_np(x.dtype), kind="ExternalInput").ap()
         for k, x in arrays.items()}
    o = {k: nc.dram_tensor(f"out_{k}", s, F32, kind="ExternalOutput").ap() for k, s in _OUTS.items()}
    trunk_program(nc, a, o)
    r = run_bass_kernel_spmd(nc, [{f"in_{k}": x for k, x in arrays.items()}], core_ids=[0]).results[0]
    y, tails, last = r["out_y"], r["out_tails"], r["out_lru_last"]

    def rows(x):
        return np.ascontiguousarray(x.transpose(2, 1, 0)).reshape(x.shape[2], -1)

    def conv_state(first, c0, c1):
        return rows(tails[:, c0:c1, first:first + HIST])[None, None]

    def lru_h(n):
        return rows(last[:, :, n:n + 1])[None]

    return (y[None, :TP], y[None, TP:],
            r["out_dn_p"].transpose(1, 0, 2)[None, None], conv_state(0, KC, 4 * KC), lru_h(0), conv_state(0, 0, KC),
            r["out_dn_s"].transpose(1, 0, 2)[None, None], conv_state(HIST, KC, 4 * KC), lru_h(1),
            conv_state(HIST, 0, KC))
```

```python
from contextlib import ExitStack

import concourse.bass as bass
import numpy as np
from concourse import mybir

F32 = mybir.dt.float32
F32R = mybir.dt.float32r
I32 = mybir.dt.int32
U32 = mybir.dt.uint32
ALU = mybir.AluOpType
ACT = mybir.ActivationFunctionType
AX_X = mybir.AxisListType.X
ds = bass.ds

P = 128
D = 1024
KC = D // P
TP, TS = 512, 32
NT = TP + TS
HALF = NT // 2
NTILE = TP // P
H = 8
CW = 4
HIST = CW - 1
PADW = HIST + TP + HIST + TS
SMP0 = HIST + TP + HIST
CONVW = PADW - HIST
YS0 = TP + HIST
EPS = 1e-6
LRU_C = 8.0
NKEYS = 128
TOPK = 16
LEVELS = 7
RING = 4
SLOTS = 8
NEG = -3.0e38

GROUP_CHUNKS = {"lx": KC, "ly": KC, "ga": KC, "gb": KC, "branch_b": KC, "z": KC, "qkv": 3 * KC, "branch_a": KC,
                "w_q": KC}
N_STREAM = sum(GROUP_CHUNKS.values())


def trunk_program(nc, a, o):
    ctx = ExitStack()
    with ctx:
        def sb(name, shape, dt=F32):
            return ctx.enter_context(nc.sbuf_tensor(name, shape, dt))

        def sem(name):
            return ctx.enter_context(nc.semaphore(name))

        ident = sb("ident", [P, P])
        ones = sb("ones", [P, P])
        upper = sb("upper", [P, P])
        lvl = sb("lvl", [P, LEVELS, P])
        fold = sb("fold", [P, TS])
        iota16 = sb("iota16", [P, TOPK])
        ln1 = sb("ln1", [P, KC])
        dn_w = sb("dn_w", [P, 3 * KC, CW])
        lru_w = sb("lru_w", [P, KC, CW])
        lru_b = sb("lru_b", [P, KC])
        b_r = sb("b_r", [P, KC])
        b_i = sb("b_i", [P, KC])
        lam = sb("lam", [P, KC])
        h0 = sb("h0", [P, KC])
        dn_hist = sb("dn_hist", [P, 3 * KC, HIST])
        lru_hist = sb("lru_hist", [P, KC, HIST])
        alog = sb("alog", [P, H])
        dtb = sb("dtb", [P, H])
        dn_g = sb("dn_g", [P, 1])
        w_ba = sb("w_ba", [P, KC, 2 * H])
        cn = sb("cn", [P, KC])
        tails = sb("tails", [P, 4 * KC, 2 * HIST])
        lru_last = sb("lru_last", [P, KC, 2])
        spx = sb("spx", [P, KC + (NTILE + 1) * H])
        spl = sb("spl", [P, KC + (NTILE + 1) * H])
        glog = sb("glog", [P, (NTILE + 1) * H])
        rs2 = sb("rs2", [P, NTILE + 1])
        bg = sb("bg", [P, NTILE + 1, 2 * H])
        beta = sb("beta", [P, NTILE + 1, H])
        gcum = sb("gcum", [P, NTILE + 1, H])
        gam_col = sb("gam_col", [P, NTILE + 1, H])
        eps_col = sb("eps_col", [P, 1])

        def rounded(name, at, *dims):
            with ExitStack() as before:
                if at:
                    before.enter_context(nc.sbuf_tensor(f"before_{name}", [P, at], F32))
                return before.enter_context(nc.sbuf_tensor(name, [P, *dims], F32R))

        W = KC * NT
        TAIL = 9 * W
        WHI = TAIL + RING * KC * P
        n_lo, n_hi = rounded("n_lo", 0, KC, NT), rounded("n_hi", W, KC, NT)
        b_hi, b_lo = rounded("b_hi", 4 * W, KC, NT), rounded("b_lo", 6 * W, KC, NT)
        a_hi, a_lo = rounded("a_hi", 5 * W, KC, NT), rounded("a_lo", 4 * W, KC, NT)
        n2_hi, n2_lo = rounded("n2_hi", 4 * W, KC, NT), rounded("n2_lo", 5 * W, KC, NT)
        w_lo = [rounded(f"w_lo{s}", TAIL + s * KC * P, KC, P) for s in range(RING)]
        w_hi = [rounded(f"w_hi{s}", WHI + s * KC * P, KC, P) for s in range(2)]
        arena = sb("arena", [P, 47520])

        def view(at, *dims):
            n = int(np.prod(dims))
            v = arena[:, at:at + n]
            if len(dims) == 1:
                return v
            if len(dims) == 2:
                return v.rearrange("p (a b) -> p a b", b=dims[1])
            return v.rearrange("p (a b c) -> p a b c", b=dims[1], c=dims[2])

        x_t = view(0, KC, NT)
        ga_t = view(2 * W, KC, NT)
        gb_t = view(3 * W, KC, NT)
        ob_t = view(4 * W, KC, NT)
        n_t = ob_t
        z_t = ob_t
        qkv_t = view(5 * W, 3 * KC, NT)
        lru_a = view(5 * W, KC, NT)
        lru_i = view(6 * W, KC, NT)
        lru_th = view(7 * W, KC, NT)
        gelu_y = view(8 * W, KC, NT)
        wring = [view(TAIL + s * KC * P, KC, P) for s in range(RING)]
        o1 = WHI + 2 * KC * P
        xpad = [view(o1 + s * 552, 552) for s in range(2)]
        ycv = [view(o1 + 1104 + s * 552, 552) for s in range(2)]
        lru_v = [ycv[s][:, 0:NT] for s in range(2)]
        assert o1 + 2208 <= 47520
        rstd1 = ycv[0][:, 0:NT]
        x2_sq = view(5 * D, D)
        sq_x = qkv_t
        homes = iter([k * 1024 for k in range(7)] + [8 * W + k * 1024 for k in range(4)]
                     + [WHI, WHI + 1024, o1, o1 + 1024])

        def head_buf():
            return view(next(homes), H, P)

        dgam, dbet = head_buf(), head_buf()
        kn, qn = head_buf(), head_buf()
        vn, dec = head_buf(), head_buf()
        gam, nmat = head_buf(), head_buf()
        ct, tinv, tinvt = head_buf(), head_buf(), head_buf()
        pmat, qk = head_buf(), head_buf()
        kend, vtok = head_buf(), head_buf()
        sq_q, sq_k = tinv, tinvt
        dq, dk = ct, pmat
        rmat, umat = ct, pmat
        rqk = sb("rqk", [P, 2, H])
        ro = sb("ro", [P, H])
        o_sb, o_sq = dgam, dbet
        state = {True: view(7 * 1024, H, P), False: sb("state_s", [P, H, P])}
        wr_v = view(3 * W, KC, P)
        wi_v = view(3 * W + KC * P, KC, P)

        x2 = view(0, NTILE + 1, D)
        mix_t = view(6 * W, KC, NT)
        w_out = view(7 * W, KC, D)
        assert 7 * W + KC * D <= TAIL
        q_t = ga_t
        g2 = view(3 * W, D)
        gf = view(3 * W + D, D)
        keys = view(3 * W + 2 * D, H, NKEYS)
        n2 = view(3 * W + 3 * D, D)
        assert 3 * W + 4 * D <= 4 * W
        ring = [view(4 * W + s * 2 * D, 2 * D) for s in range(SLOTS)]
        o2 = 4 * W + SLOTS * 2 * D
        o3 = o2 + 768 + 2 * NT
        ybuf = view(o3, D)
        qs = view(o3 + D, H, P)
        fin = view(o3 + 2 * D, D)
        fin_sq_t = view(o3 + 3 * D, D)
        n2p = view(o3 + 4 * D, D)
        diag = [view(o3 + 5 * D + b * P, P) for b in range(8)]
        assert o3 + 7 * D <= 47520
        sch = view(o2, 2, NKEYS)
        v16 = sb("v16", [P, 2, TOPK])
        i16 = sb("i16", [P, 2, TOPK], U32)
        i16f = sb("i16f", [P, 2, TOPK])
        cand = view(o2 + 256, 1, TOPK * TOPK)
        hot = view(o2 + 512, TOPK, TOPK)
        top = sb("top", [P, 1, TOPK])
        pos = sb("pos", [P, 1, TOPK], U32)
        posu = sb("posu", [P, 2, TOPK], U32)
        posf = sb("posf", [P, 2, TOPK])
        e12 = sb("e12", [P, 2, TOPK])
        gexp = sb("gexp", [P, TOPK])
        gsum = sb("gsum", [P, 2])
        idx = view(o2 + 768, NT).bitcast(I32)
        gate = view(o2 + 768 + NT, NT)
        qsp = view(o3 + 6 * D, H, P)
        idxs = [sb(f"idxs{b}", [P, SLOTS], I32) for b in range(2)]
        dots = [sb(f"dots{b}", [P, 2]) for b in range(4)]
        gelu_d = [sb(f"gelu_d{b}", [P, 2]) for b in range(4)]
        ssum = sb("ssum", [P, 4])

        ps = ctx.enter_context(nc.psum_tensor("ps", [P, 8, 512], F32))

        def both(b):
            return ps[:, b:b + 2, 0:HALF]

        params_in = sem("params_in")
        x_in = [sem(f"x_in{c}") for c in range(KC)]
        ones_ready = sem("ones_ready")
        chunk_in = [sem(f"chunk_in{s}") for s in range(RING)]
        sq_done = sem("sq_done")
        ssq_done = sem("ssq_done")
        root_done = sem("root_done")
        rstd_done = sem("rstd_done")
        n_ready = sem("n_ready")
        n_hi_ready = sem("n_hi_ready")
        n_lo_ready = sem("n_lo_ready")
        hi_ready = sem("hi_ready")
        lo_ready = sem("lo_ready")
        a_hi_ready = sem("a_hi_ready")
        a_lo_ready = sem("a_lo_ready")
        n2_hi_ready = sem("n2_hi_ready")
        ba_done = sem("ba_done")
        prod_ready = sem("prod_ready")
        prod_used = sem("prod_used")
        pad_ready = sem("pad_ready")
        conv_step = sem("conv_step")
        conv_ready = sem("conv_ready")
        conv_used = sem("conv_used")
        lru_sq = sem("lru_sq")
        lru_exp = sem("lru_exp")
        lru_tanh = sem("lru_tanh")
        lru_one = sem("lru_one")
        lru_root = sem("lru_root")
        lru_step = sem("lru_step")
        lru_done = sem("lru_done")
        lru_ob_n = sem("lru_ob_n")
        sp_x = sem("sp_x")
        sp_abs = sem("sp_abs")
        sp_log = sem("sp_log")
        sp_sum = sem("sp_sum")
        g_ready = sem("g_ready")
        bg_zero = sem("bg_zero")
        bg_ready = sem("bg_ready")
        gcum_mm = sem("gcum_mm")
        gcum_ready = sem("gcum_ready")
        gam_ready = sem("gam_ready")
        gam_beta = sem("gam_beta")
        state_zero = sem("state_zero")
        state_in = sem("state_in")

        d_diag = sem("d_diag")
        d_bc = sem("d_bc")
        d_sq = sem("d_sq")
        d_vn = sem("d_vn")
        d_ssq = sem("d_ssq")
        d_root = sem("d_root")
        d_rcp = sem("d_rcp")
        d_rdiag = sem("d_rdiag")
        d_rbc = sem("d_rbc")
        d_norm = sem("d_norm")
        d_diff = sem("d_diff")
        d_min = sem("d_min")
        d_exp = sem("d_exp")
        d_mask = sem("d_mask")
        d_dec = sem("d_dec")
        d_tr = sem("d_tr")
        d_kend = sem("d_kend")
        d_vtok = sem("d_vtok")
        d_kk = sem("d_kk")
        d_nm = sem("d_nm")
        d_qg = sem("d_qg")
        d_ct = sem("d_ct")
        d_p = sem("d_p")
        d_pc = sem("d_pc")
        d_xy = sem("d_xy")
        d_t = sem("d_t")
        d_ks = sem("d_ks")
        d_r1 = sem("d_r1")
        d_r = sem("d_r")
        d_u = sem("d_u")
        d_uc = sem("d_uc")
        d_os = sem("d_os")
        d_s1 = sem("d_s1")
        d_s = sem("d_s")
        d_oss = sem("d_oss")
        d_or = sem("d_or")
        d_orr = sem("d_orr")
        d_on = sem("d_on")
        d_otr = sem("d_otr")
        d_og = sem("d_og")

        late_w = sem("late_w")
        late_p = sem("late_p")
        mix_ready = sem("mix_ready")
        out_mm = sem("out_mm")
        x2_ready = sem("x2_ready")
        n2_sq = sem("n2_sq")
        n2_root = sem("n2_root")
        n2_rcp = sem("n2_rcp")
        n2_ready = sem("n2_ready")
        n2_tr = sem("n2_tr")
        n2_copied = sem("n2_copied")

        qs_first = sem("qs_first")
        sc_first = sem("sc_first")
        qs_ready = sem("qs_ready")
        sc_mm = sem("sc_mm")
        pick_step = sem("pick_step")
        shift_ready = sem("shift_ready")
        gate_exp = sem("gate_exp")
        idx_ready = sem("idx_ready")
        gate_ready = sem("gate_ready")
        tile_ready = sem("tile_ready")
        idxs_ready = sem("idxs_ready")
        slot_free = sem("slot_free")
        row_in = [sem(f"row_in{s}") for s in range(SLOTS)]
        dot_ready = sem("dot_ready")
        gelu_ready = sem("gelu_ready")
        diag_ready = sem("diag_ready")
        sch_ready = sem("sch_ready")
        packed = sem("packed")
        qsp_zero = sem("qsp_zero")
        fin_step = sem("fin_step")
        fin_copy = sem("fin_copy")
        fin_sq = sem("fin_sq")
        fin_root = sem("fin_root")
        y_ready = sem("y_ready")
        y_out = sem("y_out")
        small_out = sem("small_out")

        block = ctx.enter_context(nc.Block())

        PARAMS = [(ident, "ident"), (upper, "upper"), (lvl, "lvl"), (fold, "fold"),
                  (iota16, "iota16"), (ln1, "ln1_g"), (dn_w, "dn_conv_w"), (lru_w, "lru_conv_w"),
                  (lru_b, "lru_conv_b"), (b_r, "lru_b_r"), (b_i, "lru_b_i"), (lam, "lru_lambda"),
                  (h0, "state_lru_h"), (dn_hist, "state_dn_conv"), (lru_hist, "state_lru_conv"),
                  (dn_g, "dn_norm_g"), (w_ba, "w_ba")]
        N_PARAMS = 16 * (len(PARAMS) + 4)

        SHIFT = 2 * KC
        starts = np.cumsum([0] + list(GROUP_CHUNKS.values())).tolist()
        CH_LX, CH_LY, CH_GA, CH_GB, CH_BB, CH_Z, CH_QKV, CH_BA, CH_Q, _ = starts
        PR_GATE = CH_GA
        PR_GA, PR_GB, PR_BB, PR_Z, PR_QKV, PR_BA, PR_Q, PR_END = (c + SHIFT for c in starts[2:])
        N_LX = KC
        CONVS = N_LX + 3 * KC
        NPAIR = TOPK // 2
        PICK_AT = (1, 3, 5)
        LAG = 2
        QUARTERS = P // TS
        SPREAD = H // QUARTERS
        assert SPREAD == LAG

        def rows(t):
            return TS if isinstance(t, int) and t == NTILE else P

        def out_bank(t):
            return 4 * (t % 2)

        def uses(k):
            return k * 16

        def heads(bank, L):
            return ps[0:L, bank:bank + 2, :].rearrange("p b (h i) -> p (b h) i", h=4)

        HG = H // 2
        GROUPS = [(g, slice(g * HG, (g + 1) * HG)) for g in range(2)]

        def nth(t, g):
            return t * 2 + (g + 1)

        def nth_level(t, lv, g):
            return t * (2 * LEVELS) + (2 * lv + g + 1)

        def nth_inner(t, lv, g):
            return t * (2 * (LEVELS - 1)) + (2 * (lv - 1) + g + 1)

        def wait_apart(eng, sem_, value, constant):
            if not isinstance(value, int):
                value = eng.compute_val(value)
            eng.wait_ge(constant, 1)
            eng.wait_ge(sem_, value)

        def chain(eng, sem_, base, constant=None):
            n = [0]

            def link(ins):
                n[0] += 1
                ins.then_inc(sem_, 1)
                if constant is not None:
                    wait_apart(eng, sem_, base + n[0], constant)
                else:
                    eng.wait_ge(sem_, base + n[0])
            return link, n

        def part(m, c, cols):
            return m[:, HG * c:HG * (c + 1), cols]

        @block.sync
        def _(sp):
            for c in range(KC):
                sp.dma_start(x_t[:, c, :], a["x_t"][:, c, :]).then_inc(x_in[c], 16)
            for dst, name in PARAMS:
                sp.dma_start(dst[:], a[name]).then_inc(params_in, 16)
            for dst, name in ((wr_v, "lru_w_r"), (wi_v, "lru_w_i")):
                sp.dma_start(dst, a[name]).then_inc(params_in, 16)
            for dst, name in ((alog, "dn_a_log"), (dtb, "dn_dt_bias")):
                sp.dma_start(dst[:], a[name].broadcast_to([P, H])).then_inc(params_in, 16)
            sp.dma_start(state[False][:], a["state_dn"]).then_inc(state_in, 16)

            for s in range(RING):
                sp.dma_start(wring[s], a["stream"][s]).then_inc(chunk_in[s], 16)
            refills = PR_GATE // RING + 1
            for first, last, shift in ((1, refills, 0), (refills, N_STREAM // RING, SHIFT)):
                with sp.Fori(first, last) as i:
                    for s in range(RING):
                        sp.wait_ge(prod_ready, i * RING + (s - RING + 1 + shift))
                        sp.dma_start(wring[s], a["stream"][ds(i * RING + s, 1)].rearrange(
                            "o p k n -> (o p) k n")).then_inc(chunk_in[s], 16)

            sp.wait_ge(n2_tr, NTILE + 1)
            sp.wait_ge(prod_ready, PR_END)
            for q in range(QUARTERS):
                sp.dma_start(n2p[q * TS:(q + 1) * TS, :], n2[0:TS, :]).then_inc(packed, 16)
            sp.wait_ge(y_out, uses(NTILE + 1))
            sp.wait_ge(small_out, uses(4))

        @block.tensor
        def _(pe):
            def row(m, c):
                return m[:, ds(c, 1), :].rearrange("p o n -> p (o n)")

            def quads(first, last, shift, rhs_hi, rhs_lo):
                def body(i, unheld):
                    for s in range(RING):
                        n = i * RING + s
                        pe.wait_ge(lo_ready, n + 1)
                        if s >= unheld:
                            pe.wait_ge(prod_used, n + (shift - 1))
                        b = 2 * ((s + shift) % 2)
                        for half in range(2):
                            cols = slice(half * HALF, (half + 1) * HALF)
                            for k in range(KC):
                                for w, rhs in ((w_hi[s % 2], rhs_hi), (w_hi[s % 2], rhs_lo), (w_lo[s], rhs_hi)):
                                    mm = pe.matmul(ps[:, b + half, 0:HALF], w[:, k, :], rhs[:, k, cols],
                                                   start=(k == 0 and w is w_hi[s % 2] and rhs is rhs_hi),
                                                   stop=(k == KC - 1 and w is w_lo[s]))
                        mm.then_inc(prod_ready, 1)
                i0 = first // RING
                if first == 0:
                    body(0, 2)
                    i0 = 1
                with pe.Fori(i0, last // RING) as i:
                    body(i, 0)

            pe.wait_ge(ones_ready, 1)
            for c in range(KC):
                pe.wait_ge(sq_done, c + 1)
                for half in range(2):
                    mm = pe.matmul(ps[:, half, 0:HALF], ones[:, :], sq_x[:, c, half * HALF:(half + 1) * HALF],
                                   start=(c == 0), stop=(c == KC - 1))
            mm.then_inc(ssq_done, 1)
            pe.wait_ge(n_ready, KC)
            pe.wait_ge(params_in, N_PARAMS)
            for t in range(NTILE + 1):
                n = rows(t)
                for c in range(KC):
                    mm = pe.matmul(ps[0:n, 4, t * 16:(t + 1) * 16], n_t[:, c, t * P:t * P + n], w_ba[:, c, :],
                                   start=(c == 0), stop=(c == KC - 1))
            mm.then_inc(ba_done, 1)
            pe.wait_ge(n_lo_ready, KC)
            quads(0, CH_GA, 0, n_hi, n_lo)
            for n in range(KC):
                pe.wait_ge(conv_used, n + 1)
                for j, w in enumerate((wr_v, wi_v)):
                    pr = PR_GATE + 2 * n + j
                    pe.wait_ge(prod_used, pr - 1)
                    for half in range(2):
                        mm = pe.matmul(ps[:, 2 * (pr % 2) + half, 0:HALF], w[:, n, :],
                                       ob_t[:, n, half * HALF:(half + 1) * HALF], start=True, stop=True)
                    mm.then_inc(prod_ready, 1)
            pe.wait_ge(g_ready, 1)
            pe.matmul(ps[:, 5, 0:(NTILE + 1) * H], upper[:, :], glog[:, :], start=True, stop=True
                      ).then_inc(gcum_mm, 1)
            quads(CH_GA, CH_BB, SHIFT, n_hi, n_lo)
            pe.wait_ge(lru_ob_n, KC)
            quads(CH_BB, CH_Z, SHIFT, b_hi, b_lo)
            quads(CH_Z, CH_BA, SHIFT, n_hi, n_lo)

            def delta(t, first):
                L = rows(t)
                NL = (L - 1).bit_length()
                S = state[L == P]
                if first:
                    pe.wait_ge(gcum_ready, 1)
                    pe.wait_ge(prod_used, PR_BA)
                else:
                    pe.wait_ge(d_on, nth(t - 1, 1))
                for g, hs in GROUPS:
                    pe.wait_ge(d_sq, nth(t, g))
                    for j, src in enumerate((sq_q, sq_k)):
                        for h in range(HG):
                            c = j * HG + h
                            mm = pe.matmul(ps[0:L, 4 + g, c:c + 1], src[:, hs.start + h, 0:L], ones[:, 0:1],
                                           start=True, stop=True)
                    mm.then_inc(d_ssq, 1)
                if not first:
                    pe.wait_ge(d_og, nth(t - 1, 1))
                for g, hs in GROUPS:
                    pe.wait_ge(d_diag, nth(t, g))
                    for b, src in ((0, dgam), (2, dbet)):
                        mm = pe.matmul(heads(b, P)[:, hs, 0:L], ones[0:L, :], src[0:L, hs, 0:L],
                                       start=True, stop=True)
                    mm.then_inc(d_bc, 1)
                for g, hs in GROUPS:
                    pe.wait_ge(d_rdiag, nth(t, g))
                    for b, src in ((4, dq), (6, dk)):
                        mm = pe.matmul(heads(b, P)[:, hs, 0:L], ones[0:L, :], src[0:L, hs, 0:L],
                                       start=True, stop=True)
                    mm.then_inc(d_rbc, 1)
                for g, hs in GROUPS:
                    pe.wait_ge(d_norm, nth(t, g))
                    pe.wait_ge(d_vn, nth(t, g))
                    for h in range(hs.start, hs.stop):
                        pe.transpose(heads(4, L)[:, h, :], kn[:, h, 0:L], ident[:, :])
                        mm = pe.transpose(heads(6, L)[:, h, :], vn[:, h, 0:L], ident[:, :])
                    mm.then_inc(d_tr, 1)
                for g, hs in GROUPS:
                    pe.wait_ge(d_dec, nth(t, g))
                    for h in range(hs.start, hs.stop):
                        pe.matmul(heads(0, L)[:, h, 0:L], kn[:, h, 0:L], kn[:, h, 0:L], start=True, stop=True)
                        mm = pe.matmul(heads(2, L)[:, h, 0:L], kn[:, h, 0:L], qn[:, h, 0:L], start=True, stop=True)
                    mm.then_inc(d_kk, 1)
                for lv in range(NL):
                    for g, hs in GROUPS:
                        pe.wait_ge(d_ct, nth_level(t, lv, g))
                        if lv:
                            pe.wait_ge(d_t, nth_level(t, lv - 1, g))
                        for h in range(hs.start, hs.stop):
                            mm = pe.matmul(heads(0, L)[:, h, 0:L], ct[0:L, h, 0:L],
                                           tinv[0:L, h, 0:L] if lv else ident[0:L, 0:L], start=True, stop=True)
                        mm.then_inc(d_p, 1)
                    if lv == 0:
                        continue
                    for g, hs in GROUPS:
                        pe.wait_ge(d_pc, nth_inner(t, lv, g))
                        if lv == 1:
                            pe.wait_ge(d_kend, nth(t, g))
                            pe.wait_ge(d_vtok, nth(t, g))
                        for h in range(hs.start, hs.stop):
                            if lv < NL - 1:
                                pe.matmul(heads(4, L)[:, h, 0:L], tinvt[0:L, h, 0:L], pmat[0:L, h, 0:L],
                                          start=True, stop=True)
                            mm = pe.matmul(heads(6, L)[:, h, 0:L], pmat[0:L, h, 0:L], tinvt[0:L, h, 0:L],
                                           start=True, stop=True)
                        mm.then_inc(d_xy, 1)
                if L != P:
                    pe.wait_ge(state_in, 16)
                elif first:
                    pe.wait_ge(state_zero, 1)
                else:
                    pe.wait_ge(d_s, nth(t - 1, 1))
                for g, hs in GROUPS:
                    for h in range(hs.start, hs.stop):
                        mm = pe.matmul(heads(0, L)[:, h, :], kn[:, h, 0:L], S[:, h, :], start=True, stop=True)
                    mm.then_inc(d_ks, 1)
                for g, hs in GROUPS:
                    pe.wait_ge(d_t, nth_level(t, NL - 1, g))
                    pe.wait_ge(d_r, nth(t, g))
                    for h in range(hs.start, hs.stop):
                        mm = pe.matmul(heads(2, L)[:, h, :], tinvt[0:L, h, 0:L], rmat[0:L, h, :],
                                       start=True, stop=True)
                    mm.then_inc(d_u, 1)
                for g, hs in GROUPS:
                    pe.wait_ge(d_uc, nth(t, g))
                    pe.wait_ge(d_qg, nth(t, g))
                    for h in range(hs.start, hs.stop):
                        pe.matmul(heads(4, L)[:, h, :], qn[:, h, 0:L], S[:, h, :], start=True, stop=False)
                        pe.matmul(heads(4, L)[:, h, :], qk[0:L, h, 0:L], umat[0:L, h, :],
                                  start=False, stop=True)
                    for h in range(hs.start, hs.stop):
                        mm = pe.matmul(heads(6, P)[:, h, :], kend[0:L, h, :], umat[0:L, h, :],
                                       start=True, stop=True)
                    mm.then_inc(d_os, 1)
                for g, hs in GROUPS:
                    pe.wait_ge(d_on, nth(t, g))
                    for h in range(hs.start, hs.stop):
                        mm = pe.transpose(heads(0, P)[:, h, 0:L], o_sb[0:L, h, :], ident[0:L, 0:L])
                    mm.then_inc(d_otr, 1)

            delta(0, True)
            with pe.Fori(1, NTILE) as t:
                delta(t, False)
            delta(NTILE, False)
            pe.wait_ge(d_og, nth(NTILE, 1))
            pe.wait_ge(a_lo_ready, NTILE + 1)
            quads(CH_BA, CH_Q, SHIFT, a_hi, a_lo)

            def head_scores(h):
                for p in range(2):
                    mm = pe.matmul(heads(4 + 2 * p, P)[:, h, :], qs[64 * p:64 * p + 64, h, :],
                                   keys[64 * p:64 * p + 64, h, :], start=True, stop=True)
                return mm

            pe.wait_ge(mix_ready, KC)
            pe.wait_ge(late_w, uses(4))
            def project(t):
                n = rows(t)
                if t > 1:
                    pe.wait_ge(x2_ready, t - 1)
                for half in range(2):
                    for k in range(KC):
                        mm = pe.matmul(ps[0:n, out_bank(t) + half, :], mix_t[:, k, t * P:t * P + n],
                                       w_out[:, k, half * 512:(half + 1) * 512], start=(k == 0), stop=(k == KC - 1))
                mm.then_inc(out_mm, 1)

            project(0)
            for t in range(NTILE + 1):
                n = rows(t)
                if t < NTILE:
                    project(t + 1)
                pe.wait_ge(n2_ready, t + 1)
                if t:
                    pe.wait_ge(n2_copied, t)
                for c in range(KC):
                    mm = pe.transpose(heads(6, P)[:, c, 0:n], n2[0:n, c * P:(c + 1) * P], ident[0:n, 0:n])
                mm.then_inc(n2_tr, 1)
            pe.wait_ge(n2_copied, NTILE + 1)
            quads(CH_Q, CH_Q + RING, SHIFT, n2_hi, n2_lo)
            pe.wait_ge(late_p, uses(3))
            pe.wait_ge(qs_first, 1)
            for h in range(LAG):
                mm = head_scores(h)
            mm.then_inc(sc_first, 1)
            quads(CH_Q + RING, N_STREAM, SHIFT, n2_hi, n2_lo)

            def scores(t):
                pe.wait_ge(qs_ready, t + 1)
                first = LAG if isinstance(t, int) and t == 0 else 0
                if not isinstance(t, int) or t:
                    pe.wait_ge(sch_ready, t * H)
                for h in range(first, H if not isinstance(t, int) or t < NTILE else 0):
                    mm = head_scores(h)
                for r in range(SPREAD if isinstance(t, int) and t == NTILE else 0):
                    for p in range(2):
                        for j in range(QUARTERS):
                            h = SPREAD * j + r
                            mm = pe.matmul(heads(4 + 2 * p, P)[:, r, :], qsp[64 * p:64 * p + 64, h, :],
                                           keys[64 * p:64 * p + 64, h, :], start=(j == 0), stop=(j == QUARTERS - 1))
                mm.then_inc(sc_mm, 1)

            def experts(t, steps):
                L = rows(t)
                if not isinstance(t, int) or t:
                    pe.wait_ge(fin_copy, t)
                for half in range(2):
                    pe.matmul(ps[0:L, half, :], ident[0:L, 0:L],
                              row(x2, t)[0:L, half * 512:(half + 1) * 512], start=True, stop=False)

                def step(i, last):
                    for k in range(TOPK):
                        pe.wait_ge(diag_ready, (t * H + i) * TOPK + (k + 1))
                        for half in range(2):
                            mm = pe.matmul(ps[0:L, half, :], diag[k % 8][:, 0:L],
                                           ring[k % SLOTS][:, D + half * 512:D + (half + 1) * 512],
                                           start=False, stop=last and k == TOPK - 1)
                        mm.then_inc(slot_free, 1)
                if steps == H:
                    with pe.Fori(0, H - LAG) as i:
                        step(i, False)
                    scores(t + 1)
                for i in range(steps - LAG, steps):
                    step(i, i == steps - 1)

            scores(0)
            with pe.Fori(0, NTILE - 1) as t:
                experts(t, H)
            experts(NTILE - 1, H)
            experts(NTILE, SPREAD)

        @block.scalar
        def _(act):
            def evac(j, pr, hist, slot, held):
                act.wait_ge(prod_ready, pr + 1)
                if held:
                    act.wait_ge(conv_ready, j - 1)
                b = 2 * slot
                act.copy(tails[:, ds(j, 1), :].rearrange("p o (a n) -> p (o a) n", a=2),
                         ps[:, b + 1, TP - HALF - TS:HALF].rearrange("p (a n) -> p a n", a=2)[:, :, TS - HIST:TS])
                x = xpad[slot]
                act.copy(x[:, HIST:HIST + HALF], ps[:, b, 0:HALF])
                act.copy(x[:, HIST + HALF:HIST + TP], ps[:, b + 1, 0:TP - HALF])
                act.copy(x[:, SMP0:SMP0 + TS], ps[:, b + 1, TP - HALF:HALF]).then_inc(prod_used, 1)
                act.copy(x[:, TP + HIST:SMP0], hist).then_inc(pad_ready, 1)

            def post(j, slot, dst, func, bias=0.0):
                act.wait_ge(conv_ready, j + 1)
                y = ycv[slot]
                act.activation(dst[:, 0:TP], y[:, 0:TP], func, bias=bias)
                act.activation(dst[:, TP:NT], y[:, YS0:YS0 + TS], func, bias=bias).then_inc(conv_used, 1)

            def row(m, c):
                return m[:, ds(c, 1), :].rearrange("p o n -> p (o n)")

            for c in range(KC):
                act.wait_ge(x_in[c], 16)
                act.activation(sq_x[:, c, :], x_t[:, c, :], ACT.Square).then_inc(sq_done, 1)
            act.wait_ge(ssq_done, 1)
            act.wait_ge(bg_zero, 1)
            act.activation(rstd1.rearrange("p (b n) -> p b n", b=2), both(0), ACT.Sqrt, scale=1.0 / D,
                           bias=eps_col[:, 0:1]).then_inc(root_done, 1)

            def split(c, quad=None):
                more, slot = divmod(c, RING)
                act.wait_ge(chunk_in[slot], uses(more + 1) if quad is None else uses(quad + (more + 1)))
                act.copy(w_hi[c % 2][:, :, :], wring[slot]).then_inc(hi_ready, 1)

            for c in range(KC):
                act.wait_ge(n_ready, c + 1)
                act.copy(n_hi[:, c, :], n_t[:, c, :]).then_inc(n_hi_ready, 1)
            split(0)
            split(1)
            act.wait_ge(sp_x, 1)
            act.activation(spl[:, :], spx[:, :], ACT.Abs).then_inc(sp_abs, 1)
            act.wait_ge(sp_abs, 1)
            act.activation(spl[:, :], spl[:, :], ACT.Exp, scale=-1.0).then_inc(sp_abs, 1)
            act.activation(alog[:, :], alog[:, :], ACT.Exp)
            act.wait_ge(sp_abs, 2)
            act.activation(spl[:, :], spl[:, :], ACT.Ln, bias=1.0).then_inc(sp_log, 1)
            act.activation(beta[:, :, :], bg[:, :, 0:H], ACT.Sigmoid).then_inc(sp_log, 1)

            def conv_group(first, last, ch0, pr0, hist, split_last, finish):
                def quad(i, first_quad, splits):
                    for s in range(RING):
                        j = i * RING + s
                        evac(j, j + (pr0 - first), row(hist, j - first), s % 2, first > 0 or not first_quad or s > 1)
                        if s < splits:
                            split(s + 2, i + (ch0 - first) // RING)
                        if s or not first_quad:
                            finish(j - 1, 1 - s % 2)
                quad(first // RING, True, RING)
                if last - first > 2 * RING:
                    with act.Fori(first // RING + 1, last // RING - 1) as i:
                        quad(i, False, RING)
                quad(last // RING - 1, False, split_last)
                finish(last - 1, 1)

            def group(ch0, body):
                pr0 = ch0 + (SHIFT if ch0 >= CH_GA else 0)
                with act.Fori(0, KC // RING) as i:
                    for s in range(RING):
                        act.wait_ge(prod_ready, i * RING + (pr0 + s + 1))
                        body(i * RING + s, s % 2)
                        split(s + 2, i + ch0 // RING)

            def through(dst, func):
                def body(n, slot):
                    act.activation(row(dst, n).rearrange("p (b n) -> p b n", b=2), both(2 * slot), func
                                   ).then_inc(prod_used, 1)
                return body

            conv_group(0, N_LX, CH_LX, CH_LX, lru_hist, RING,
                       lambda j, s: post(j, s, row(ob_t, j), ACT.Identity, bias=lru_b[:, ds(j, 1)]))
            group(CH_LY, through(gelu_y, ACT.Gelu_apprx_tanh))
            for n in range(KC):
                for s, (dst, b) in enumerate(((lru_a, b_r), (lru_i, b_i))):
                    act.wait_ge(prod_ready, n * 2 + (PR_GATE + s + 1))
                    act.activation(row(dst, n).rearrange("p (b n) -> p b n", b=2), both(2 * s), ACT.Sigmoid,
                                   bias=b[:, ds(n, 1)]).then_inc(prod_used, 1)
            act.wait_ge(prod_used, PR_GA)
            act.wait_ge(g_ready, 1)
            for n in range(KC):
                act.activation(row(lru_th, n), row(lru_a, n), ACT.Tanh, scale=cn[:, ds(n, 1)]).then_inc(lru_tanh, 1)
            for n in range(KC):
                act.wait_ge(lru_tanh, n + 1)
                act.activation(row(lru_a, n), row(lru_a, n), ACT.Exp, scale=cn[:, ds(n, 1)]).then_inc(lru_exp, 1)
            group(CH_GA, through(ga_t, ACT.Sigmoid))
            for n in range(KC):
                act.wait_ge(lru_one, n + 1)
                act.activation(row(lru_th, n), row(lru_th, n), ACT.Sqrt, scale=-1.0).then_inc(lru_root, 1)
            group(CH_GB, through(gb_t, ACT.Sigmoid))
            group(CH_BB, lambda n, slot: None)
            act.wait_ge(prod_used, PR_Z)
            group(CH_Z, through(z_t, ACT.Silu))
            act.wait_ge(lru_done, 1)
            conv_group(N_LX, CONVS, CH_QKV, PR_QKV, dn_hist, 2,
                       lambda j, s: post(j, s, row(qkv_t, j - N_LX), ACT.Silu))
            act.wait_ge(gcum_ready, 1)
            act.activation(gam_col[:, :, :], gcum[:, :, :], ACT.Exp).then_inc(gam_ready, 1)

            act.wait_ge(prod_ready, PR_BA)
            act.wait_ge(conv_used, CONVS)

            def delta(t, first):
                L = rows(t)
                NL = (L - 1).bit_length()
                cols = ds(t * P, L)
                if not first:
                    act.wait_ge(d_os, nth(t - 1, 1))
                for g, hs in GROUPS:
                    act.activation(sq_q[:, hs, 0:L], part(qkv_t, g, cols), ACT.Square)
                    act.activation(sq_k[:, hs, 0:L], part(qkv_t, 2 + g, cols), ACT.Square).then_inc(d_sq, 1)
                for g, hs in GROUPS:
                    act.copy(vn[:, hs, 0:L], part(qkv_t, 4 + g, cols)).then_inc(d_vn, 1)
                for g, hs in GROUPS:
                    act.wait_ge(d_ssq, nth(t, g))
                    act.activation(rqk[0:L, g, :], ps[0:L, 4 + g, 0:2 * HG], ACT.Sqrt, bias=eps_col[0:L, 0:1]
                                   ).then_inc(d_root, 1)
                for g, hs in GROUPS:
                    act.wait_ge(d_min, nth(t, g))
                    act.activation(dec[0:L, hs, 0:L], dec[0:L, hs, 0:L], ACT.Exp)
                    act.activation(gam[:, hs, 0:L], heads(0, P)[:, hs, 0:L], ACT.Exp).then_inc(d_exp, 1)
                for g, hs in GROUPS:
                    act.wait_ge(d_tr, nth(t, g))
                    for h in range(hs.start, hs.stop):
                        ins = act.activation(vtok[0:L, h, :], heads(6, L)[:, h, :], ACT.Identity,
                                             scale=row(beta, t)[0:L, h:h + 1])
                    ins.then_inc(d_vtok, 1)
                for lv in range(1, NL):
                    for g, hs in GROUPS:
                        act.wait_ge(d_p, nth_level(t, lv, g))
                        act.copy(pmat[0:L, hs, 0:L], heads(0, L)[:, hs, 0:L]).then_inc(d_pc, 1)
                for g, hs in GROUPS:
                    act.wait_ge(d_u, nth(t, g))
                    act.copy(umat[0:L, hs, :], heads(2, L)[:, hs, :]).then_inc(d_uc, 1)
                for g, hs in GROUPS:
                    act.wait_ge(d_os, nth(t, g))
                    for h in range(hs.start, hs.stop):
                        ins = act.activation(o_sq[0:L, h, :], heads(4, L)[:, h, :], ACT.Square,
                                             accum_out=ro[0:L, h:h + 1])
                    ins.then_inc(d_oss, 1)
                for g, hs in GROUPS:
                    act.wait_ge(d_oss, nth(t, g))
                    act.activation(ro[0:L, hs], ro[0:L, hs], ACT.Sqrt, scale=1.0 / P, bias=eps_col[0:L, 0:1]
                                   ).then_inc(d_or, 1)
                for g, hs in GROUPS:
                    act.wait_ge(d_orr, nth(t, g))
                    for h in range(hs.start, hs.stop):
                        ins = act.activation(o_sb[0:L, h, :], heads(4, L)[:, h, :], ACT.Identity,
                                             scale=ro[0:L, h:h + 1])
                    ins.then_inc(d_on, 1)

            delta(0, True)
            with act.Fori(1, NTILE) as t:
                delta(t, False)
            delta(NTILE, False)

            act.wait_ge(d_os, nth(NTILE, 1))
            split(CH_BA)
            split(CH_BA + 1)
            group(CH_BA, lambda n, slot: None)
            for t in range(NTILE + 1):
                n = rows(t)
                act.wait_ge(x2_ready, t + 1)
                act.activation(x2_sq[0:n, :], x2[0:n, t, :], ACT.Square, accum_out=ssum[0:n, 0:1]
                               ).then_inc(n2_sq, 1)
                act.wait_ge(n2_sq, t + 1)
                act.activation(ssum[0:n, 1:2], ssum[0:n, 0:1], ACT.Sqrt, scale=1.0 / D,
                               bias=eps_col[0:n, 0:1]).then_inc(n2_root, 1)
                act.wait_ge(n2_tr, t + 1)
                act.copy(n2_hi[:, :, t * P:t * P + n], heads(6, P)[:, :, 0:n]).then_inc(n2_hi_ready, 1)
            def pick_scores(t, i, first=False):
                if first:
                    act.wait_ge(sc_first, 1)
                else:
                    act.wait_ge(sc_mm, t + 1)
                if not first or i:
                    act.wait_ge(idx_ready, t * H + i)
                for p in range(2):
                    c = act.copy(sch[:, p, :], flat[:, ds(i * P + (2048 + p * 1024), P)])
                c.then_inc(sch_ready, 1)

            def pick_gates(t, i):
                act.wait_ge(shift_ready, t * H + i + 1)
                act.activation(gexp[:, :], gexp[:, :], ACT.Exp).then_inc(gate_exp, 1)

            flat = ps[:, :, :].rearrange("p b n -> p (b n)")

            for n in range(KC):
                act.wait_ge(prod_ready, PR_Q + n + 1)
                act.copy(row(q_t, n).rearrange("p (b n) -> p b n", b=2), both(2 * (n % 2))).then_inc(prod_used, 1)
                if CH_Q + n + 2 < N_STREAM:
                    split(CH_Q + n + 2)
                if n == LAG - 1:
                    act.wait_ge(prod_used, PR_Q + LAG)
                    act.copy(qs[:, 0:LAG, :], q_t[:, 0:LAG, 0:P]).then_inc(qs_first, 1)
                for i in range(LAG):
                    if n == RING - 1 + 2 * i:
                        pick_scores(0, i, True)
                    if n == RING + 1 + 2 * i:
                        pick_gates(0, i)

            act.wait_ge(prod_used, PR_END)

            def queries(t):
                act.wait_ge(sc_mm, t)
                act.copy(qs[:, :, :], q_t[:, :, ds(t * P, P)]).then_inc(qs_ready, 1)

            def spread_queries():
                act.wait_ge(qsp_zero, 1)
                for j in range(QUARTERS):
                    hs = slice(SPREAD * j, SPREAD * (j + 1))
                    ins = act.copy(qsp[:, hs, j * TS:(j + 1) * TS], q_t[:, hs, TP:NT])
                ins.then_inc(qs_ready, 1)


            def gelus(t, i, pairs):
                for u in pairs:
                    act.wait_ge(dot_ready, (t * H + i) * NPAIR + (u + 1))
                    act.activation(gelu_d[u % 4][:, :], dots[u % 4][:, :], ACT.Gelu).then_inc(gelu_ready, 1)

            def experts(t):
                for first, last, t_pick, shift in ((0, H - LAG, t, LAG), (H - LAG, H, t + 1, LAG - H)):
                    with act.Fori(first, last) as i:
                        pick_scores(t_pick, i + shift)
                        gelus(t, i, range(PICK_AT[1] + 2))
                        pick_gates(t_pick, i + shift)
                        gelus(t, i, range(PICK_AT[1] + 2, NPAIR))

            def store(t):
                act.wait_ge(y_ready, t + 1)
                act.dma_start(o["y"][ds(t * P, rows(t)), :], ybuf[0:rows(t), :]).then_inc(y_out, 16)

            def finish(t):
                L = rows(t)
                act.wait_ge(slot_free, (t + 1) * P + SLOTS if L == P else SLOTS + NTILE * P + TS)
                act.copy(fin[0:L, :], ps[0:L, 0:2, :].rearrange("p b n -> p (b n)")).then_inc(fin_copy, 1)
                act.wait_ge(fin_copy, t + 1)
                act.activation(fin_sq_t[0:L, :], fin[0:L, :], ACT.Square, accum_out=ssum[0:L, 0:1]
                               ).then_inc(fin_sq, 1)
                act.wait_ge(fin_sq, t + 1)
                act.activation(ssum[0:L, 1:2], ssum[0:L, 0:1], ACT.Sqrt, scale=1.0 / D,
                               bias=eps_col[0:L, 0:1]).then_inc(fin_root, 1)

            act.copy(qs[:, LAG:H, :], q_t[:, LAG:H, 0:P]).then_inc(qs_ready, 1)
            queries(1)
            experts(0)
            finish(0)
            with act.Fori(1, NTILE - 1) as t:
                queries(t + 1)
                experts(t)
                store(t - 1)
                finish(t)
            spread_queries()
            experts(NTILE - 1)
            store(NTILE - 2)
            finish(NTILE - 1)
            store(NTILE - 1)
            with act.Fori(0, SPREAD) as i:
                gelus(NTILE, i, range(NPAIR))
            finish(NTILE)
            store(NTILE)

        @block.gpsimd
        def _(pool):
            def lower(first, last):
                with pool.Fori(first // RING, last // RING) as i:
                    for s in range(RING):
                        pool.wait_ge(hi_ready, i * RING + (s + 1))
                        pool.tensor_tensor(w_lo[s][:, :, :], wring[s], w_hi[s % 2][:, :, :].bitcast(F32), ALU.subtract
                                           ).then_inc(lo_ready, 1)

            for c in range(KC):
                pool.wait_ge(n_hi_ready, c + 1)
                pool.tensor_tensor(n_lo[:, c, :], n_t[:, c, :], n_hi[:, c, :].bitcast(F32), ALU.subtract
                                   ).then_inc(n_lo_ready, 1)
            lower(0, CH_Z)
            pool.wait_ge(lru_done, 1)
            pool.dma_start(o["lru_last"], lru_last[:, :, :]).then_inc(small_out, 16)
            lower(CH_Z, CH_BA)
            pool.wait_ge(prod_ready, PR_BA)
            pool.memset(state[True][:, :, :], 0.0).then_inc(state_zero, 1)
            pool.wait_ge(prod_used, PR_BA)
            pool.dma_start(o["tails"], tails[:, :, :]).then_inc(small_out, 16)

            def split_tile(t):
                cols = ds(t * P, rows(t))
                pool.wait_ge(d_og, nth(t, 1))
                pool.tensor_copy(a_hi[:, :, cols], z_t[:, :, cols]).then_inc(a_hi_ready, 1)
                pool.wait_ge(a_hi_ready, t + 1)
                pool.tensor_tensor(a_lo[:, :, cols], z_t[:, :, cols], a_hi[:, :, cols].bitcast(F32), ALU.subtract
                                   ).then_inc(a_lo_ready, 1)

            with pool.Fori(0, NTILE) as t:
                split_tile(t)
            pool.wait_ge(d_s, nth(NTILE - 1, 1))
            pool.dma_start(o["dn_p"], state[True][:, :, :]).then_inc(small_out, 16)
            pool.wait_ge(d_s, nth(NTILE, 1))
            pool.dma_start(o["dn_s"], state[False][:, :, :]).then_inc(small_out, 16)
            split_tile(NTILE)
            pool.dma_start(x2[:, 0:NTILE, :], a["x_prompt"].rearrange("(t p) d -> p t d", p=P)).then_inc(late_w, 16)
            pool.dma_start(x2[0:TS, NTILE, :], a["x_sample"]).then_inc(late_w, 16)
            for c in range(CH_BA, CH_Q, RING):
                lower(c, c + RING)
                ks = slice((c - CH_BA), (c - CH_BA) + RING)
                pool.dma_start(w_out[:, ks, :], a["w_out"][:, ks, :]).then_inc(late_w, 16)
            pool.wait_ge(mix_ready, KC)
            pool.dma_start(g2, a["ln2_g"].broadcast_to([P, D])).then_inc(late_p, 16)
            pool.dma_start(gf, a["final_g"].broadcast_to([P, D])).then_inc(late_p, 16)
            pool.dma_start(keys, a["keys"]).then_inc(late_p, 16)
            lower(CH_Q, N_STREAM)

            def gathers(t, steps):
                with pool.Fori(0, steps) as i:
                    n = t * H + i
                    wait_apart(pool, idx_ready, n + 1, state_zero)
                    for b in range(2):
                        pool.wait_ge(slot_free, n * TOPK + (SLOTS * b + 1))
                        pool.tensor_copy(idxs[b][:, :], idx[:, ds(n * TOPK + SLOTS * b, SLOTS)]
                                         ).then_inc(idxs_ready, 1)
                        wait_apart(pool, idxs_ready, n * 2 + (b + 1), idx_ready)
                        for s in range(SLOTS):
                            wait_apart(pool, slot_free, n * TOPK + (SLOTS * b + s + 1), idx_ready)
                            pool.indirect_dma_start(
                                out=ring[s], out_offset=None, in_=a["uv"],
                                in_offset=bass.IndirectOffsetOnAxis(ap=idxs[b][:, s:s + 1], axis=0),
                            ).then_inc(row_in[s], 16)

            with pool.Fori(0, NTILE) as t:
                gathers(t, H)
            gathers(NTILE, SPREAD)

        @block.vector
        def _(dve):
            def row(m, c):
                return m[:, ds(c, 1), :].rearrange("p o n -> p (o n)")

            dve.memset(ones[:, :], 1.0).then_inc(ones_ready, 1)
            dve.memset(bg[:, :, :], 0.0)
            for s in range(2):
                dve.memset(xpad[s][:, 0:HIST], 0.0)
            dve.memset(eps_col[:, :], EPS).then_inc(bg_zero, 1)
            dve.wait_ge(root_done, 1)
            dve.wait_ge(params_in, N_PARAMS)
            dve.reciprocal(rstd1, rstd1).then_inc(rstd_done, 1)
            dve.wait_ge(rstd_done, 1)
            for c in range(KC):
                dve.scalar_tensor_tensor(out=n_t[:, c, :], in0=x_t[:, c, :], scalar=ln1[:, c:c + 1], in1=rstd1,
                                         op0=ALU.mult, op1=ALU.mult).then_inc(n_ready, 1)
            dve.wait_ge(ba_done, 1)
            dve.wait_ge(bg_zero, 1)
            dve.tensor_copy(bg[:, 0:NTILE, :], ps[:, 4, 0:NTILE * 16].rearrange("p (t n) -> p t n", t=NTILE))
            dve.tensor_copy(bg[0:TS, NTILE, :], ps[0:TS, 4, NTILE * 16:NTILE * 16 + 16]).then_inc(bg_ready, 1)
            dve.wait_ge(bg_ready, 1)
            dve.tensor_scalar(spx[:, 0:KC], lam[:, :], -1.0, None, ALU.mult)
            dve.tensor_tensor(spx[:, KC:].rearrange("p (t h) -> p t h", h=H), bg[:, :, H:2 * H],
                              dtb[:, :].unsqueeze(1).broadcast_to([P, NTILE + 1, H]), ALU.add).then_inc(sp_x, 1)
            dve.wait_ge(sp_log, 2)
            dve.scalar_tensor_tensor(out=spx[:, :], in0=spx[:, :], scalar=0.0, in1=spl[:, :],
                                     op0=ALU.max, op1=ALU.add).then_inc(sp_sum, 1)
            dve.wait_ge(sp_sum, 1)
            dve.tensor_scalar(cn[:, :], spx[:, 0:KC], -LRU_C, None, ALU.mult)
            dve.scalar_tensor_tensor(out=glog[:, :].rearrange("p (t h) -> p t h", h=H),
                                     in0=spx[:, KC:].rearrange("p (t h) -> p t h", h=H), scalar=-1.0,
                                     in1=alog[:, :].unsqueeze(1).broadcast_to([P, NTILE + 1, H]),
                                     op0=ALU.mult, op1=ALU.mult).then_inc(g_ready, 1)

            def conv(j, w, s, held):
                dve.wait_ge(pad_ready, j + 1)
                if held:
                    dve.wait_ge(conv_used, j - 1)
                x, y = xpad[s], ycv[s]
                ins = dve.tensor_scalar(y[:, 0:CONVW], x[:, 0:CONVW], w[:, 0:1], None, ALU.mult)
                for k in range(1, CW):
                    ins.then_inc(conv_step, 1)
                    dve.wait_ge(conv_step, j * HIST + k)
                    ins = dve.scalar_tensor_tensor(out=y[:, 0:CONVW], in0=x[:, k:k + CONVW], scalar=w[:, k:k + 1],
                                                   in1=y[:, 0:CONVW], op0=ALU.mult, op1=ALU.add)
                ins.then_inc(conv_ready, 1)

            for j in range(2):
                conv(j, lru_w[:, j, :], j, False)
            with dve.Fori(1, N_LX // 2) as i:
                for s in range(2):
                    conv(i * 2 + s, row(lru_w, i * 2 + s), s, True)
            with dve.Fori(0, KC // 2) as i:
                for s in range(2):
                    n = i * 2 + s
                    dve.wait_ge(lru_exp, n + 1)
                    dve.tensor_tensor(lru_v[s], row(lru_a, n), row(lru_a, n), ALU.mult).then_inc(lru_sq, 1)
                    dve.wait_ge(lru_sq, n + 1)
                    dve.scalar_tensor_tensor(out=row(lru_th, n), in0=lru_v[s], scalar=1.0, in1=row(lru_th, n),
                                             op0=ALU.add, op1=ALU.mult).then_inc(lru_one, 1)
            with dve.Fori(0, KC) as n:
                A, I = row(lru_a, n), row(lru_i, n)
                link, made = chain(dve, lru_step, n * 5)
                link(dve.tensor_tensor(I, I, row(ob_t, n), ALU.mult))
                dve.wait_ge(lru_root, n + 1)
                link(dve.tensor_tensor(I, I, row(lru_th, n), ALU.mult))
                dve.tensor_tensor_scan(A[:, 0:TP], A[:, 0:TP], I[:, 0:TP], 0.0, ALU.mult, ALU.add)
                link(dve.tensor_tensor_scan(A[:, TP:NT], A[:, TP:NT], I[:, TP:NT], h0[:, ds(n, 1)],
                                            ALU.mult, ALU.add))
                link(dve.tensor_tensor(I, A, row(gelu_y, n), ALU.mult))
                link(dve.tensor_copy(row(b_hi, n), I))
                dve.tensor_tensor(row(b_lo, n), I, row(b_hi, n).bitcast(F32), ALU.subtract).then_inc(lru_ob_n, 1)
                assert made[0] == 5
            dve.wait_ge(lru_ob_n, KC)
            dve.tensor_copy(lru_last[:, :, 0:1], lru_a[:, :, TP - 1:TP])
            dve.tensor_copy(lru_last[:, :, 1:2], lru_a[:, :, NT - 1:NT]).then_inc(lru_done, 1)
            dve.wait_ge(gcum_mm, 1)
            dve.tensor_copy(gcum[:, :, :], ps[:, 5, 0:(NTILE + 1) * H].rearrange("p (t h) -> p t h", h=H)
                            ).then_inc(gcum_ready, 1)
            dve.wait_ge(prod_used, PR_BB)
            with dve.Fori(0, KC // 2) as i:
                for s in range(2):
                    n = i * 2 + s
                    dve.wait_ge(prod_ready, n + (PR_BB + 1))
                    gb = row(gb_t, n).rearrange("p (b n) -> p b n", b=2)
                    dve.tensor_tensor(gb, both(2 * s), gb, ALU.mult).then_inc(prod_used, 1)
            with dve.Fori(N_LX // 2, CONVS // 2) as i:
                for s in range(2):
                    conv(i * 2 + s, row(dn_w, i * 2 + (s - N_LX)), s, True)

            dve.wait_ge(gam_ready, 1)
            dve.tensor_tensor(gam_col[:, :, :], gam_col[:, :, :], beta[:, :, :], ALU.mult).then_inc(gam_beta, 1)
            dve.wait_ge(gam_beta, 1)

            def over(col, L, n):
                return col.unsqueeze(2).broadcast_to([L, HG, n])

            def each(m, L):
                return m.unsqueeze(1).broadcast_to([L, HG, L])

            def delta(t, first):
                L = rows(t)
                NL = (L - 1).bit_length()
                cols = ds(t * P, L)
                G, B, GC = (m[:, ds(t, 1), :].rearrange("p o h -> p (o h)") for m in (gcum, beta, gam_col))
                S = state[L == P]
                eye = each(ident[0:L, 0:L], L)
                if not first:
                    dve.wait_ge(d_og, nth(t - 1, 1))
                for g, hs in GROUPS:
                    dve.tensor_tensor(dgam[0:L, hs, 0:L], eye, over(G[0:L, hs], L, L), ALU.mult)
                    dve.tensor_tensor(dbet[0:L, hs, 0:L], eye, over(B[0:L, hs], L, L), ALU.mult
                                      ).then_inc(d_diag, 1)
                for g, hs in GROUPS:
                    dve.wait_ge(d_root, nth(t, g))
                    dve.reciprocal(rqk[0:L, g, :], rqk[0:L, g, :]).then_inc(d_rcp, 1)
                for g, hs in GROUPS:
                    dve.wait_ge(d_rcp, nth(t, g))
                    dve.tensor_tensor(dq[0:L, hs, 0:L], eye, over(rqk[0:L, g, 0:HG], L, L), ALU.mult)
                    dve.tensor_tensor(dk[0:L, hs, 0:L], eye, over(rqk[0:L, g, HG:2 * HG], L, L), ALU.mult
                                      ).then_inc(d_rdiag, 1)
                for g, hs in GROUPS:
                    dve.wait_ge(d_bc, nth(t, g))
                    dve.tensor_tensor(dec[0:L, hs, 0:L], heads(0, L)[:, hs, 0:L], over(G[0:L, hs], L, L),
                                      ALU.subtract).then_inc(d_diff, 1)
                for g, hs in GROUPS:
                    dve.wait_ge(d_diff, nth(t, g))
                    dve.tensor_scalar(dec[0:L, hs, 0:L], dec[0:L, hs, 0:L], 0.0, None, ALU.min).then_inc(d_min, 1)
                for g, hs in GROUPS:
                    dve.wait_ge(d_rbc, nth(t, g))
                    dve.scalar_tensor_tensor(out=qn[:, hs, 0:L], in0=part(qkv_t, g, cols), scalar=float(P) ** -0.5,
                                             in1=heads(4, P)[:, hs, 0:L], op0=ALU.mult, op1=ALU.mult)
                    dve.tensor_tensor(kn[:, hs, 0:L], part(qkv_t, 2 + g, cols), heads(6, P)[:, hs, 0:L], ALU.mult
                                      ).then_inc(d_norm, 1)
                for g, hs in GROUPS:
                    dve.wait_ge(d_exp, nth(t, g))
                    dve.tensor_tensor(dec[0:L, hs, 0:L], dec[0:L, hs, 0:L], each(upper[0:L, 0:L], L), ALU.mult
                                      ).then_inc(d_mask, 1)
                for g, hs in GROUPS:
                    dve.wait_ge(d_mask, nth(t, g))
                    dve.tensor_tensor(nmat[0:L, hs, 0:L], heads(2, L)[:, hs, 0:L], dec[0:L, hs, 0:L], ALU.mult
                                      ).then_inc(d_dec, 1)
                for g, hs in GROUPS:
                    dve.wait_ge(d_tr, nth(t, g))
                    dve.tensor_tensor(kend[0:L, hs, :], heads(4, L)[:, hs, :],
                                      dec[0:L, hs, L - 1:L].broadcast_to([L, HG, P]), ALU.mult).then_inc(d_kend, 1)
                for g, hs in GROUPS:
                    dve.wait_ge(d_kk, nth(t, g))
                    dve.wait_ge(d_dec, nth(t, g))
                    dve.tensor_tensor(nmat[0:L, hs, 0:L], heads(0, L)[:, hs, 0:L], nmat[0:L, hs, 0:L], ALU.mult
                                      ).then_inc(d_nm, 1)
                def blocks(lv, g, hs):
                    dve.tensor_tensor(ct[0:L, hs, 0:L], nmat[0:L, hs, 0:L], each(lvl[0:L, lv, 0:L], L), ALU.mult
                                      ).then_inc(d_ct, 1)

                for g, hs in GROUPS:
                    dve.wait_ge(d_nm, nth(t, g))
                    blocks(0, g, hs)
                for lv in range(NL):
                    for g, hs in GROUPS:
                        if 0 < lv < NL - 1:
                            dve.wait_ge(d_p, nth_level(t, lv, g))
                            blocks(lv + 1, g, hs)
                    for g, hs in GROUPS:
                        if lv == 0:
                            dve.tensor_tensor(qk[0:L, hs, 0:L], heads(2, L)[:, hs, 0:L], dec[0:L, hs, 0:L], ALU.mult)
                            dve.tensor_tensor(qn[:, hs, 0:L], qn[:, hs, 0:L], gam[:, hs, 0:L], ALU.mult
                                              ).then_inc(d_qg, 1)
                            dve.wait_ge(d_ct, nth_level(t, 0, g))
                            dve.tensor_tensor(tinvt[0:L, hs, 0:L], eye, ct[0:L, hs, 0:L], ALU.subtract)
                            dve.wait_ge(d_p, nth_level(t, 0, g))
                            dve.tensor_tensor(tinv[0:L, hs, 0:L], eye, heads(0, L)[:, hs, 0:L], ALU.subtract
                                              ).then_inc(d_t, 1)
                            dve.wait_ge(d_t, nth_level(t, 0, g))
                            blocks(1, g, hs)
                            continue
                        dve.wait_ge(d_xy, nth_inner(t, lv, g))
                        if lv < NL - 1:
                            dve.tensor_tensor(tinv[0:L, hs, 0:L], tinv[0:L, hs, 0:L], heads(4, L)[:, hs, 0:L],
                                              ALU.subtract)
                        dve.tensor_tensor(tinvt[0:L, hs, 0:L], tinvt[0:L, hs, 0:L], heads(6, L)[:, hs, 0:L],
                                          ALU.subtract).then_inc(d_t, 1)
                for g, hs in GROUPS:
                    dve.wait_ge(d_ks, nth(t, g))
                    dve.wait_ge(d_vtok, nth(t, g))
                    dve.tensor_tensor(rmat[0:L, hs, :], heads(0, L)[:, hs, :], over(GC[0:L, hs], L, P), ALU.mult
                                      ).then_inc(d_r1, 1)
                for g, hs in GROUPS:
                    dve.wait_ge(d_r1, nth(t, g))
                    dve.tensor_tensor(rmat[0:L, hs, :], vtok[0:L, hs, :], rmat[0:L, hs, :], ALU.subtract
                                      ).then_inc(d_r, 1)
                for g, hs in GROUPS:
                    dve.wait_ge(d_os, nth(t, g))
                    if g == 1:
                        dve.wait_ge(d_or, nth(t, 0))
                        dve.reciprocal(ro[0:L, 0:HG], ro[0:L, 0:HG]).then_inc(d_orr, 1)
                    dve.tensor_tensor(S[:, hs, :], S[:, hs, :], gam[:, hs, L - 1:L].broadcast_to([P, HG, P]),
                                      ALU.mult).then_inc(d_s1, 1)
                for g, hs in GROUPS:
                    dve.wait_ge(d_s1, nth(t, g))
                    dve.tensor_tensor(S[:, hs, :], S[:, hs, :], heads(6, P)[:, hs, :], ALU.add).then_inc(d_s, 1)
                dve.wait_ge(d_or, nth(t, 1))
                dve.reciprocal(ro[0:L, HG:H], ro[0:L, HG:H]).then_inc(d_orr, 1)
                for g, hs in GROUPS:
                    dve.wait_ge(d_otr, nth(t, g))
                    dve.scalar_tensor_tensor(out=part(z_t, g, cols), in0=heads(0, P)[:, hs, 0:L], scalar=dn_g[:, 0:1],
                                             in1=part(z_t, g, cols), op0=ALU.mult, op1=ALU.mult).then_inc(d_og, 1)

            delta(0, True)
            with dve.Fori(1, NTILE) as t:
                delta(t, False)
            delta(NTILE, False)
            dve.wait_ge(prod_used, PR_BA)
            with dve.Fori(0, KC // 2) as i:
                for s in range(2):
                    n = i * 2 + s
                    dve.wait_ge(prod_ready, n + (PR_BA + 1))
                    ga = row(ga_t, n).rearrange("p (b n) -> p b n", b=2)
                    dve.tensor_tensor(ga, both(2 * s), ga, ALU.mult).then_inc(prod_used, 1)
                    dve.wait_ge(prod_used, n + (PR_BA + 1))
                    dve.tensor_tensor(row(mix_t, n), row(ga_t, n), row(gb_t, n), ALU.add).then_inc(mix_ready, 1)
            dve.wait_ge(late_w, uses(4))
            dve.wait_ge(late_p, uses(3))
            for t in range(NTILE + 1):
                n = rows(t)
                dve.wait_ge(out_mm, t + 1)
                dve.tensor_tensor(x2[0:n, t, :], ps[0:n, out_bank(t):out_bank(t) + 2, :].rearrange(
                    "p b n -> p (b n)"), x2[0:n, t, :],
                                  ALU.add).then_inc(x2_ready, 1)
                dve.wait_ge(n2_root, t + 1)
                dve.reciprocal(rs2[0:n, t:t + 1], ssum[0:n, 1:2]).then_inc(n2_rcp, 1)
                dve.wait_ge(n2_rcp, t + 1)
                if t:
                    dve.wait_ge(n2_tr, t)
                dve.scalar_tensor_tensor(out=n2[0:n, :], in0=x2[0:n, t, :], scalar=rs2[0:n, t:t + 1],
                                         in1=g2[0:n, :], op0=ALU.mult, op1=ALU.mult).then_inc(n2_ready, 1)
                dve.wait_ge(n2_hi_ready, t + 1)
                cols = slice(t * P, t * P + n)
                dve.tensor_tensor(n2_lo[:, :, cols], heads(6, P)[:, :, 0:n], n2_hi[:, :, cols].bitcast(F32),
                                  ALU.subtract).then_inc(n2_copied, 1)

            dve.wait_ge(n2_tr, NTILE + 1)

            def top16(src, n, vals, inds, link):
                for half in range(2):
                    to = slice(8 * half, 8 * half + 8)
                    for j in range(n):
                        ins = dve.max(out=vals[:, j, to], in_=src[:, j, :])
                    link(ins)
                    for j in range(n):
                        ins = dve.max_index(out=inds[:, j, to], in_max=vals[:, j, to], in_values=src[:, j, :])
                    if half:
                        break
                    for j in range(n):
                        ins = dve.match_replace(out=src[:, j, :], in_to_replace=vals[:, j, to],
                                                in_values=src[:, j, :], imm_value=NEG)
                    link(ins)
                link(ins)

            PICKS = 19

            def pick_halves(n):
                link, made = chain(dve, pick_step, n * PICKS, constant=n_ready)
                wait_apart(dve, sch_ready, n + 1, n_ready)
                top16(sch, 2, v16, i16, link)
                dve.tensor_copy(i16f[:, :, :], i16[:, :, :])
                link(dve.tensor_tensor(cand[:, 0, :].rearrange("p (a b) -> p a b", a=TOPK),
                                       v16[:, 0, :].unsqueeze(2).broadcast_to([P, TOPK, TOPK]),
                                       v16[:, 1, :].unsqueeze(1).broadcast_to([P, TOPK, TOPK]), ALU.add))
                return made[0]

            def pick_top(n, done):
                link, made = chain(dve, pick_step, n * PICKS + done, constant=n_ready)
                top16(cand, 1, top, pos, link)
                dve.tensor_scalar(gexp[:, :], top[:, 0, :], top[:, 0, 0:1], None, ALU.subtract
                                  ).then_inc(shift_ready, 1)
                return done + made[0]

            def pick_experts(n, done):
                link, made = chain(dve, pick_step, n * PICKS + done, constant=n_ready)
                dve.tensor_scalar(posu[:, 0, :], pos[:, 0, :], 4, None, ALU.logical_shift_right)
                link(dve.tensor_scalar(posu[:, 1, :], pos[:, 0, :], 15, None, ALU.bitwise_and))
                link(dve.tensor_copy(posf[:, :, :], posu[:, :, :]))
                for p in range(2):
                    link(dve.tensor_tensor(hot[:, :, :],
                                           posf[:, p, :].unsqueeze(2).broadcast_to([P, TOPK, TOPK]),
                                           iota16[:, :].unsqueeze(1).broadcast_to([P, TOPK, TOPK]), ALU.is_equal))
                    link(dve.tensor_tensor(hot[:, :, :], hot[:, :, :],
                                           i16f[:, p, :].unsqueeze(1).broadcast_to([P, TOPK, TOPK]), ALU.mult))
                    link(dve.tensor_reduce(e12[:, p, :], hot[:, :, :], AX_X, ALU.add))
                dve.scalar_tensor_tensor(out=idx[:, ds(n * TOPK, TOPK)], in0=e12[:, 0, :],
                                         scalar=float(NKEYS), in1=e12[:, 1, :], op0=ALU.mult, op1=ALU.add
                                         ).then_inc(idx_ready, 1)
                dve.wait_ge(gate_exp, n + 1)
                link(dve.tensor_reduce(gsum[:, 0:1], gexp[:, :], AX_X, ALU.add))
                link(dve.reciprocal(gsum[:, 1:2], gsum[:, 0:1]))
                dve.tensor_scalar(gate[:, ds(n * TOPK, TOPK)], gexp[:, :], gsum[:, 1:2], None,
                                  ALU.mult).then_inc(gate_ready, 1)
                dve.wait_ge(gate_ready, n + 1)
                assert done + made[0] == PICKS, made

            def dot_pair(n, u, norm):
                for j in range(2):
                    k = 2 * u + j
                    s = k % SLOTS
                    dve.wait_ge(row_in[s], uses(n * 2 + (k // SLOTS + 1)))
                    ins = dve.tensor_tensor_reduce(ring[s][:, 0:D], ring[s][:, 0:D], norm, 1.0, 0.0,
                                                   ALU.mult, ALU.add, dots[u % 4][:, j:j + 1])
                ins.then_inc(dot_ready, 1)

            def diag_pair(n, u, gates, eye, L):
                dve.wait_ge(gelu_ready, n * NPAIR + (u + 1))
                for j in range(2):
                    k = 2 * u + j
                    dve.wait_ge(slot_free, n * TOPK + (k + 1))
                    dve.tensor_scalar(diag[k % 8][:, 0:L], eye, gelu_d[u % 4][:, j:j + 1], gates(k), ALU.mult,
                                      ALU.mult).then_inc(diag_ready, 1)

            def experts(t, norm, steps):
                L = rows(t)
                eye = ident[:, :] if L == P else fold[:, :]
                with dve.Fori(0, steps) as i:
                    n = t * H + i
                    dot_pair(n, 0, norm)
                    for u in range(NPAIR):
                        if u < NPAIR - 1:
                            dot_pair(n, u + 1, norm)
                        diag_pair(n, u, lambda k: gate[:, ds(n * TOPK + k, 1)], eye, L)
                        if steps == H and u == PICK_AT[0]:
                            done = pick_halves(n + LAG)
                        if steps == H and u == PICK_AT[1]:
                            done = pick_top(n + LAG, done)
                        if steps == H and u == PICK_AT[2]:
                            pick_experts(n + LAG, done)

            def norm_of(t):
                L = rows(t)
                if not isinstance(t, int) or t:
                    dve.wait_ge(dot_ready, t * (H * NPAIR))
                else:
                    dve.wait_ge(packed, uses(QUARTERS))
                dve.scalar_tensor_tensor(out=n2[0:L, :], in0=row(x2, t)[0:L, :], scalar=rs2[0:L, ds(t, 1)],
                                         in1=g2[0:L, :], op0=ALU.mult, op1=ALU.mult).then_inc(tile_ready, 1)
                wait_apart(dve, tile_ready, t + 1, n_ready)

            def finish(t):
                L = rows(t)
                dve.wait_ge(fin_root, t + 1)
                dve.reciprocal(ssum[0:L, 2:3], ssum[0:L, 1:2]).then_inc(fin_step, 1)
                dve.wait_ge(fin_step, t + 1)
                if not isinstance(t, int) or t:
                    dve.wait_ge(y_out, uses(t))
                dve.scalar_tensor_tensor(out=ybuf[0:L, :], in0=fin[0:L, :], scalar=ssum[0:L, 2:3],
                                         in1=gf[0:L, :], op0=ALU.mult, op1=ALU.mult).then_inc(y_ready, 1)

            def tile(t):
                norm_of(t)
                experts(t, n2, H)

            for n in range(LAG):
                pick_experts(n, pick_top(n, pick_halves(n)))
            dve.wait_ge(prod_ready, PR_END)
            dve.sem_inc(slot_free, SLOTS)
            dve.memset(qsp[:, :, :], 0.0).then_inc(qsp_zero, 1)
            tile(0)
            with dve.Fori(1, NTILE - 1) as t:
                tile(t)
                finish(t - 1)
            tile(NTILE - 1)
            finish(NTILE - 2)
            finish(NTILE - 1)
            experts(NTILE, n2p, SPREAD)
            finish(NTILE)


def _chunks(w):
    k, n = w.shape
    return np.ascontiguousarray(w.reshape(k // P, P, n // P, P).transpose(2, 1, 0, 3))


def _features(v):
    v = v.reshape(*v.shape[:-1], v.shape[-1] // P, P)
    return np.ascontiguousarray(np.moveaxis(np.moveaxis(v, -1, 0), -1, 1))


def _constants():
    i = np.arange(P)
    upper = (i[None, :] >= i[:, None]).astype(np.float32)
    lvl = np.zeros((P, LEVELS, P), np.float32)
    for lv in range(LEVELS):
        s = 1 << lv
        same = (i[:, None] // (2 * s)) == (i[None, :] // (2 * s))
        lvl[:, lv, :] = same & ((i[:, None] // s) % 2 == 0) & ((i[None, :] // s) % 2 == 1)
    return {
        "ident": np.eye(P, dtype=np.float32), "upper": upper, "lvl": lvl,
        "fold": (i[:, None] % TS == np.arange(TS)[None, :]).astype(np.float32),
        "iota16": np.broadcast_to(np.arange(TOPK, dtype=np.float32), (P, TOPK)).copy(),
    }


_OUTS = {"y": (NT, D), "tails": (P, 4 * KC, 2 * HIST), "lru_last": (P, KC, 2), "dn_p": (P, H, P),
         "dn_s": (P, H, P)}


def kernel(**inputs):
    import concourse.bacc as bacc
    from concourse.bass_utils import run_bass_kernel_spmd

    v = {k: np.asarray(x) for k, x in inputs.items()}
    w_in = v["w_in"][0]
    at = np.cumsum([0, 3 * D, D, D, D, D, D])
    part = [w_in[:, at[n]:at[n + 1]] for n in range(6)]
    qkv, z, lx, ly, ga, gb = part
    arrays = _constants()
    arrays["x_t"] = _features(np.concatenate([v["x_prompt"][0], v["x_sample"][0]], 0))
    arrays["x_prompt"], arrays["x_sample"] = v["x_prompt"][0], v["x_sample"][0]
    arrays["stream"] = np.concatenate([_chunks(w) for w in (
        lx, ly, ga, gb, v["w_branch_b"][0], z, qkv, v["w_branch_a"][0], v["peer_w_q"][0])], 0)
    arrays["w_ba"] = np.ascontiguousarray(w_in[:, at[6]:].reshape(KC, P, 2 * H).transpose(1, 0, 2))
    arrays["w_out"] = np.ascontiguousarray(v["w_out"][0].reshape(KC, P, D).transpose(1, 0, 2))
    arrays["ln1_g"] = _features(v["ln1_g"][0])
    arrays["dn_conv_w"] = _features(v["dn_conv_w"][0])
    arrays["lru_conv_w"] = _features(v["lru_conv_w"][0])
    arrays["lru_conv_b"] = _features(v["lru_conv_b"][0])
    arrays["lru_b_r"] = np.ascontiguousarray(v["lru_b_r"][0].T)
    arrays["lru_b_i"] = np.ascontiguousarray(v["lru_b_i"][0].T)
    arrays["lru_lambda"] = _features(v["lru_lambda"][0])
    arrays["state_lru_h"] = _features(v["state_lru_h"][0, 0])
    arrays["state_dn_conv"] = _features(v["state_dn_conv"][0, 0])
    arrays["state_lru_conv"] = _features(v["state_lru_conv"][0, 0])
    arrays["dn_norm_g"] = v["dn_norm_g"][0].reshape(P, 1)
    arrays["dn_a_log"], arrays["dn_dt_bias"] = v["dn_a_log"], v["dn_dt_bias"]
    arrays["lru_w_r"] = np.ascontiguousarray(v["lru_w_r"][0].transpose(1, 0, 2))
    arrays["lru_w_i"] = np.ascontiguousarray(v["lru_w_i"][0].transpose(1, 0, 2))
    arrays["state_dn"] = np.ascontiguousarray(v["state_dn"][0, 0].transpose(1, 0, 2))
    arrays["ln2_g"], arrays["final_g"] = v["ln2_g"], v["final_g"].reshape(1, D)
    arrays["keys"] = np.ascontiguousarray(v["peer_keys"][0].transpose(1, 3, 0, 2).reshape(P, H, NKEYS))
    arrays["uv"] = np.concatenate([v["peer_u"][0], v["peer_v"][0]], 1)

    nc = bacc.Bacc("TRN2", target_bir_lowering=False, num_devices=1)
    arrays = {k: np.ascontiguousarray(x) for k, x in arrays.items()}
    a = {k: nc.dram_tensor(f"in_{k}", x.shape, mybir.dt.from_np(x.dtype), kind="ExternalInput").ap()
         for k, x in arrays.items()}
    o = {k: nc.dram_tensor(f"out_{k}", s, F32, kind="ExternalOutput").ap() for k, s in _OUTS.items()}
    trunk_program(nc, a, o)
    r = run_bass_kernel_spmd(nc, [{f"in_{k}": x for k, x in arrays.items()}], core_ids=[0]).results[0]
    y, tails, last = r["out_y"], r["out_tails"], r["out_lru_last"]

    def rows(x):
        return np.ascontiguousarray(x.transpose(2, 1, 0)).reshape(x.shape[2], -1)

    def conv_state(first, c0, c1):
        return rows(tails[:, c0:c1, first:first + HIST])[None, None]

    def lru_h(n):
        return rows(last[:, :, n:n + 1])[None]

    return (y[None, :TP], y[None, TP:],
            r["out_dn_p"].transpose(1, 0, 2)[None, None], conv_state(0, KC, 4 * KC), lru_h(0), conv_state(0, 0, KC),
            r["out_dn_s"].transpose(1, 0, 2)[None, None], conv_state(HIST, KC, 4 * KC), lru_h(1),
            conv_state(HIST, 0, KC))
```
